# Optimizing a Trainium2 kernel written in Bass

```python
import math
import jax
import jax.numpy as jnp
from jax import lax
import numpy as np

D_MODEL = 1024
BATCH = 1
SEQ = 256
DEPTH = 2

MIX_WIDTH = D_MODEL
GROUP_WIDTH = MIX_WIDTH // 4
HEAD_DIM = 64
NORM_EPS = 1e-6

SSD_HEADS = GROUP_WIDTH // HEAD_DIM
SSD_STATE = 64
SSD_BC_GROUPS = 2
SSD_CONV = 4
SSD_CHUNK = 128
SSD_BC = SSD_BC_GROUPS * SSD_STATE
SSD_XBC = GROUP_WIDTH + 2 * SSD_BC
SSD_COLS = SSD_XBC + GROUP_WIDTH + SSD_HEADS

ATT_HEADS = GROUP_WIDTH // HEAD_DIM
DILATED_PATTERNS = ((128, 1), (512, 4), (2048, 16))
ATT_BLOCK = 128
ATT_COLS = 3 * GROUP_WIDTH

RWKV_HEADS = GROUP_WIDTH // HEAD_DIM
RWKV_DECAY_RANK = 64
RWKV_A_RANK = 64
RWKV_GATE_RANK = 128
RWKV_DECAY_SCALE = 0.606531
RWKV_GN_EPS = 64e-5
RWKV_COLS = 3 * GROUP_WIDTH + RWKV_DECAY_RANK + RWKV_A_RANK + RWKV_GATE_RANK
RWKV_SPLITS = (GROUP_WIDTH, 2 * GROUP_WIDTH, 3 * GROUP_WIDTH,
               3 * GROUP_WIDTH + RWKV_DECAY_RANK,
               3 * GROUP_WIDTH + RWKV_DECAY_RANK + RWKV_A_RANK)

S5_GROUP = 16
S5_GROUPS = GROUP_WIDTH // S5_GROUP
S5_STATE = 64
S5_COLS = GROUP_WIDTH

MIX_COLS = SSD_COLS + ATT_COLS + RWKV_COLS + S5_COLS
MIX_SPLITS = (SSD_XBC, SSD_XBC + GROUP_WIDTH, SSD_COLS, SSD_COLS + ATT_COLS,
              SSD_COLS + ATT_COLS + RWKV_COLS)

D_FF = 2816
N_EXPERTS = 8
TOP_K = 2
MOE_BLOCK = 256
N_DENSE = (DEPTH + 1) // 2
N_MOE = DEPTH // 2

kernel_name = 'hybrid_ssd_dilatedattn_rwkv7_s5_moe_trunk'

def rms_norm(x, gain, eps=NORM_EPS):
    xf = x.astype(jnp.float32)
    y = xf * lax.rsqrt(jnp.mean(xf * xf, axis=-1, keepdims=True) + eps)
    return (y * gain.astype(jnp.float32)).astype(x.dtype)

def swiglu(h, w_gate, w_up, w_down):
    return (jax.nn.silu(h @ w_gate) * (h @ w_up)) @ w_down

def causal_depthwise_conv(u, w, b):
    ch = u.shape[-1]
    out = lax.conv_general_dilated(
        u, w[:, None, :].astype(u.dtype), window_strides=(1,),
        padding=[(w.shape[0] - 1, 0)], dimension_numbers=('NWC', 'WIO', 'NWC'),
        feature_group_count=ch)
    return out + b.astype(u.dtype)

def segsum(a):
    t = a.shape[-1]
    cs = jnp.cumsum(a, axis=-1)
    diff = cs[..., :, None] - cs[..., None, :]
    return jnp.where(jnp.tril(jnp.ones((t, t), dtype=bool)), diff, -jnp.inf)

def ssd_chunked(x, a, b_mat, c_mat):
    bsz, seq, heads, hd = x.shape
    n_chunks = seq // SSD_CHUNK
    x = x.reshape(bsz, n_chunks, SSD_CHUNK, heads, hd)
    b_mat = b_mat.reshape(bsz, n_chunks, SSD_CHUNK, heads, -1)
    c_mat = c_mat.reshape(bsz, n_chunks, SSD_CHUNK, heads, -1)
    a = a.reshape(bsz, n_chunks, SSD_CHUNK, heads).transpose(0, 3, 1, 2)
    a_cs = jnp.cumsum(a, axis=-1)
    decay = jnp.exp(segsum(a))
    scores = jnp.einsum('bclhn,bcshn->bhcls', c_mat, b_mat) * decay
    y_diag = jnp.einsum('bhcls,bcshp->bclhp', scores, x)
    decay_to_end = jnp.exp(a_cs[..., -1:] - a_cs)
    states = jnp.einsum('bclhn,bhcl,bclhp->bchpn', b_mat, decay_to_end, x)
    states = jnp.concatenate([jnp.zeros_like(states[:, :1]), states], axis=1)
    chunk_decay = jnp.exp(segsum(jnp.pad(a_cs[..., -1], ((0, 0), (0, 0), (1, 0)))))
    states = jnp.einsum('bhzc,bchpn->bzhpn', chunk_decay, states)[:, :-1]
    y_off = jnp.einsum('bclhn,bchpn,bhcl->bclhp', c_mat, states, jnp.exp(a_cs))
    return (y_diag + y_off).reshape(bsz, seq, heads, hd)

def ssd_mixer(xbc, z, dt_raw, conv_w, conv_b, dt_bias, a_log, d_skip, norm_gain):
    bsz, seq, _ = xbc.shape
    xbc = jax.nn.silu(causal_depthwise_conv(xbc, conv_w, conv_b)).astype(jnp.float32)
    xs, b_mat, c_mat = jnp.split(xbc, (GROUP_WIDTH, GROUP_WIDTH + SSD_BC), axis=-1)
    xs = xs.reshape(bsz, seq, SSD_HEADS, HEAD_DIM)
    heads_per_group = SSD_HEADS // SSD_BC_GROUPS
    b_mat = jnp.repeat(b_mat.reshape(bsz, seq, SSD_BC_GROUPS, SSD_STATE), heads_per_group, axis=2)
    c_mat = jnp.repeat(c_mat.reshape(bsz, seq, SSD_BC_GROUPS, SSD_STATE), heads_per_group, axis=2)
    dt = jax.nn.softplus(dt_raw.astype(jnp.float32) + dt_bias.astype(jnp.float32))
    a = -jnp.exp(a_log.astype(jnp.float32))
    y = ssd_chunked(xs * dt[..., None], dt * a, b_mat, c_mat)
    y = y + d_skip.astype(jnp.float32)[:, None] * xs
    y = y.reshape(bsz, seq, GROUP_WIDTH) * jax.nn.silu(z.astype(jnp.float32))
    return rms_norm(y, norm_gain)

def dilated_branch(q, k, v, slopes, window, dilation):
    bsz, seq, heads, hd = q.shape
    n_cls = seq // dilation
    span = window // dilation
    n_blk = -(-n_cls // ATT_BLOCK)
    pad = n_blk * ATT_BLOCK - n_cls

    def to_blocks(t):
        t = t.reshape(bsz, n_cls, dilation, heads, hd).transpose(0, 2, 1, 3, 4)
        t = jnp.pad(t, ((0, 0), (0, 0), (0, pad), (0, 0), (0, 0)))
        return t.reshape(bsz, dilation, n_blk, ATT_BLOCK, heads, hd)

    def with_prev(t):
        prev = jnp.pad(t, ((0, 0), (0, 0), (1, 0), (0, 0), (0, 0), (0, 0)))[:, :, :-1]
        return jnp.concatenate([prev, t], axis=3)

    def from_blocks(t):
        t = t.reshape(bsz, dilation, n_blk * ATT_BLOCK, *t.shape[4:])[:, :, :n_cls]
        t = jnp.swapaxes(t, 1, 2)
        return t.reshape(bsz, seq, *t.shape[3:])

    qb = to_blocks(q)
    kb = with_prev(to_blocks(k))
    vb = with_prev(to_blocks(v))
    scores = jnp.einsum('bdnqhe,bdnkhe->bdnhqk', qb, kb) / math.sqrt(hd)
    q_idx = jnp.arange(ATT_BLOCK)[:, None]
    k_idx = jnp.arange(2 * ATT_BLOCK)[None, :] - ATT_BLOCK
    rel = q_idx - k_idx
    key_pos = jnp.arange(n_blk)[:, None] * ATT_BLOCK + k_idx
    valid = ((rel >= 0) & (rel <= span))[None] & (key_pos >= 0)[:, None, :]
    alibi = -slopes[:, None, None] * (rel * dilation).astype(jnp.float32)[None]
    scores = scores + alibi[None, None, None]
    scores = jnp.where(valid[None, None, :, None], scores, -jnp.inf)
    row_max = jnp.max(scores, axis=-1)
    probs = jnp.exp(scores - row_max[..., None])
    denom = jnp.sum(probs, axis=-1)
    row_max = row_max.transpose(0, 1, 2, 4, 3)
    denom = denom.transpose(0, 1, 2, 4, 3)
    out = jnp.einsum('bdnhqk,bdnkhe->bdnqhe', probs, vb) / denom[..., None]
    return from_blocks(out), from_blocks(row_max), from_blocks(denom)

def dilated_attention(qkv, q_gain, k_gain, out_gain):
    bsz, seq, _ = qkv.shape
    q, k, v = jnp.split(qkv.astype(jnp.float32), 3, axis=-1)
    q = rms_norm(q.reshape(bsz, seq, ATT_HEADS, HEAD_DIM), q_gain)
    k = rms_norm(k.reshape(bsz, seq, ATT_HEADS, HEAD_DIM), k_gain)
    v = v.reshape(bsz, seq, ATT_HEADS, HEAD_DIM)
    slopes = jnp.exp2(-8.0 / ATT_HEADS * jnp.arange(1, ATT_HEADS + 1, dtype=jnp.float32))
    outs, maxes, dens = [], [], []
    for window, dilation in DILATED_PATTERNS:
        o, m, s = dilated_branch(q, k, v, slopes, window, dilation)
        outs.append(o)
        maxes.append(m)
        dens.append(s)
    o = jnp.stack(outs)
    m = jnp.stack(maxes)
    s = jnp.stack(dens)
    wgt = s * jnp.exp(m - jnp.max(m, axis=0, keepdims=True))
    y = jnp.sum(wgt[..., None] * o, axis=0) / jnp.sum(wgt, axis=0)[..., None]
    return rms_norm(y.reshape(bsz, seq, GROUP_WIDTH), out_gain)

def rwkv7_mixer(p, mu, w0, w2, a0, a2, g2, k_k, k_a, r_k, ln_w, ln_b):
    bsz, seq, _ = p.shape
    pf = p.astype(jnp.float32)
    prev = jnp.pad(pf, ((0, 0), (1, 0), (0, 0)))[:, :-1]
    pf = pf + mu * (prev - pf)
    r, k, v, wd, ad, gd = jnp.split(pf, RWKV_SPLITS, axis=-1)
    log_w = -RWKV_DECAY_SCALE * jax.nn.sigmoid(w0 + jnp.tanh(wd) @ w2)
    a = jax.nn.sigmoid(a0 + ad @ a2)
    g = jax.nn.sigmoid(gd) @ g2

    def heads(t):
        return t.reshape(bsz, seq, RWKV_HEADS, HEAD_DIM)

    kk = heads(k * k_k)
    kk = kk * lax.rsqrt(jnp.sum(kk * kk, axis=-1, keepdims=True) + 1e-12)
    k = k * (1.0 + (a - 1.0) * k_a)
    r_h, k_h, v_h, a_h, w_h = heads(r), heads(k), heads(v), heads(a), heads(jnp.exp(log_w))

    def step(state, inp):
        r_t, w_t, k_t, v_t, kk_t, a_t = inp
        s_a = jnp.einsum('bhvk,bhk->bhv', state, -kk_t)
        state = (state * w_t[:, :, None, :] + s_a[..., None] * (kk_t * a_t)[:, :, None, :]
                 + v_t[..., None] * k_t[:, :, None, :])
        return state, jnp.einsum('bhvk,bhk->bhv', state, r_t)

    state0 = jnp.zeros((bsz, RWKV_HEADS, HEAD_DIM, HEAD_DIM), jnp.float32)
    xs = tuple(jnp.swapaxes(t, 0, 1) for t in (r_h, w_h, k_h, v_h, kk, a_h))
    _, y = lax.scan(step, state0, xs)
    y = jnp.swapaxes(y, 0, 1)
    mean = jnp.mean(y, axis=-1, keepdims=True)
    var = jnp.mean(jnp.square(y - mean), axis=-1, keepdims=True)
    y = (y - mean) * lax.rsqrt(var + RWKV_GN_EPS)
    y = y.reshape(bsz, seq, GROUP_WIDTH) * ln_w + ln_b
    bonus = jnp.sum(r_h * k_h * r_k.reshape(RWKV_HEADS, HEAD_DIM), axis=-1, keepdims=True) * v_h
    return (y + bonus.reshape(bsz, seq, GROUP_WIDTH)) * g

def s5_combine(e1, e2):
    a1r, a1i, b1r, b1i = e1
    a2r, a2i, b2r, b2i = e2
    ar = a2r * a1r - a2i * a1i
    ai = a2r * a1i + a2i * a1r
    br = a2r[:, None] * b1r - a2i[:, None] * b1i + b2r
    bi = a2r[:, None] * b1i + a2i[:, None] * b1r + b2i
    return ar, ai, br, bi

def s5_mixer(u, a_re, a_im, b_re, b_im, c_re, c_im, log_dt, d_skip, glu_w, glu_b, out_gain):
    bsz, seq, _ = u.shape
    uf = u.astype(jnp.float32)
    ug = uf.reshape(bsz, seq, S5_GROUPS, S5_GROUP)
    a_re = a_re.astype(jnp.float32)
    a_im = a_im.astype(jnp.float32)
    dt = jnp.exp(log_dt.astype(jnp.float32))[:, None]
    mag = jnp.exp(dt * a_re)
    ab_re = mag * jnp.cos(dt * a_im)
    ab_im = mag * jnp.sin(dt * a_im)
    den = a_re * a_re + a_im * a_im
    f_re = ((ab_re - 1.0) * a_re + ab_im * a_im) / den
    f_im = (ab_im * a_re - (ab_re - 1.0) * a_im) / den
    bb_re = f_re[..., None] * b_re - f_im[..., None] * b_im
    bb_im = f_re[..., None] * b_im + f_im[..., None] * b_re
    bu_re = jnp.einsum('gpc,bsgc->sbgp', bb_re, ug)
    bu_im = jnp.einsum('gpc,bsgc->sbgp', bb_im, ug)
    a_seq_re = jnp.broadcast_to(ab_re, (seq,) + ab_re.shape)
    a_seq_im = jnp.broadcast_to(ab_im, (seq,) + ab_im.shape)
    _, _, h_re, h_im = lax.associative_scan(s5_combine, (a_seq_re, a_seq_im, bu_re, bu_im), axis=0)
    y = (jnp.einsum('gcp,sbgp->bsgc', c_re, h_re)
         - jnp.einsum('gcp,sbgp->bsgc', c_im, h_im))
    y = y.reshape(bsz, seq, GROUP_WIDTH) + d_skip * uf
    h = jax.nn.gelu(y)
    out = h * jax.nn.sigmoid(h @ glu_w + glu_b)
    return rms_norm(out, out_gain)

def moe_swiglu(h, router_w, router_b, w_gate, w_up, w_down):
    bsz, seq, dm = h.shape
    tokens = h.reshape(-1, dm)
    n_tok = tokens.shape[0]
    logits = tokens.astype(jnp.float32) @ router_w.astype(jnp.float32) + router_b.astype(jnp.float32)
    top_logit, top_idx = lax.top_k(logits, TOP_K)
    gates = jax.nn.softmax(top_logit, axis=-1)
    n_assign = n_tok * TOP_K
    flat_exp = top_idx.reshape(-1)
    flat_tok = jnp.repeat(jnp.arange(n_tok, dtype=jnp.int32), TOP_K)
    flat_gate = gates.reshape(-1)
    order = jnp.argsort(flat_exp)
    sorted_exp = flat_exp[order]
    counts = jnp.bincount(flat_exp, length=N_EXPERTS)
    padded = (counts + MOE_BLOCK - 1) // MOE_BLOCK * MOE_BLOCK
    pad_end = jnp.cumsum(padded)
    pad_start = pad_end - padded
    start = jnp.cumsum(counts) - counts
    dest = pad_start[sorted_exp] + (jnp.arange(n_assign) - start[sorted_exp])
    n_blocks = -(-n_assign // MOE_BLOCK) + N_EXPERTS
    cap = n_blocks * MOE_BLOCK
    slot_tok = jnp.zeros((cap,), jnp.int32).at[dest].set(flat_tok[order])
    slot_gate = jnp.zeros((cap,), jnp.float32).at[dest].set(flat_gate[order])
    block_exp = jnp.minimum(
        jnp.searchsorted(pad_end, jnp.arange(n_blocks) * MOE_BLOCK, side='right'), N_EXPERTS - 1)
    xs = tokens[slot_tok].reshape(n_blocks, MOE_BLOCK, dm)

    def expert_block(args):
        xb, e = args
        return (jax.nn.silu(xb @ w_gate[e]) * (xb @ w_up[e])) @ w_down[e]

    ys = lax.map(expert_block, (xs, block_exp)).reshape(cap, dm)
    ys = ys * slot_gate[:, None].astype(ys.dtype)
    out = jax.ops.segment_sum(ys, slot_tok, num_segments=n_tok)
    return out.reshape(bsz, seq, dm)

def setup_inputs(seed: int = 0) -> dict:
    key = jax.random.key(seed)
    ks = iter(jax.random.split(key, 64))
    f32 = jnp.float32

    def normal(shape, scale):
        return scale * jax.random.normal(next(ks), shape, f32)

    def gain(shape):
        return 1.0 + 0.02 * jax.random.normal(next(ks), shape, f32)

    def uniform(shape, lo, hi):
        return jax.random.uniform(next(ks), shape, f32, lo, hi)

    L, GW = DEPTH, GROUP_WIDTH
    x = normal((BATCH, SEQ, D_MODEL), 1.0)
    ln_mix = gain((L, D_MODEL))
    w_in = normal((L, D_MODEL, MIX_COLS), D_MODEL ** -0.5)
    w_out = normal((L, MIX_WIDTH, D_MODEL), MIX_WIDTH ** -0.5)
    ssd_conv_w = normal((L, SSD_CONV, SSD_XBC), SSD_CONV ** -0.5)
    ssd_conv_b = normal((L, SSD_XBC), 0.02)
    ssd_dt = jnp.exp(uniform((L, SSD_HEADS), math.log(1e-3), math.log(1e-1)))
    ssd_dt_bias = ssd_dt + jnp.log(-jnp.expm1(-ssd_dt))
    ssd_a_log = jnp.log(uniform((L, SSD_HEADS), 1.0, 16.0))
    ssd_d = gain((L, SSD_HEADS))
    ssd_norm = gain((L, GW))
    att_q_norm = gain((L, HEAD_DIM))
    att_k_norm = gain((L, HEAD_DIM))
    att_out_norm = gain((L, GW))
    rwkv_mu = uniform((L, RWKV_COLS), 0.0, 1.0)
    rwkv_w0 = uniform((L, GW), -4.0, 2.0)
    rwkv_w2 = normal((L, RWKV_DECAY_RANK, GW), 0.1)
    rwkv_a0 = normal((L, GW), 0.1)
    rwkv_a2 = normal((L, RWKV_A_RANK, GW), 0.5 * RWKV_A_RANK ** -0.5)
    rwkv_g2 = normal((L, RWKV_GATE_RANK, GW), RWKV_GATE_RANK ** -0.5)
    rwkv_k_k = 0.85 + normal((L, GW), 0.02)
    rwkv_k_a = gain((L, GW))
    rwkv_r_k = normal((L, GW), 0.1)
    rwkv_ln_w = gain((L, GW))
    rwkv_ln_b = normal((L, GW), 0.02)
    s5_a_re = -0.5 + normal((L, S5_GROUPS, S5_STATE), 0.01)
    s5_a_im = math.pi * jnp.arange(S5_STATE, dtype=f32) + normal((L, S5_GROUPS, S5_STATE), 0.01)
    s5_b_re = normal((L, S5_GROUPS, S5_STATE, S5_GROUP), (2 * S5_GROUP) ** -0.5)
    s5_b_im = normal((L, S5_GROUPS, S5_STATE, S5_GROUP), (2 * S5_GROUP) ** -0.5)
    s5_c_re = normal((L, S5_GROUPS, S5_GROUP, S5_STATE), S5_STATE ** -0.5)
    s5_c_im = normal((L, S5_GROUPS, S5_GROUP, S5_STATE), S5_STATE ** -0.5)
    s5_log_dt = uniform((L, S5_GROUPS), math.log(1e-3), math.log(1e-1))
    s5_d = normal((L, GW), 1.0)
    s5_glu_w = normal((L, GW, GW), GW ** -0.5)
    s5_glu_b = normal((L, GW), 0.02)
    s5_out_norm = gain((L, GW))
    ln_ffn = gain((L, D_MODEL))
    ffn_w_gate = normal((N_DENSE, D_MODEL, D_FF), D_MODEL ** -0.5)
    ffn_w_up = normal((N_DENSE, D_MODEL, D_FF), D_MODEL ** -0.5)
    ffn_w_down = normal((N_DENSE, D_FF, D_MODEL), D_FF ** -0.5)
    moe_router_w = normal((N_MOE, D_MODEL, N_EXPERTS), D_MODEL ** -0.5)
    moe_router_b = normal((N_MOE, N_EXPERTS), 0.01)
    moe_w_gate = normal((N_MOE, N_EXPERTS, D_MODEL, D_FF), D_MODEL ** -0.5)
    moe_w_up = normal((N_MOE, N_EXPERTS, D_MODEL, D_FF), D_MODEL ** -0.5)
    moe_w_down = normal((N_MOE, N_EXPERTS, D_FF, D_MODEL), D_FF ** -0.5)
    return {
        'x': x, 'ln_mix': ln_mix, 'w_in': w_in, 'w_out': w_out,
        'ssd_conv_w': ssd_conv_w, 'ssd_conv_b': ssd_conv_b, 'ssd_dt_bias': ssd_dt_bias,
        'ssd_a_log': ssd_a_log, 'ssd_d': ssd_d, 'ssd_norm': ssd_norm,
        'att_q_norm': att_q_norm, 'att_k_norm': att_k_norm, 'att_out_norm': att_out_norm,
        'rwkv_mu': rwkv_mu, 'rwkv_w0': rwkv_w0, 'rwkv_w2': rwkv_w2, 'rwkv_a0': rwkv_a0,
        'rwkv_a2': rwkv_a2, 'rwkv_g2': rwkv_g2, 'rwkv_k_k': rwkv_k_k, 'rwkv_k_a': rwkv_k_a,
        'rwkv_r_k': rwkv_r_k, 'rwkv_ln_w': rwkv_ln_w, 'rwkv_ln_b': rwkv_ln_b,
        's5_a_re': s5_a_re, 's5_a_im': s5_a_im, 's5_b_re': s5_b_re, 's5_b_im': s5_b_im,
        's5_c_re': s5_c_re, 's5_c_im': s5_c_im, 's5_log_dt': s5_log_dt, 's5_d': s5_d,
        's5_glu_w': s5_glu_w, 's5_glu_b': s5_glu_b, 's5_out_norm': s5_out_norm,
        'ln_ffn': ln_ffn, 'ffn_w_gate': ffn_w_gate, 'ffn_w_up': ffn_w_up, 'ffn_w_down': ffn_w_down,
        'moe_router_w': moe_router_w, 'moe_router_b': moe_router_b,
        'moe_w_gate': moe_w_gate, 'moe_w_up': moe_w_up, 'moe_w_down': moe_w_down,
    }

def reference(x, ln_mix, w_in, w_out,
              ssd_conv_w, ssd_conv_b, ssd_dt_bias, ssd_a_log, ssd_d, ssd_norm,
              att_q_norm, att_k_norm, att_out_norm,
              rwkv_mu, rwkv_w0, rwkv_w2, rwkv_a0, rwkv_a2, rwkv_g2, rwkv_k_k, rwkv_k_a,
              rwkv_r_k, rwkv_ln_w, rwkv_ln_b,
              s5_a_re, s5_a_im, s5_b_re, s5_b_im, s5_c_re, s5_c_im, s5_log_dt, s5_d,
              s5_glu_w, s5_glu_b, s5_out_norm,
              ln_ffn, ffn_w_gate, ffn_w_up, ffn_w_down,
              moe_router_w, moe_router_b, moe_w_gate, moe_w_up, moe_w_down):
    for layer in range(DEPTH):
        h = rms_norm(x, ln_mix[layer])
        proj = h @ w_in[layer]
        xbc, z, dt_raw, qkv, rwkv_in, s5_in = jnp.split(proj, MIX_SPLITS, axis=-1)
        y_a = ssd_mixer(xbc, z, dt_raw, ssd_conv_w[layer], ssd_conv_b[layer],
                        ssd_dt_bias[layer], ssd_a_log[layer], ssd_d[layer], ssd_norm[layer])
        y_b = dilated_attention(qkv, att_q_norm[layer], att_k_norm[layer], att_out_norm[layer])
        y_c = rwkv7_mixer(rwkv_in, rwkv_mu[layer], rwkv_w0[layer], rwkv_w2[layer], rwkv_a0[layer],
                          rwkv_a2[layer], rwkv_g2[layer], rwkv_k_k[layer], rwkv_k_a[layer],
                          rwkv_r_k[layer], rwkv_ln_w[layer], rwkv_ln_b[layer])
        y_d = s5_mixer(s5_in, s5_a_re[layer], s5_a_im[layer], s5_b_re[layer], s5_b_im[layer],
                       s5_c_re[layer], s5_c_im[layer], s5_log_dt[layer], s5_d[layer],
                       s5_glu_w[layer], s5_glu_b[layer], s5_out_norm[layer])
        mixed = jnp.concatenate([y_a, y_b, y_c, y_d], axis=-1).astype(x.dtype)
        x = x + mixed @ w_out[layer]
        h = rms_norm(x, ln_ffn[layer])
        idx = layer // 2
        if layer % 2 == 0:
            x = x + swiglu(h, ffn_w_gate[idx], ffn_w_up[idx], ffn_w_down[idx])
        else:
            x = x + moe_swiglu(h, moe_router_w[idx], moe_router_b[idx],
                               moe_w_gate[idx], moe_w_up[idx], moe_w_down[idx])
    return x


_drawn_inputs = setup_inputs


def setup_inputs(seed=0):
    import zlib

    import numpy as np

    out = dict(_drawn_inputs(seed))
    spreads = {}
    factors = {'att_q_norm': 3.533,
     'att_k_norm': 3.253,
     'att_out_norm': 8.917,
     'rwkv_k_k': 130.242,
     'rwkv_k_a': 3.39,
     'rwkv_ln_w': 15.932,
     'rwkv_ln_b': 17.181,
     's5_a_re': 200.0,
     's5_glu_b': 4.803,
     'moe_router_b': 31.088,
     'ssd_conv_b': 2.761,
     'ssd_d': 12.198,
     'ssd_norm': 3.439,
     's5_a_im': 22.24,
     's5_b_re': 28.272,
     's5_b_im': 28.64,
     's5_c_re': 23.64,
     's5_c_im': 27.184,
     's5_log_dt': 22.632,
     's5_out_norm': 3.414,
     'ln_ffn': 4.323}
    for name, (base, spread) in spreads.items():
        noise = np.random.default_rng([zlib.crc32(name.encode()), seed]).standard_normal(out[name].shape)
        drawn = base * np.exp(spread * noise) if base else spread * noise
        out[name] = jnp.asarray(drawn.astype(out[name].dtype))
    for name, factor in factors.items():
        out[name] = (out[name] * factor).astype(out[name].dtype)
    return out
```

```python
from contextlib import ExitStack

import numpy as np

import concourse.bass as bass
from concourse import mybir

F32 = mybir.dt.float32
I32 = mybir.dt.int32
ALU = mybir.AluOpType
ACT = mybir.ActivationFunctionType
AX = mybir.AxisListType

P = 128
D = 1024
KT = D // P
T = 256
TT = T // P
GW = 256
HD = 64
H = GW // HD
DEPTH = 2
F = 2816
NE = 8
EPS = 1e-6
GN_EPS = 64e-5
DECAY = 0.606531
LOG2E_SLOPES = [2.0 ** (-8.0 / H * (h + 1)) for h in range(H)]
PATTERNS = ((128, 1), (512, 4), (2048, 16))
CONV = 4

FC = 256
NC_ = F // FC
GUK = 2
GUQ = KT // GUK
GU_UNITS = NC_ * GUQ
R_GU = 4
NF = F // P
D_UNITS = NF * 2
R_D = 4
R_M = 5
TMW = 2 * GW + H

PCOLS = {}
_at = 0
for _name, _n in (("ln_mix", 8), ("ln_ffn", 8), ("conv_w", 16), ("conv_b", 4), ("ssd_norm", 2), ("att_out", 2),
                  ("q_gain", 1), ("k_gain", 1), ("mu", 8), ("w0", 2), ("a0", 2), ("k_k", 2), ("k_a", 2),
                  ("r_k", 2), ("ln_w", 2), ("ln_b", 2), ("s5_d", 2), ("glu_b", 2), ("s5_out", 2),
                  ("a_re", 8), ("a_im", 8), ("log_dt", 8), ("dt_bias", 4), ("a_log", 4), ("ssd_d", 4),
                  ("router_b", 8)):
    PCOLS[_name] = (_at, _n)
    _at += _n
NPAR = _at
WCOLS = {}
_at = 0
for _name, _n in (("w2a2", 256), ("g2", 256), ("glu", 512), ("b_re", 256), ("b_im", 256), ("c_re", 128),
                  ("c_im", 128), ("router", 64)):
    WCOLS[_name] = (_at, _n)
    _at += _n
NSW = _at
ARENA = 11796 + 13 * 512 + 256 + 6144
MUNIT = 4 * 258
M_UNITS = 22 + 8


class Flag:

    def __init__(self, nc, ctx, name, per):
        self.sem, self.per, self.n = ctx.enter_context(nc.semaphore(name)), per, 0

    def at(self, layer, i):
        return layer * self.per + i


class Chain:

    def __init__(self, eng, sem):
        self.eng, self.sem, self.n = eng, sem, 0

    def __call__(self, ins, flag=None):
        if flag is None:
            self.n += 1
            ins.then_inc(self.sem, 1)
            self.eng.wait_ge(self.sem, self.n)
        else:
            flag.n += 1
            ins.then_inc(flag.sem, 1)
            self.eng.wait_ge(flag.sem, flag.n)


def trunk(nc, x_in, params, small_w, mix_w, gu_dense, d_dense, gu_moe, d_moe, out):
    ctx = ExitStack()
    with ctx:
        def sb(name, shape, dt=F32):
            return ctx.enter_context(nc.sbuf_tensor(name, shape, dt))

        def flag(name, per=1):
            return Flag(nc, ctx, name, per)

        x = sb("x", [P, TT, D])
        par = sb("par", [P, DEPTH, NPAR])
        sw = sb("sw", [P, NSW])
        mring = sb("mring", [P, R_M, MUNIT])
        guring = sb("guring", [P, R_GU, GUK, 2 * FC])
        dring = sb("dring", [P, R_D, 512])
        ident = sb("ident", [P, P])
        ones = sb("ones", [P, P])
        blk = sb("blk", [P, P])
        m_gt = sb("m_gt", [P, P])
        m_lt = sb("m_lt", [P, P])
        m_leo = sb("m_leo", [P, T])
        m_le = m_leo[:, 0:P]
        lvl = sb("lvl", [P, 7, P])
        bias0 = sb("bias0", [P, H, P])
        bias1 = sb("bias1", [P, H, T])
        cnt0 = sb("cnt0", [P, P])
        cnt1 = sb("cnt1", [P, T])
        iota = sb("iota", [P, P])
        tie = sb("tie", [P, NE, NE])
        s5p = sb("s5p", [P, DEPTH, 6, 8])
        s5t = sb("s5t", [P, 10, DEPTH * 8])
        e_re = sb("e_re", [P, 8, T])
        e_im = sb("e_im", [P, 8, T])
        st = sb("st", [P, 128])
        xh = sb("xh", [P, TT, D])
        arena = sb("arena", [P, ARENA])
        at = [0]

        def v3(a, m):
            return a.rearrange("p (m t) -> p m t", m=m)

        def take(n, reset=None):
            if reset is not None:
                at[0] = reset
            a = arena[:, at[0]:at[0] + n]
            at[0] += n
            assert at[0] <= ARENA, at[0]
            return a

        hT = v3(take(2048), KT)
        mixT = v3(take(2048), 8)
        zv = v3(take(1024), TT)
        rk_raw = take(8 * 257)
        rk = v3(rk_raw, 8)
        pf = v3(take(2048), 8)
        u5 = v3(take(512), 2)
        xbc = v3(take(4 * 259), 4)
        qk = v3(take(1024), 4)
        sA, cs, cp, eE, eX, eM, kk, kp, rw_g, rw_b, kk2, rsq = (v3(take(512), 2) for _ in range(12))
        gy = v3(take(512), TT)
        s0 = v3(take(256), 2)
        nm, m2, mb, mk = (v3(rk_raw[:, i * 512:(i + 1) * 512], H) for i in range(4))
        hflat = arena[:, 0:2048]
        tm_, tt_, xs_ = (v3(hflat[:, i * 512:(i + 1) * 512], H) for i in range(3))
        zs, us = hflat[:, 1536:1792], hflat[:, 1792:2048]
        xflat = xh[:, :, :].rearrange("p a d -> p (a d)")
        vt = v3(xflat[:, 0:512], TT)
        bkt = v3(xflat[:, 512:1024], 4)
        noff = xflat[:, 1024:2048].rearrange("p (b h t) -> p b h t", b=2, h=H)
        scratch = at[0]
        cv = v3(take(1024), 4)
        sg = v3(take(1024), 4)
        r0 = sg
        xs = v3(take(512), TT)
        xd = v3(take(512), TT)
        L0 = v3(take(1024), H)
        L1 = v3(take(512), H)
        sc0 = v3(take(512), 2)
        sc1 = v3(take(256), 2)
        r1 = v3(take(512), H)
        sq = v3(take(1024, scratch), 4)
        a0 = v3(take(512), H)
        a1 = v3(take(1024), H)
        pt0, pt1, pt2 = (v3(take(512), H) for _ in range(3))
        ya = v3(take(512), TT)
        z5 = take(4096, scratch).rearrange("p (j c t) -> p j c t", j=8, c=2)
        p5raw = take(2048)
        p5 = p5raw.rearrange("p (b s c t) -> p b s c t", b=2, s=2, c=2)
        y5, g5, q5, g5s = (v3(p5raw[:, i * 512:(i + 1) * 512], 2) for i in range(4))
        cpad_re = pf[:, 0:4, :].rearrange("p m (a t) -> p (m a) t", a=2)
        cpad_im = pf[:, 4:8, :].rearrange("p m (a t) -> p (m a) t", a=2)
        sil = v3(take(512, 2048), 2)
        av = v3(take(512), 2)
        avT = take(512).rearrange("p (b f s) -> p b f s", b=2, f=2)
        xgT = v3(take(1024), KT)
        ys = take(1024)
        G = v3(take(256), TT)
        Gg = v3(take(256), TT)
        GT = v3(take(256), TT)
        rt = take(1024)
        tab_tmp = sb("tab_tmp", [P, 512])
        c5 = sb("c5", [P, 3, P])
        sel_, rl, rlg, rrk, rmx = rt[:, 0:16], rt[:, 16:32], rt[:, 32:48], rt[:, 48:64], rt[:, 64:66]
        rtab = rt[:, 66:120]
        rgate, rsel, rpos = (v3(rtab[:, 18 * i:18 * i + 18], 2) for i in range(3))
        st_at = [0]

        def small_tile(n):
            st_at[0] += n
            return st[:, st_at[0] - n:st_at[0]]

        ssx, rsx, ssy, ssa, dec = (small_tile(2) for _ in range(5))
        ncm, ael = small_tile(4), small_tile(4)
        dtr, dta, dte, dtl, dtu, sa, gst, amx = (small_tile(8) for _ in range(8))
        dtr3 = v3(dtr, 2)
        gsq = p5raw[:, 0:256]
        pw = sb("pw", [P, 3, 8])
        S_AT = ("dt", "da", "r", "k", "r2", "mag", "sin", "cos")

        def S(name):
            return s5t[:, S_AT.index(name), :].rearrange("p (l j) -> p l j", l=DEPTH)

        def par3(name):
            a_, n_ = PCOLS[name]
            return par[:, :, a_:a_ + n_]

        ovf = sb("ovf", [P, 1], I32)
        it_x = sb("it_x", [P, P], I32)
        it_y = sb("it_y", [P, P], I32)
        it_d = sb("it_d", [P, 384], I32)

        ps = ctx.enter_context(nc.psum_tensor("ps", [P, 8, 512], F32))

        ch_act, ch_dve, ch_pool = (ctx.enter_context(nc.semaphore(n)) for n in ("act_chain", "dve_chain", "pool_chain"))
        x_in_sem = ctx.enter_context(nc.semaphore("x_loaded"))
        par_sem = ctx.enter_context(nc.semaphore("params_loaded"))
        sw_sem = ctx.enter_context(nc.semaphore("small_weights_loaded"))
        out_sem = ctx.enter_context(nc.semaphore("out_stored"))
        m_full = [ctx.enter_context(nc.semaphore(f"mix_weight_full{i}")) for i in range(R_M)]
        gu_full_s = [ctx.enter_context(nc.semaphore(f"gate_up_full{i}")) for i in range(R_GU)]
        d_full_s = [ctx.enter_context(nc.semaphore(f"down_full{i}")) for i in range(R_D)]
        bank_full = [ctx.enter_context(nc.semaphore(f"bank_full{i}")) for i in range(8)]

        consts_pool = flag("consts_pool")
        consts_dve = flag("consts_dve")
        poles = flag("poles", 1)
        pole_a = flag("pole_a", 3)
        pole_d = flag("pole_d", 2)
        sumsq = flag("sumsq", 2)
        rs_in = flag("rs_in", 2)
        rs_out = flag("rs_out", 2)
        xh_ready = flag("xh_ready", 2)
        h_evac = flag("h_evac", 8)
        fm_out = flag("fm_out", 9)
        zv_out = flag("zv_out", 2)
        dt_out = flag("dt_out", 1)
        rk_mixed = flag("rk_mixed", 1)
        lora_in = flag("lora_in", 1)
        rk_act = flag("rk_act", 3)
        rk_cs = flag("rk_cs", 1)
        rk_exp = flag("rk_exp", 1)
        rk_sq = flag("rk_sq", 1)
        rk_ss = flag("rk_ss", 1)
        rk_rs = flag("rk_rs", 1)
        rk_hat = flag("rk_hat", 1)
        rk_bon = flag("rk_bon", 1)
        rk_bonus = flag("rk_bonus", 1)
        rk_tok = flag("rk_tok", 2)
        rk_mat = flag("rk_mat", 8)
        rk_off = flag("rk_off", 14)
        rk_x = flag("rk_x", 12)
        rk_tt = flag("rk_tt", 14)
        rk_t = flag("rk_t", 12)
        rk_z = flag("rk_z", 2)
        rk_u = flag("rk_u", 2)
        rk_s = flag("rk_s", 1)
        gn_in = flag("gn_in", 2)
        gn_rs = flag("gn_rs", 2)
        gn_y = flag("gn_y", 2)
        rk_yt = flag("rk_yt", 2)
        mix_done = flag("mix_done", 4)
        ssd_cv = flag("ssd_cv", 1)
        ssd_sg = flag("ssd_sg", 1)
        ssd_xbc = flag("ssd_xbc", 1)
        dt_a = flag("dt_a", 1)
        dt_b = flag("dt_b", 1)
        dt_c = flag("dt_c", 1)
        dt_d = flag("dt_d", 1)
        ssd_a = flag("ssd_a", 1)
        ssd_xs = flag("ssd_xs", 1)
        ssd_xd = flag("ssd_xd", 1)
        ssd_r = flag("ssd_r", 1)
        ssd_l = flag("ssd_l", 3)
        ssd_sc = flag("ssd_sc", 2)
        ssd_p = flag("ssd_p", 1)
        ssd_y = flag("ssd_y", 1)
        ssd_ss = flag("ssd_ss", 1)
        ssd_v = flag("ssd_v", 1)
        ssd_rs = flag("ssd_rs", 1)
        ssd_n = flag("ssd_n", 1)
        att_sq = flag("att_sq", 1)
        att_ss = flag("att_ss", 2)
        att_rs = flag("att_rs", 1)
        att_qk = flag("att_qk", 1)
        att_s = flag("att_s", 4)
        att_m = flag("att_m", 2)
        att_e = flag("att_e", 2)
        att_p = flag("att_p", 2)
        att_pt = flag("att_pt", 3)
        att_y = flag("att_y", 1)
        att_v = flag("att_v", 1)
        att_rs2 = flag("att_rs2", 1)
        att_n = flag("att_n", 1)
        tab = flag("tab", 1)
        s5_c = flag("s5_c", 1)
        s5_in = flag("s5_in", 8)
        s5_z = flag("s5_z", 8)
        s5_back = flag("s5_back", 8)
        s5_h = flag("s5_h", 8)
        s5_y = flag("s5_y", 1)
        s5_g = flag("s5_g", 1)
        s5_sig = flag("s5_sig", 1)
        s5_sq = flag("s5_sq", 1)
        s5_ss = flag("s5_ss", 1)
        s5_rs = flag("s5_rs", 1)
        wo_used = flag("wo_used", 7)
        x_mixed = flag("x_mixed", 4)
        gu_used = flag("gu_used", NC_ * (GUQ - 1))
        gu_done = flag("gu_done", NC_)
        gu_done0 = flag("gu_done0", NC_)
        av_ready = flag("av_ready", NC_)
        sil_ready = flag("sil_ready", NC_)
        t_full = flag("t_full", NC_)
        avT_ready = flag("avT_ready", NC_)
        d_used = flag("d_used", D_UNITS - 2)
        y_done = flag("y_done", 2)
        x_ffn = flag("x_ffn", 4)
        g_ready = flag("g_ready", 1)
        gat_full = flag("gat_full", 2)
        xg_ready = flag("xg_ready", 2)
        sc_full = flag("sc_full", 4)
        x_added = flag("x_added", 4)
        gt_full = flag("gt_full", 1)
        gt_ready = flag("gt_ready", 1)
        ys_ready = flag("ys_ready", 2)
        router_s = flag("router_s", 2)
        router_d = flag("router_d", 2)
        router_a = flag("router_a", 1)

        def need(eng, f, layer, i):
            eng.wait_ge(f.sem, f.at(layer, i))

        def pp(layer, name, i=0, n=None):
            a, m = PCOLS[name]
            return par[:, layer, a + i:a + i + (m if n is None else n)]

        def ww(name):
            a, m = WCOLS[name]
            return sw[:, a:a + m]

        def bc(a, shape, axis):
            return a.unsqueeze(axis).to_broadcast(shape)

        tiles = []

        def tile_(key, f, i):
            tiles.append((key, f, i))

        for q in range(4):
            tile_(("h", q), h_evac, q + 1)
        for q in range(4):
            tile_(("fm", q), fm_out, q + 1)
        tile_(("fm", 4), fm_out, 5)
        tile_("lw", rk_act, 1)
        tile_("la", rk_act, 2)
        tile_("lg", rk_act, 3)
        tile_(("fm", 5), fm_out, 6)
        tile_(("fm", 6), fm_out, 7)
        tile_("kks", rk_ss, 1)
        tile_("zv0", zv_out, 1)
        tile_("zv1", zv_out, 2)
        tile_("dt", dt_out, 1)
        tile_("bon", rk_bonus, 1)
        tile_(("fm", 7), fm_out, 8)
        tile_(("fm", 8), fm_out, 9)
        tile_("xt", ssd_xs, 1)
        tile_("dA", ssd_l, 1)
        tile_("dB", ssd_l, 2)
        tile_("d1", ssd_l, 3)
        tile_("sc0", ssd_sc, 1)
        tile_("sc1", ssd_sc, 2)
        tile_("sy", ssd_y, 1)
        tile_("vt", rk_tok, 1)
        tile_("bkt", rk_tok, 2)
        tile_("syt", mix_done, 1)
        tile_("qs", att_ss, 1)
        tile_("ks", att_ss, 2)

        PRODUCT_TILES = ("NM2e", "NM2o", "MBKe", "MBKo")

        def rwkv_tiles(c):
            for q, n in enumerate(PRODUCT_TILES):
                tile_((n, c), rk_mat, 4 * c + q + 1)

        def level_tiles(c, l):
            if l == 0:
                tile_(("X", c, 0), rk_tt, 7 * c + 1)
                return
            tile_(("X", c, l), rk_x, 6 * c + l)
            tile_(("TT", c, l), rk_tt, 7 * c + l + 1)
            if l < 6:
                tile_(("T", c, l), rk_t, 6 * c + l + 1)

        rwkv_tiles(0)
        for l in range(7):
            level_tiles(0, l)
        tile_(("Z", 0), rk_z, 1)
        tile_(("U", 0), rk_u, 1)
        tile_("S", rk_s, 1)
        tile_(("Y", 0), gn_y, 1)
        rwkv_tiles(1)
        for l in range(7):
            level_tiles(1, l)
        tile_(("Z", 1), rk_z, 2)
        tile_(("U", 1), rk_u, 2)
        tile_(("Y", 1), gn_y, 2)
        tile_(("yt", 0), rk_yt, 1)
        tile_(("yt", 1), rk_yt, 2)
        ATT_TILES = (("S0e", 0, (0, 2)), ("S0o", 0, (1, 3)), ("S1e", 1, (0, 2)), ("S1o", 1, (1, 3)))
        for i, (key, _, _) in enumerate(ATT_TILES):
            tile_(key, att_s, i + 1)
        tile_("P0", att_pt, 1)
        tile_("P1", att_pt, 2)
        tile_("P2", att_pt, 3)
        tile_("ya", att_n, 1)
        tile_("yat", mix_done, 3)
        for j in range(8):
            tile_(("bu", j), s5_in, j + 1)
        tile_("y5", s5_y, 1)
        tile_("glu", s5_sig, 1)
        tile_("o5", s5_ss, 1)
        for q in range(4):
            tile_(("wo", q), x_mixed, q + 1)
        for q in range(4):
            tile_(("h2", q), h_evac, 4 + q + 1)
        place = {key: i for i, (key, _, _) in enumerate(tiles)}
        uses = [sum(1 for i in range(len(tiles)) if i % 8 == b) for b in range(8)]

        def bank(key, i0=0, n=512):
            return ps[:, place[key] % 8, i0:i0 + n]

        def acquire(pe, layer, key):
            i = place[key]
            if i >= 8:
                _, f, n = tiles[i - 8]
                need(pe, f, layer, n)
            return ps[:, i % 8, :]

        def filled(ins, key):
            ins.then_inc(bank_full[place[key] % 8], 1)

        def has(eng, layer, key, i0=0, n=512):
            i = place[key]
            eng.wait_ge(bank_full[i % 8], layer * uses[i % 8] + i // 8 + 1)
            return ps[:, i % 8, i0:i0 + n]

        UNITS = ([("fm", i) for i in range(10)] + [("fm", i) for i in range(10, 14)]
                 + [("tm", i) for i in range(4)] + [("fm", i) for i in range(14, 18)] + [("wo", i) for i in range(8)])
        unit_at = {u: i for i, u in enumerate(UNITS)}
        assert len(UNITS) == M_UNITS and M_UNITS % R_M == 0

        def unit_read(u):
            kind, i = u
            if kind == "fm":
                return fm_out, i // 2 + 1
            if kind == "tm":
                return dt_out, 1
            return (wo_used, i + 1) if i < 7 else (x_mixed, 4)

        def unit(pe, layer, u):
            i = unit_at[u]
            pe.wait_ge(m_full[i % R_M], 16 * (layer * (M_UNITS // R_M) + i // R_M + 1))
            return mring[:, i % R_M, :]

        def gu_read(e, q):
            if q % GUQ < GUQ - 1:
                return gu_used, e * gu_used.per + (q // GUQ) * (GUQ - 1) + q % GUQ + 1
            return gu_done, e * gu_done.per + q // GUQ + 1

        def d_read(e, q):
            if q < D_UNITS - 2:
                return d_used, e * d_used.per + q + 1
            return y_done, e * y_done.per + q - (D_UNITS - 2) + 1

        block = ctx.enter_context(nc.Block())

        @block.sync
        def _(sp):
            sp.dma_start(x[:], x_in.rearrange("(a p) d -> p a d", p=P)).then_inc(x_in_sem, 16)
            sp.dma_start(par[:], params.rearrange("l p n -> p l n")).then_inc(par_sem, 16)

            def small(layer):
                if layer:
                    need(sp, x_mixed, layer - 1, 4)
                sp.dma_start(sw[:], small_w[layer]).then_inc(sw_sem, 16)

            def mix_unit(layer, i):
                g = layer * M_UNITS + i
                if g >= R_M:
                    f, n = unit_read(UNITS[(i - R_M) % M_UNITS])
                    need(sp, f, (g - R_M) // M_UNITS, n)
                sp.dma_start(mring[:, i % R_M, :], mix_w[layer, i]).then_inc(m_full[i % R_M], 16)

            def gu_unit(e, q, src, first):
                if not first:
                    f, n = gu_read(e, q - R_GU) if q >= R_GU else gu_read(e - 1, GU_UNITS + q - R_GU)
                    sp.wait_ge(f.sem, n)
                sp.dma_start(guring[:, q % R_GU], src).then_inc(gu_full_s[q % R_GU], 16)

            def d_unit(e, q, src, first):
                if not first:
                    f, n = d_read(e, q - R_D) if q >= R_D else d_read(e - 1, D_UNITS + q - R_D)
                    sp.wait_ge(f.sem, n)
                sp.dma_start(dring[:, q % R_D], src).then_inc(d_full_s[q % R_D], 16)

            def ffn_stream(e, gu_src, d_src, q0, d0):
                dq = d0
                for c in range(NC_ + 1):
                    if c < NC_:
                        for q in range(GUQ * c, GUQ * c + GUQ):
                            if q >= q0:
                                gu_unit(e, q, gu_src(q), False)
                    if c >= 1:
                        for q in range(4 * (c - 1), 4 * c):
                            if q >= d0:
                                d_unit(e, q, d_src(q), False)

            def d_rows(w, q):
                return w[(q // 2) * P:(q // 2 + 1) * P, (q % 2) * 512:(q % 2) * 512 + 512]

            for i in range(R_M):
                mix_unit(0, i)
            small(0)
            for i in range(R_M, M_UNITS):
                mix_unit(0, i)
                if i == 12:
                    for q in range(R_GU):
                        gu_unit(0, q, gu_dense[q], True)
                    for q in range(R_D):
                        d_unit(0, q, d_rows(d_dense, q), True)
            small(1)
            ffn_stream(0, lambda q: gu_dense[q], lambda q: d_rows(d_dense, q), R_GU, R_D)
            for i in range(M_UNITS):
                mix_unit(1, i)

            def experts(first):
                with sp.Fori(first, first + NE) as e:
                    gw = gu_moe[bass.ds(e - first, 1)].rearrange("a q p k n -> (a q) p k n")
                    dw = d_moe[bass.ds(e - first, 1)].rearrange("a f d -> (a f) d")
                    ffn_stream(e, lambda q: gw[q], lambda q: d_rows(dw, q), 0, 0)

            experts(1)
            sp.wait_ge(router_d.sem, 2)
            over = sp.value_load(ovf[0:1, 0:1])
            with sp.If(over > 0):
                experts(1 + NE)
                sp.wait_ge(x_added.sem, 8 * NE + 8)
            sp.wait_ge(x_added.sem, 4 * NE + 4)
            sp.dma_start(out.rearrange("(a p) d -> p a d", p=P), x[:]).then_inc(out_sem, 16)
            sp.wait_ge(out_sem, 16)

        @block.tensor
        def _(pe):
            mm = pe.matmul

            def transposes(layer, key, srcs):
                t = acquire(pe, layer, key)
                for i, s in enumerate(srcs):
                    ins = pe.transpose(t[:, i * P:(i + 1) * P], s, ident[:])
                filled(ins, key)

            def norm_transpose(layer, name, n):
                need(pe, xh_ready, layer, n)
                for q in range(4):
                    transposes(layer, (name, q), [xh[:, q // 2, (4 * (q % 2) + i) * P:(4 * (q % 2) + i + 1) * P]
                                                  for i in range(4)])

            def fm(layer, q):
                t = acquire(pe, layer, ("fm", q))
                if q == 0:
                    need(pe, h_evac, layer, 4)
                for i in range(2):
                    w = unit(pe, layer, ("fm", 2 * q + i))
                    for k in range(KT):
                        ins = mm(t[:, i * T:(i + 1) * T], w[:, k * P:(k + 1) * P], hT[:, k, :],
                                 start=(k == 0), stop=(k == KT - 1))
                filled(ins, ("fm", q))

            def tm(layer):
                ws = [unit(pe, layer, ("tm", i)) for i in range(4)]
                for tt in range(TT):
                    t = acquire(pe, layer, f"zv{tt}")
                    for k in range(KT):
                        w = ws[k // 2][:, (k % 2) * TMW:(k % 2) * TMW + 2 * GW]
                        ins = mm(t, hT[:, k, tt * P:(tt + 1) * P], w, start=(k == 0), stop=(k == KT - 1))
                    filled(ins, f"zv{tt}")
                t = acquire(pe, layer, "dt")
                for tt in range(TT):
                    for k in range(KT):
                        w = ws[k // 2][:, (k % 2) * TMW + 2 * GW:(k % 2 + 1) * TMW]
                        ins = mm(t[:, tt * H:(tt + 1) * H], hT[:, k, tt * P:(tt + 1) * P], w,
                                 start=(k == 0), stop=(k == KT - 1))
                filled(ins, "dt")

            def lora(layer):
                need(pe, lora_in, layer, 1)
                pe.wait_ge(sw_sem, 16 * (layer + 1))
                for key, rows, src in (("lw", slice(0, 64), 6), ("la", slice(64, 128), 6), ("lg", slice(0, 128), 7)):
                    w = ww("g2") if key == "lg" else ww("w2a2")
                    t = acquire(pe, layer, key)
                    for m in range(2):
                        ins = mm(t[:, m * T:(m + 1) * T], w[rows, m * P:(m + 1) * P], pf[rows, src, :],
                                 start=True, stop=True)
                    filled(ins, key)

            def block_sum(layer, key, f, n, src):
                need(pe, f, layer, n)
                t = acquire(pe, layer, key)
                filled(mm(t, blk[:], src, start=True, stop=True), key)

            def head(h):
                return slice(HD * (h % 2), HD * (h % 2) + HD), h // 2

            def ssd(layer):
                need(pe, ssd_xbc, layer, 1)
                transposes(layer, "xt", [cv[:, m, tt * P:(tt + 1) * P] for tt in range(TT) for m in range(2)])
                need(pe, ssd_r, layer, 1)
                for key, h in (("dA", 0), ("dB", 2)):
                    t = acquire(pe, layer, key)
                    mm(t, m_gt[:], r0[:, h:h + 2, :], start=True, stop=False)
                    ins = mm(v3(t, 2)[:, :, P:T], ones[:], r1[:, h:h + 2, :], start=False, stop=True)
                    filled(ins, key)
                t = acquire(pe, layer, "d1")
                filled(mm(t, m_gt[:], r1, start=True, stop=True), "d1")
                for g in range(2):
                    t = acquire(pe, layer, f"sc{g}")
                    rows = slice(64 * g, 64 * g + 64)
                    mm(t[:, 0:T], cv[rows, 2, 0:P], cv[rows, 3, :], start=True, stop=True)
                    filled(mm(t[:, T:T + P], cv[rows, 2, P:T], cv[rows, 3, P:T], start=True, stop=True), f"sc{g}")
                t = acquire(pe, layer, "sy")
                need(pe, ssd_p, layer, 1)
                for h in range(H):
                    c = slice(h * HD, (h + 1) * HD)
                    mm(t[:, h * HD:(h + 1) * HD], L0[:, h, 0:P], xd[:, 0, c], start=True, stop=True)
                    o = t[:, T + h * HD:T + (h + 1) * HD]
                    mm(o, L0[:, h, P:T], xd[:, 0, c], start=True, stop=False)
                    ins = mm(o, L1[:, h, :], xd[:, 1, c], start=False, stop=True)
                filled(ins, "sy")

            def att_scores(layer):
                need(pe, att_qk, layer, 1)
                for key, tt, hs in ATT_TILES:
                    t = acquire(pe, layer, key)
                    n = P * (tt + 1)
                    for i, h in enumerate(hs):
                        rows, m = head(h)
                        ins = mm(t[:, i * n:(i + 1) * n], qk[rows, m, tt * P:(tt + 1) * P], qk[rows, 2 + m, 0:n],
                                 start=True, stop=True)
                    filled(ins, key)

            def att_values(layer):
                need(pe, att_p, layer, 1)
                transposes(layer, "P0", [a0[:, h, :] for h in range(H)])
                need(pe, att_p, layer, 2)
                transposes(layer, "P1", [a1[:, h, 0:P] for h in range(H)])
                transposes(layer, "P2", [a1[:, h, P:T] for h in range(H)])
                t = acquire(pe, layer, "ya")
                need(pe, att_pt, layer, 3)
                for h in range(H):
                    c = slice(GW + h * HD, GW + (h + 1) * HD)
                    mm(t[:, h * HD:(h + 1) * HD], pt0[:, h, :], zv[:, 0, c], start=True, stop=True)
                    o = t[:, T + h * HD:T + (h + 1) * HD]
                    mm(o, pt1[:, h, :], zv[:, 0, c], start=True, stop=False)
                    ins = mm(o, pt2[:, h, :], zv[:, 1, c], start=False, stop=True)
                filled(ins, "ya")

            def token_to_feature(layer, key, f, n, src):
                need(pe, f, layer, n)
                transposes(layer, key, [src[:, tt, m * P:(m + 1) * P] for m in range(2) for tt in range(TT)])

            def rwkv_products(layer, c):
                ch = slice(c * P, (c + 1) * P)
                for q, key in enumerate(PRODUCT_TILES):
                    t = acquire(pe, layer, (key, c))
                    for i, (a, b) in enumerate((((eX, cp), (kp, eX)), ((cp, eE), (kp, eE)))[q // 2]):
                        for m in range(2):
                            rows, _ = head(q % 2)
                            ins = mm(t[:, (2 * i + m) * P:(2 * i + m + 1) * P], a[rows, m, ch], b[rows, m, ch],
                                     start=True, stop=True)
                    filled(ins, (key, c))

            def rwkv_level(layer, c, l):
                t = acquire(pe, layer, ("X", c, l))
                need(pe, rk_off, layer, 7 * c + l + 1)
                if l:
                    need(pe, rk_tt, layer, 7 * c + l)
                for h in range(H):
                    ins = mm(t[:, h * P:(h + 1) * P], noff[:, l % 2, h, :], tt_[:, h, :] if l else ident[:],
                             start=True, stop=True)
                filled(ins, ("X", c, l))
                if l == 0:
                    return
                t = acquire(pe, layer, ("TT", c, l))
                need(pe, rk_x, layer, 6 * c + l)
                need(pe, rk_t, layer, 6 * c + l)
                for h in range(H):
                    ins = mm(t[:, h * P:(h + 1) * P], tm_[:, h, :], xs_[:, h, :], start=True, stop=True)
                filled(ins, ("TT", c, l))
                if l < 6:
                    t = acquire(pe, layer, ("T", c, l))
                    for h in range(H):
                        ins = mm(t[:, h * P:(h + 1) * P], xs_[:, h, :], tm_[:, h, :], start=True, stop=True)
                    filled(ins, ("T", c, l))

            def rwkv_solve(layer, c):
                ch = slice(c * P, (c + 1) * P)
                t = acquire(pe, layer, ("Z", c))
                need(pe, rk_mat, layer, 4 * c + 2)
                if c:
                    need(pe, rk_s, layer, 1)
                for m in range(2):
                    if c:
                        mm(t[:, m * P:(m + 1) * P], eX[:, m, ch], s0[:, m, :], start=True, stop=False)
                    for h in (2 * m, 2 * m + 1):
                        ins = mm(t[:, h * HD:(h + 1) * HD], m2[:, h, :], vt[:, c, h * HD:(h + 1) * HD],
                                 start=(c == 0), stop=(c == 0 or h % 2 == 1))
                filled(ins, ("Z", c))
                t = acquire(pe, layer, ("U", c))
                need(pe, rk_tt, layer, 7 * c + 7)
                need(pe, rk_z, layer, c + 1)
                for h in range(H):
                    ins = mm(t[:, h * HD:(h + 1) * HD], tt_[:, h, :], zs[:, h * HD:(h + 1) * HD], start=True, stop=True)
                filled(ins, ("U", c))
                need(pe, rk_u, layer, c + 1)
                if c == 0:
                    t = acquire(pe, layer, "S")
                    for m in range(2):
                        o = t[:, m * P:(m + 1) * P]
                        mm(o, bkt[:, m, :], us[:, m * P:(m + 1) * P], start=True, stop=False)
                        ins = mm(o, bkt[:, 2 + m, :], vt[:, 0, m * P:(m + 1) * P], start=False, stop=True)
                    filled(ins, "S")
                t = acquire(pe, layer, ("Y", c))
                need(pe, rk_mat, layer, 4 * c + 4)
                for m in range(2):
                    if c:
                        mm(t[:, m * P:(m + 1) * P], eE[:, m, ch], s0[:, m, :], start=True, stop=False)
                    for h in (2 * m, 2 * m + 1):
                        o = t[:, h * HD:(h + 1) * HD]
                        mm(o, mb[:, h, :], us[:, h * HD:(h + 1) * HD], start=(c == 0), stop=False)
                        ins = mm(o, mk[:, h, :], vt[:, c, h * HD:(h + 1) * HD], start=False,
                                 stop=(c == 0 or h % 2 == 1))
                filled(ins, ("Y", c))

            def rwkv_y(layer, c):
                need(pe, gn_y, layer, c + 1)
                t = acquire(pe, layer, ("yt", c))
                for m in range(2):
                    ins = pe.transpose(t[:, m * P:(m + 1) * P], gy[:, c, m * P:(m + 1) * P], ident[:])
                filled(ins, ("yt", c))

            def s5(layer):
                for j in range(8):
                    t = acquire(pe, layer, ("bu", j))
                    if j == 0:
                        need(pe, fm_out, layer, 5)
                    rows = slice(32 * (j % 4), 32 * (j % 4) + 32)
                    for i, w in enumerate((ww("b_re"), ww("b_im"))):
                        ins = mm(t[:, i * T:(i + 1) * T], w[rows, (j // 4) * P:(j // 4 + 1) * P], u5[rows, j // 4, :],
                                 start=True, stop=True)
                    filled(ins, ("bu", j))
                t = acquire(pe, layer, "y5")
                need(pe, s5_c, layer, 1)
                for j in range(8):
                    need(pe, s5_h, layer, j + 1)
                    o = t[:, (j // 4) * T:(j // 4 + 1) * T]
                    mm(o, cpad_re[:, j, :], z5[:, j, 0, :], start=(j % 4 == 0), stop=False)
                    ins = mm(o, cpad_im[:, j, :], z5[:, j, 1, :], start=False, stop=(j % 4 == 3))
                filled(ins, "y5")
                t = acquire(pe, layer, "glu")
                need(pe, s5_g, layer, 1)
                w = v3(ww("glu"), 2)
                for m in range(2):
                    for k in range(2):
                        ins = mm(t[:, m * T:(m + 1) * T], w[:, k, m * P:(m + 1) * P], g5[:, k, :],
                                 start=(k == 0), stop=(k == 1))
                filled(ins, "glu")
                t = acquire(pe, layer, "o5")
                need(pe, s5_sq, layer, 1)
                for k in range(2):
                    ins = mm(t[:, 0:T], ones[:], q5[:, k, :], start=(k == 0), stop=(k == 1))
                filled(ins, "o5")

            def out_projection(layer):
                ts = [acquire(pe, layer, ("wo", q)) for q in range(4)]
                need(pe, mix_done, layer, 4)
                for k in range(8):
                    w = unit(pe, layer, ("wo", k))
                    for q in range(4):
                        ins = mm(ts[q], mixT[:, k, (q // 2) * P:(q // 2 + 1) * P], w[:, (q % 2) * 512:(q % 2) * 512 + 512],
                                 start=(k == 0), stop=(k == 7))
                        if k == 7:
                            filled(ins, ("wo", q))
                    if k < 7:
                        ins.then_inc(wo_used.sem, 1)

            def gu_slot(e, q):
                pe.wait_ge(gu_full_s[q % R_GU], 16 * (GU_UNITS // R_GU) * e + 16 * (q // R_GU + 1))
                return guring[:, q % R_GU]

            def d_slot(e, q):
                pe.wait_ge(d_full_s[q % R_D], 16 * (D_UNITS // R_D) * e + 16 * (q // R_D + 1))
                return dring[:, q % R_D]

            def ffn(e, src, nb):
                def gate_up(c, qs):
                    for q in qs:
                        u = GUQ * c + q
                        w = gu_slot(e, u)
                        if q == 0 and c:
                            pe.wait_ge(av_ready.sem, av_ready.per * e + c)
                        for b in range(nb):
                            for kk_ in range(GUK):
                                k = q * GUK + kk_
                                ins = mm(ps[:, b, :], src[:, k, b * P:(b + 1) * P], w[:, kk_, :],
                                         start=(k == 0), stop=(k == KT - 1))
                            if q == GUQ - 1:
                                ins.then_inc((gu_done if b == nb - 1 else gu_done0).sem, 1)
                        if q < GUQ - 1:
                            ins.then_inc(gu_used.sem, 1)

                def turn(c):
                    pe.wait_ge(av_ready.sem, av_ready.per * e + c + 1)
                    for b in range(nb):
                        for f in range(2):
                            ins = pe.transpose(ps[:, 2, (2 * b + f) * P:(2 * b + f + 1) * P],
                                               av[:, b, f * P:(f + 1) * P], ident[:])
                    ins.then_inc(t_full.sem, 1)

                def down(c):
                    pe.wait_ge(avT_ready.sem, avT_ready.per * e + c + 1)
                    for f in range(2):
                        for hf in range(2):
                            u = (2 * c + f) * 2 + hf
                            w = d_slot(e, u)
                            for b in range(nb):
                                ins = mm(ps[:, 4 + 2 * b + hf, :], avT[:, b, f, :], w,
                                         start=(c == 0 and f == 0), stop=(c == NC_ - 1 and f == 1))
                            ins.then_inc((d_used if u < D_UNITS - 2 else y_done).sem, 1)

                for c in range(NC_):
                    gate_up(c, range(0, GUQ // 2))
                    if c:
                        turn(c - 1)
                    gate_up(c, range(GUQ // 2, GUQ))
                    if c:
                        down(c - 1)
                turn(NC_ - 1)
                down(NC_ - 1)

            def router():
                need(pe, h_evac, 1, 8)
                w = v3(ww("router"), KT)
                for tt in range(TT):
                    for k in range(KT):
                        ins = mm(ps[:, 0, tt * NE:(tt + 1) * NE], hT[:, k, tt * P:(tt + 1) * P], w[:, k, :],
                                 start=(k == 0), stop=(k == KT - 1))
                ins.then_inc(router_s.sem, 1)
                pe.wait_ge(router_d.sem, 1)
                sel = rt[:, 0:16]
                mm(ps[:, 1, 0:8], m_lt[:], sel[:, 0:8], start=True, stop=True)
                mm(ps[:, 1, 8:16], ones[:], sel[:, 0:8], start=True, stop=False)
                mm(ps[:, 1, 8:16], m_lt[:], sel[:, 8:16], start=False, stop=True)
                mm(ps[:, 1, 16:24], ones[:], sel[:, 0:8], start=True, stop=False)
                mm(ps[:, 1, 16:24], ones[:], sel[:, 8:16], start=False, stop=True).then_inc(router_s.sem, 1)

            def scatter(ve):
                pe.wait_ge(ys_ready.sem, 2 * ve + 2)
                pe.wait_ge(gt_ready.sem, ve + 1)
                for q in range(4):
                    if q >= 2:
                        pe.wait_ge(x_added.sem, 4 * ve + q - 1)
                    mm(ps[:, 1 + 2 * (q % 2), :], GT[:, q // 2, :], ys[:, (q % 2) * 512:(q % 2) * 512 + 512],
                       start=True, stop=True).then_inc(sc_full.sem, 1)

            def experts(first, ps_no):
                with pe.Fori(first, first + NE) as e:
                    ve = e - 1 + ps_no
                    pe.wait_ge(g_ready.sem, ve + 1)
                    for r in range(2):
                        for i in range(4):
                            k = 4 * r + i
                            for tt in range(TT):
                                ins = mm(ps[:, 6 + r, i * P:(i + 1) * P], xh[:, tt, k * P:(k + 1) * P], G[:, tt, :],
                                         start=(tt == 0), stop=(tt == TT - 1))
                        ins.then_inc(gat_full.sem, 1)
                    scatter(ve)
                    for tt in range(TT):
                        ins = pe.transpose(ps[:, 2, tt * P:(tt + 1) * P], Gg[:, tt, :], ident[:])
                    ins.then_inc(gt_full.sem, 1)
                    pe.wait_ge(xg_ready.sem, 2 * (e - 1) + 2)
                    pe.wait_ge(gt_ready.sem, ve + 2)
                    ffn(e, xgT, 1)
                scatter(first + NE - 1 + ps_no)

            pe.wait_ge(consts_pool.sem, 1)
            pe.wait_ge(consts_dve.sem, 1)
            for layer in range(DEPTH):
                norm_transpose(layer, "h", 1)
                for q in range(5):
                    fm(layer, q)
                lora(layer)
                fm(layer, 5)
                fm(layer, 6)
                block_sum(layer, "kks", rk_sq, 1, kk2)
                tm(layer)
                block_sum(layer, "bon", rk_bon, 1, kk2)
                fm(layer, 7)
                fm(layer, 8)
                ssd(layer)
                need(pe, rk_hat, layer, 1)
                transposes(layer, "vt", [pf[:, 4 + m, c * P:(c + 1) * P] for c in range(TT) for m in range(2)])
                transposes(layer, "bkt", [a[:, m, 0:P] for a in (cp, kp) for m in range(2)])
                token_to_feature(layer, "syt", ssd_n, 1, xs)
                need(pe, att_sq, layer, 1)
                for key, i in (("qs", 0), ("ks", 2)):
                    t = acquire(pe, layer, key)
                    filled(mm(t, blk[:], sq[:, i:i + 2, :], start=True, stop=True), key)
                for c in range(TT):
                    rwkv_products(layer, c)
                    for l in range(7):
                        rwkv_level(layer, c, l)
                    if c == 0:
                        need(pe, rk_tok, layer, 2)
                    rwkv_solve(layer, c)
                for c in range(TT):
                    rwkv_y(layer, c)
                att_scores(layer)
                att_values(layer)
                token_to_feature(layer, "yat", att_n, 1, ya)
                s5(layer)
                out_projection(layer)
                norm_transpose(layer, "h2", 2)
                if layer == 0:
                    need(pe, h_evac, 0, 8)
                    ffn(0, hT, 2)
                else:
                    router()
                    experts(1, 0)
                    pe.wait_ge(router_d.sem, 2)
                    over = pe.value_load(ovf[0:1, 0:1])
                    with pe.If(over > 0):
                        experts(1 + NE, 1)

        @block.scalar
        def _(act):
            do = Chain(act, ch_act)
            A = act.activation

            def rsqrt(src, dst, f=None):
                do(A(dst, src, ACT.Ln))
                do(A(dst, dst, ACT.Exp, scale=-0.5), f)

            def norm(layer, n):
                if layer == 0 and n == 1:
                    act.wait_ge(x_in_sem, 16)
                elif n == 1:
                    need(act, x_ffn, layer - 1, 4)
                else:
                    need(act, x_mixed, layer, 4)
                for tt in range(TT):
                    ins = A(xh[:, tt, :], x[:, tt, :], ACT.Square, accum_out=ssx[:, tt:tt + 1])
                    do(ins, sumsq if tt == 1 else None)
                need(act, rs_in, layer, n)
                rsqrt(ssx, rsx, rs_out)

            def evac_fm(layer, q):
                t = has(act, layer, ("fm", q))
                dst = (rk[:, 2 * q:2 * q + 2, 1:1 + T] if q < 4 else u5 if q == 4 else
                       xbc[:, 2 * (q - 5):2 * (q - 5) + 2, CONV - 1:CONV - 1 + T] if q < 7 else
                       qk[:, 2 * (q - 7):2 * (q - 7) + 2, :])
                do(act.copy(dst, v3(t, 2)), fm_out)

            def bank_copy(layer, key, dst, f, n=512, m=None):
                t = has(act, layer, key, 0, n)
                do(act.copy(dst, v3(t, m) if m else t), f)

            def poles_act():
                act.wait_ge(par_sem, 16)
                do(A(S("dt"), par3("log_dt"), ACT.Exp), pole_a)
                act.wait_ge(pole_d.sem, 1)
                do(A(S("mag"), S("da"), ACT.Exp), pole_a)
                act.wait_ge(pole_d.sem, 2)
                do(A(S("sin"), S("r"), ACT.Sin))
                do(A(S("cos"), S("r2"), ACT.Sin), pole_a)

            act.preload_act_table_set("natural_log_exp_and_others")
            poles_act()
            act.wait_ge(consts_pool.sem, 1)
            for layer in range(DEPTH):
                act.preload_act_table_set("natural_log_exp_and_others")
                norm(layer, 1)
                for q in range(4):
                    evac_fm(layer, q)
                evac_fm(layer, 4)
                need(act, rk_mixed, layer, 1)
                do(A(pf[0:64, 6, :], pf[0:64, 6, :], ACT.Tanh))
                do(A(pf[:, 7, :], pf[:, 7, :], ACT.Sigmoid), lora_in)
                for key, dst, b in (("lw", rw_b, "w0"), ("la", sA, "a0")):
                    t = has(act, layer, key)
                    for m in range(2):
                        do(A(dst[:, m, :], t[:, m * T:(m + 1) * T], ACT.Sigmoid, bias=pp(layer, b, m, 1)),
                           rk_act if m else None)
                bank_copy(layer, "lg", rw_g, rk_act, m=2)
                evac_fm(layer, 5)
                evac_fm(layer, 6)
                bank_copy(layer, "zv0", zv[:, 0, :], zv_out)
                bank_copy(layer, "zv1", zv[:, 1, :], zv_out)
                need(act, ssd_cv, layer, 1)
                do(A(sg, cv, ACT.Sigmoid))
                do(A(xd, zv[:, :, 0:GW], ACT.Sigmoid), ssd_sg)
                act.preload_act_table_set("natural_log_exp_and_others")
                need(act, rk_cs, layer, 1)
                for m in range(2):
                    for c in range(TT):
                        ch = slice(c * P, (c + 1) * P)
                        i = 2 * m + c
                        do(A(eE[:, m, ch], cs[:, m, ch], ACT.Exp, bias=ncm[:, i:i + 1]))
                        do(A(eX[:, m, ch], cp[:, m, ch], ACT.Exp, bias=ncm[:, i:i + 1]))
                        do(A(eM[:, m, ch], cs[:, m, ch], ACT.Exp, scale=-1.0, bias=cs[:, m, c * P + 63:c * P + 64]))
                do(A(dec, dec, ACT.Exp), rk_exp)
                need(act, rk_ss, layer, 1)
                rsqrt(rsq, rsq, rk_rs)
                need(act, dt_a, layer, 1)
                do(A(ael, pp(layer, "a_log"), ACT.Exp))
                do(A(dte, dta, ACT.Exp, scale=-1.0), dt_b)
                need(act, dt_c, layer, 1)
                do(A(dtl, dtu, ACT.Ln), dt_d)
                evac_fm(layer, 7)
                evac_fm(layer, 8)
                bank_copy(layer, "xt", xs, ssd_xs, m=2)
                for key, dst in (("dA", L0[:, 0:2, :]), ("dB", L0[:, 2:4, :]), ("d1", L1)):
                    t = has(act, layer, key)
                    do(A(dst, v3(t, 4 if key == "d1" else 2), ACT.Exp), ssd_l)
                need(act, ssd_y, layer, 1)
                for tt in range(TT):
                    do(A(xd[:, tt, :], xs[:, tt, :], ACT.Square, accum_out=ssy[:, tt:tt + 1]), ssd_ss if tt else None)
                need(act, ssd_v, layer, 1)
                rsqrt(ssy, ssy, ssd_rs)
                bank_copy(layer, "vt", vt, rk_tok, m=2)
                bank_copy(layer, "bkt", bkt, rk_tok, m=4)
                need(act, att_ss, layer, 2)
                rsqrt(sq, sq, att_rs)
                for c in range(TT):
                    for l in range(1, 7):
                        t = has(act, layer, ("X", c, l))
                        do(act.copy(xs_, v3(t, H)), rk_x)
                    bank_copy(layer, ("Z", c), zs, rk_z, 256)
                    bank_copy(layer, ("U", c), us, rk_u, 256)
                    need(act, gn_in, layer, c + 1)
                    rsqrt(gst[:, 4:8], gst[:, 4:8], gn_rs)
                need(act, att_m, layer, 1)
                do(A(a0, a0, ACT.Exp), att_e)
                need(act, att_m, layer, 2)
                do(A(a1, a1, ACT.Exp), att_e)
                bank_copy(layer, "P0", pt0, att_pt, m=4)
                bank_copy(layer, "P1", pt1, att_pt, m=4)
                bank_copy(layer, "P2", pt2, att_pt, m=4)
                t = has(act, layer, "ya")
                for tt in range(TT):
                    do(A(sq[:, tt, :], t[:, tt * T:(tt + 1) * T], ACT.Square, accum_out=ssa[:, tt:tt + 1]),
                       att_y if tt else None)
                need(act, att_v, layer, 1)
                rsqrt(ssa, ssa, att_rs2)
                need(act, s5_y, layer, 1)
                do(A(g5, y5, ACT.Gelu_apprx_tanh), s5_g)
                t = has(act, layer, "glu")
                for m in range(2):
                    do(A(g5s[:, m, :], t[:, m * T:(m + 1) * T], ACT.Sigmoid, bias=pp(layer, "glu_b", m, 1)),
                       s5_sig if m else None)
                act.preload_act_table_set("natural_log_exp_and_others")
                need(act, s5_ss, layer, 1)
                rsqrt(y5[:, 0, :], y5[:, 0, :], s5_rs)
                norm(layer, 2)

                def ffn(e, nb):
                    for c in range(NC_ + 1):
                        if c:
                            act.wait_ge(t_full.sem, NC_ * e + c)
                            act.copy(avT[:, 0:nb], ps[:, 2, 0:nb * 256].rearrange("p (b f s) -> p b f s", b=nb, f=2)) \
                                .then_inc(avT_ready.sem, 1)
                        if c < NC_:
                            for b in range(nb):
                                act.wait_ge((gu_done if b == nb - 1 else gu_done0).sem, NC_ * e + c + 1)
                                ins = A(sil[:, b, :], ps[:, b, 0:FC], ACT.Silu)
                            ins.then_inc(sil_ready.sem, 1)

                if layer == 0:
                    ffn(0, 2)
                    continue
                act.wait_ge(router_d.sem, 1)
                do(A(rl, rl, ACT.Exp), router_a)

                def experts(first, ps_no):
                    with act.Fori(first, first + NE) as e:
                        ffn(e, 1)
                        act.wait_ge(y_done.sem, 2 * e + 2)
                        for hf in range(2):
                            act.copy(ys[:, hf * 512:(hf + 1) * 512], ps[:, 4 + hf, :]).then_inc(ys_ready.sem, 1)

                act.wait_ge(router_d.sem, 2)
                experts(1, 0)
                act.wait_ge(router_d.sem, 2)
                over = act.value_load(ovf[0:1, 0:1])
                with act.If(over > 0):
                    experts(1 + NE, 1)

        @block.gpsimd
        def _(pool):
            do = Chain(pool, ch_pool)

            def fill_mask(dst, base, mult, pattern, op):
                do(pool.memset(dst, 1.0))
                do(pool.affine_select(out=dst, in_=dst, compare_op=op, fill=0.0, base=base,
                                      pattern=pattern, channel_multiplier=mult))

            do(pool.memset(ones[:], 1.0))
            do(pool.memset(ident[:], 0.0))
            do(pool.affine_select(out=ident[:], in_=ident[:], compare_op=ALU.not_equal, fill=1.0, base=0,
                                  pattern=[[-1, P]], channel_multiplier=1))
            do(pool.memset(blk[:], 0.0))
            do(pool.memset(blk[0:64, 0:64], 1.0))
            do(pool.memset(blk[64:128, 64:128], 1.0))
            fill_mask(m_gt[:], 0, 1, [[-1, P]], ALU.is_gt)
            fill_mask(m_lt[:], 0, -1, [[1, P]], ALU.is_gt)
            fill_mask(m_leo[:], 0, -1, [[1, T]], ALU.is_ge)
            do(pool.memset(tie[:], 1.0))
            do(pool.affine_select(out=tie[:], in_=tie[:], compare_op=ALU.is_gt, fill=0.0, base=0,
                                  pattern=[[1, NE], [-1, NE]], channel_multiplier=0))
            do(pool.iota(iota[:], pattern=[[1, P]], base=0, channel_multiplier=0, allow_small_or_imprecise_dtypes=True))
            do(pool.iota(it_x[:], pattern=[[1, P]], base=0, channel_multiplier=0))
            do(pool.iota(it_y[:], pattern=[[0, P]], base=0, channel_multiplier=1))
            do(pool.iota(it_d[:, 0:P], pattern=[[-1, P]], base=0, channel_multiplier=1))
            do(pool.iota(it_d[:, P:384], pattern=[[-1, T]], base=P, channel_multiplier=1), consts_pool)

            def tables(layer):
                pool.wait_ge(poles.sem, 1)
                if layer:
                    need(pool, s5_back, layer - 1, 8)
                do(pool.memset(e_re[:, :, 0:1], 1.0))
                do(pool.memset(e_im[:, :, 0:1], 0.0))
                do(pool.tensor_copy(pw[:, 0, :], s5p[:, layer, 0, :]))
                do(pool.tensor_copy(pw[:, 1, :], s5p[:, layer, 1, :]))
                k = 1
                while k < T:
                    nh = 2 if k == P else 1
                    for hh in range(nh):
                        js = slice(hh * (8 // nh), (hh + 1) * (8 // nh))
                        n = 8 // nh
                        tmp = tab_tmp[:, 0:n * k].rearrange("p (j t) -> p j t", j=n)
                        c_ = bc(pw[:, 0, js], [P, n, k], 2)
                        s_ = bc(pw[:, 1, js], [P, n, k], 2)
                        re, im = e_re[:, js, 0:k], e_im[:, js, 0:k]
                        do(pool.tensor_tensor(e_re[:, js, k:2 * k], re, c_, ALU.mult))
                        do(pool.tensor_tensor(tmp, im, s_, ALU.mult))
                        do(pool.tensor_tensor(e_re[:, js, k:2 * k], e_re[:, js, k:2 * k], tmp, ALU.subtract))
                        do(pool.tensor_tensor(e_im[:, js, k:2 * k], re, s_, ALU.mult))
                        do(pool.tensor_tensor(tmp, im, c_, ALU.mult))
                        do(pool.tensor_tensor(e_im[:, js, k:2 * k], e_im[:, js, k:2 * k], tmp, ALU.add))
                    k *= 2
                    if k < T:
                        do(pool.tensor_tensor(pw[:, 2, :], pw[:, 1, :], pw[:, 1, :], ALU.mult))
                        do(pool.tensor_tensor(pw[:, 1, :], pw[:, 0, :], pw[:, 1, :], ALU.mult))
                        do(pool.tensor_tensor(pw[:, 1, :], pw[:, 1, :], pw[:, 1, :], ALU.add))
                        do(pool.tensor_tensor(pw[:, 0, :], pw[:, 0, :], pw[:, 0, :], ALU.mult))
                        do(pool.tensor_tensor(pw[:, 0, :], pw[:, 0, :], pw[:, 2, :], ALU.subtract))
                do(pool.tensor_copy(pw[:, 2, :], pw[:, 0, :]), tab)

            def c_rows(layer):
                pool.wait_ge(sw_sem, 16 * (layer + 1))
                fr = bc(s5p[:, layer, 3, :], [P, 8, 16], 2)
                fi = bc(s5p[:, layer, 4, :], [P, 8, 16], 2)
                cr, ci = (v3(ww(n), 8) for n in ("c_re", "c_im"))
                o_re, o_im, tmp = (v3(c5[:, i, :], 8) for i in range(3))
                do(pool.tensor_tensor(o_re, cr, fr, ALU.mult))
                do(pool.tensor_tensor(tmp, ci, fi, ALU.mult))
                do(pool.tensor_tensor(o_re, o_re, tmp, ALU.subtract))
                do(pool.tensor_tensor(o_im, cr, fi, ALU.mult))
                do(pool.tensor_tensor(tmp, ci, fr, ALU.mult))
                do(pool.tensor_tensor(o_im, o_im, tmp, ALU.add))
                do(pool.tensor_scalar(o_im, o_im, -1.0, None, ALU.mult))
                need(pool, rk_tok, layer, 1)
                need(pool, rk_hat, layer, 1)
                do(pool.memset(cpad_re, 0.0))
                do(pool.memset(cpad_im, 0.0))
                for src, dst in ((o_re, cpad_re), (o_im, cpad_im)):
                    for j in range(8):
                        for g in range(2):
                            rows = slice(64 * g, 64 * g + 64)
                            c0 = 32 * (j % 4) + 16 * g
                            ins = pool.tensor_copy(dst[rows, j, c0:c0 + 16], src[rows, j, :])
                            last = j == 7 and g == 1
                            if last and dst is cpad_im:
                                do(ins, s5_c)
                            elif last:
                                do(ins)

            for layer in range(DEPTH):
                tables(layer)
                need(pool, ssd_a, layer, 1)
                for h0 in (0, 2):
                    do(pool.tensor_tensor(r0[:, h0:h0 + 2, :], bc(m_leo[:], [P, 2, T], 1),
                                          bc(sa[:, h0:h0 + 2], [P, 2, T], 2), ALU.mult))
                do(pool.tensor_tensor(r1, bc(m_le, [P, H, P], 1), bc(sa[:, 4:8], [P, H, P], 2), ALU.mult), ssd_r)
                c_rows(layer)
                for c in range(TT):
                    for l in range(7):
                        if l == 0:
                            need(pool, rk_mat, layer, 4 * c + 2)
                            if c:
                                need(pool, rk_x, layer, 6)
                        elif l == 2:
                            need(pool, rk_tt, layer, 7 * c + 1)
                        elif l > 2:
                            need(pool, rk_x, layer, 6 * c + l - 2)
                        do(pool.tensor_tensor(noff[:, l % 2], nm, bc(lvl[:, l, :], [P, H, P], 1), ALU.mult), rk_off)
                pool.wait_ge(tab.sem, layer + 1)
                for j in range(8):
                    need(pool, s5_in, layer, j + 1)
                    b = j % 2
                    do(pool.tensor_tensor(z5[:, j, 0, :], p5[:, b, 0, 0, :], p5[:, b, 1, 1, :], ALU.add))
                    do(pool.tensor_tensor(z5[:, j, 1, :], p5[:, b, 0, 1, :], p5[:, b, 1, 0, :], ALU.subtract), s5_z)
                for j in range(8):
                    need(pool, s5_back, layer, j + 1)
                    b = j % 2
                    do(pool.tensor_tensor(z5[:, j, 0, :], p5[:, b, 0, 0, :], p5[:, b, 1, 1, :], ALU.subtract))
                    do(pool.tensor_tensor(z5[:, j, 1, :], p5[:, b, 1, 0, :], p5[:, b, 0, 1, :], ALU.add), s5_h)

        @block.vector
        def _(dve):
            do = Chain(dve, ch_dve)
            tt_op, ts, stt = dve.tensor_tensor, dve.tensor_scalar, dve.scalar_tensor_tensor

            def constants():
                dve.wait_ge(consts_pool.sem, 1)
                do(tt_op(it_x[:], it_x[:], it_y[:], ALU.bitwise_xor))
                for l in range(7):
                    do(ts(it_y[:], it_x[:], l, None, ALU.logical_shift_right))
                    do(stt(lvl[:, l, :], it_y[:], 1.0, m_gt[:], ALU.is_equal, ALU.mult))
                for cnt, bias, d in ((cnt0, bias0, it_d[:, 0:P]), (cnt1, bias1, it_d[:, P:384])):
                    n = d.shape[1]
                    c = cnt[:]
                    dist, w = xflat[:, 0:n], xflat[:, 512:512 + n]
                    wi = xflat[:, 1024:1024 + n].bitcast(I32)
                    do(dve.tensor_copy(dist, d))
                    do(dve.memset(c, 0.0))
                    for window, dil in PATTERNS:
                        do(ts(wi, d, dil - 1, None, ALU.bitwise_and))
                        do(ts(w, wi, 0.0, None, ALU.is_equal))
                        do(stt(w, dist, float(window), w, ALU.is_le, ALU.mult))
                        do(tt_op(c, c, w, ALU.add))
                    do(stt(c, dist, 0.0, c, ALU.is_ge, ALU.mult))
                    do(ts(w, c, 0.0, -1e30, ALU.is_equal, ALU.mult))
                    for h in range(H):
                        do(stt(bias[:, h, :], dist, -LOG2E_SLOPES[h], w, ALU.mult, ALU.add))

            def pole_constants():
                inv, magic = 1.0 / (2 * np.pi), 12582912.0
                c1 = 6.28125
                c2 = float(np.float32(np.float16(2 * np.pi - c1)))
                c3 = float(np.float32(2 * np.pi - c1 - c2))
                dve.wait_ge(pole_a.sem, 1)
                are, aim = par3("a_re"), par3("a_im")
                do(tt_op(S("da"), S("dt"), are, ALU.mult), pole_d)
                do(tt_op(S("r"), S("dt"), aim, ALU.mult))
                do(ts(S("k"), S("r"), inv, magic, ALU.mult, ALU.add))
                do(ts(S("k"), S("k"), -magic, None, ALU.add))
                for c_ in (c1, c2, c3):
                    do(stt(S("r"), S("k"), -c_, S("r"), ALU.mult, ALU.add))
                pi = float(np.nextafter(np.float32(np.pi), np.float32(0)))
                do(ts(S("r"), S("r"), pi, -pi, ALU.min, ALU.max))
                do(ts(S("r2"), S("r"), float(np.pi / 2), None, ALU.add))
                do(ts(S("k"), S("r2"), pi, None, ALU.is_gt))
                do(stt(S("r2"), S("k"), float(-2 * np.pi), S("r2"), ALU.mult, ALU.add))
                do(ts(S("r2"), S("r2"), pi, -pi, ALU.min, ALU.max), pole_d)
                dve.wait_ge(pole_a.sem, 3)
                do(dve.tensor_copy(s5p[:, :, 0, :], S("cos")))
                do(dve.tensor_copy(s5p[:, :, 1, :], S("sin")))
                do(dve.tensor_copy(s5p[:, :, 2, :], S("mag")))
                do(tt_op(S("cos"), S("cos"), S("mag"), ALU.mult))
                do(tt_op(S("sin"), S("sin"), S("mag"), ALU.mult))
                do(ts(S("cos"), S("cos"), -1.0, None, ALU.add))
                do(tt_op(S("k"), are, are, ALU.mult))
                do(tt_op(S("r"), aim, aim, ALU.mult))
                do(tt_op(S("k"), S("k"), S("r"), ALU.add))
                do(dve.reciprocal(S("k"), S("k")))
                do(tt_op(S("r"), S("cos"), are, ALU.mult))
                do(tt_op(S("r2"), S("sin"), aim, ALU.mult))
                do(tt_op(S("r"), S("r"), S("r2"), ALU.add))
                do(tt_op(s5p[:, :, 3, :], S("r"), S("k"), ALU.mult))
                do(tt_op(S("r"), S("sin"), are, ALU.mult))
                do(tt_op(S("r2"), S("cos"), aim, ALU.mult))
                do(tt_op(S("r"), S("r"), S("r2"), ALU.subtract))
                do(tt_op(s5p[:, :, 4, :], S("r"), S("k"), ALU.mult), poles)

            def norm(layer, n):
                need(dve, sumsq, layer, n)
                do(ts(ssx, ssx, 1.0 / D, EPS, ALU.mult, ALU.add), rs_in)
                need(dve, rs_out, layer, n)
                for tt in range(TT):
                    do(ts(xh[:, tt, :], x[:, tt, :], rsx[:, tt:tt + 1], None, ALU.mult), xh_ready if tt else None)
                g = pp(layer, "ln_mix" if n == 1 else "ln_ffn")
                for q in range(4):
                    t = has(dve, layer, ("h" if n == 1 else "h2", q))
                    k = 4 * (q % 2)
                    do(tt_op(hT[:, k:k + 4, (q // 2) * P:(q // 2 + 1) * P], v3(t, 4),
                             bc(g[:, k:k + 4], [P, 4, P], 2), ALU.mult), h_evac)

            def rwkv_mix(layer):
                for q in range(4):
                    need(dve, fm_out, layer, q + 1)
                    m = slice(2 * q, 2 * q + 2)
                    do(tt_op(pf[:, m, :], rk[:, m, 0:T], rk[:, m, 1:1 + T], ALU.subtract))
                    for i in (2 * q, 2 * q + 1):
                        do(stt(pf[:, i, :], pf[:, i, :], pp(layer, "mu", i, 1), rk[:, i, 1:1 + T], ALU.mult, ALU.add),
                           rk_mixed if i == 7 else None)

            def conv(layer):
                need(dve, fm_out, layer, 7)
                for m in range(4):
                    w = [pp(layer, "conv_w", 4 * m + i, 1) for i in range(CONV)]
                    do(ts(cv[:, m, :], xbc[:, m, 0:T], w[0], pp(layer, "conv_b", m, 1), ALU.mult, ALU.add))
                    for i in range(1, CONV):
                        do(stt(cv[:, m, :], xbc[:, m, i:i + T], w[i], cv[:, m, :], ALU.mult, ALU.add),
                           ssd_cv if (m, i) == (3, CONV - 1) else None)

            def rwkv_decay(layer):
                need(dve, rk_act, layer, 1)
                do(ts(rw_b, rw_b, -DECAY, None, ALU.mult))
                for m in range(2):
                    for c in range(TT):
                        ch = slice(c * P, (c + 1) * P)
                        do(dve.tensor_tensor_scan(cs[:, m, ch], ones[:], rw_b[:, m, ch], 0.0, ALU.mult, ALU.add))
                do(tt_op(cp, cs, rw_b, ALU.subtract))
                do(ts(ncm.rearrange("p (m c) -> p m c", m=2), cs[:, :, 63:T:P], -1.0, None, ALU.mult))
                d3 = dec.rearrange("p (m c) -> p m c", c=1)
                do(tt_op(d3, cs[:, :, P - 1:P], cs[:, :, 63:64], ALU.subtract))
                do(tt_op(d3, d3, cs[:, :, P + 63:P + 64], ALU.add), rk_cs)

            def rwkv_keys(layer):
                need(dve, rk_act, layer, 2)
                for m in range(2):
                    do(ts(kp[:, m, :], sA[:, m, :], 1.0, pp(layer, "k_a", m, 1), ALU.subtract, ALU.mult))
                do(stt(kp, kp, 1.0, pf[:, 2:4, :], ALU.add, ALU.mult))
                t = has(dve, layer, "kks")
                do(ts(rsq, v3(t, 2), 1e-12, None, ALU.add), rk_ss)
                for m in range(2):
                    do(stt(kk2[:, m, :], pf[:, m, :], pp(layer, "r_k", m, 1), kp[:, m, :], ALU.mult, ALU.mult),
                       rk_bon if m else None)

            def rwkv_hats(layer):
                need(dve, rk_rs, layer, 1)
                do(tt_op(kk, kk, rsq, ALU.mult))
                do(stt(eX, kk, -1.0, eX, ALU.mult, ALU.mult))
                do(tt_op(cp, kk, sA, ALU.mult))
                do(tt_op(cp, cp, eM, ALU.mult))
                do(tt_op(kp, kp, eM, ALU.mult))
                t = has(dve, layer, "bon")
                do(tt_op(rw_b, v3(t, 2), pf[:, 4:6, :], ALU.mult), rk_bonus)
                do(tt_op(eE, eE, pf[:, 0:2, :], ALU.mult), rk_hat)

            def dt_first(layer):
                t = has(dve, layer, "dt", 0, 2 * H)
                do(tt_op(dtr3, v3(t, 2), bc(pp(layer, "dt_bias"), [P, 2, H], 1), ALU.add), dt_out)
                do(stt(dta, dtr, -1.0, dtr, ALU.mult, ALU.max), dt_a)

            def dt_rest(layer):
                need(dve, dt_b, layer, 1)
                do(ts(dtu, dte, 1.0, None, ALU.add), dt_c)
                do(stt(dta, dtu, -1.0, dte, ALU.add, ALU.subtract))
                do(dve.reciprocal(dte, dtu))
                do(tt_op(dta, dta, dte, ALU.mult))
                need(dve, dt_d, layer, 1)
                do(tt_op(dtl, dtl, dta, ALU.subtract))
                do(stt(dtr, dtr, 0.0, dtl, ALU.max, ALU.add))
                do(stt(sa.rearrange("p (a h) -> p a h", a=2), dtr3, -1.0, bc(ael, [P, 2, H], 1), ALU.mult, ALU.mult),
                   ssd_a)

            def heads(a):
                return a.rearrange("p a (h e) -> p (a h) e", h=H)

            def ssd(layer):
                need(dve, ssd_xs, layer, 1)
                do(tt_op(heads(xd), heads(xs), bc(dtr, [P, 2 * H, HD], 2), ALU.mult))
                for g in range(2):
                    t = has(dve, layer, f"sc{g}")
                    do(tt_op(sc0[:, g, :], t[:, 0:T], m_leo[:], ALU.mult))
                    do(tt_op(sc1[:, g, :], t[:, T:T + P], m_le, ALU.mult), ssd_sc)
                need(dve, ssd_l, layer, 3)
                for g in range(2):
                    do(tt_op(L0[:, 2 * g:2 * g + 2, :], L0[:, 2 * g:2 * g + 2, :], bc(sc0[:, g, :], [P, 2, T], 1),
                             ALU.mult))
                    do(tt_op(L1[:, 2 * g:2 * g + 2, :], L1[:, 2 * g:2 * g + 2, :], bc(sc1[:, g, :], [P, 2, P], 1),
                             ALU.mult), ssd_p if g else None)
                for tt in range(TT):
                    a = xs[:, tt, :].rearrange("p (h e) -> p h e", h=H)
                    do(tt_op(a, a, bc(pp(layer, "ssd_d"), [P, H, HD], 2), ALU.mult))
                t = has(dve, layer, "sy")
                do(tt_op(xs, v3(t, 2), xs, ALU.add))
                do(tt_op(xs, xs, zv[:, :, 0:GW], ALU.mult), ssd_y)
                need(dve, ssd_ss, layer, 1)
                do(ts(ssy, ssy, 1.0 / GW, EPS, ALU.mult, ALU.add), ssd_v)
                need(dve, ssd_rs, layer, 1)
                for tt in range(TT):
                    do(ts(xs[:, tt, :], xs[:, tt, :], ssy[:, tt:tt + 1], None, ALU.mult), ssd_n if tt else None)

            def to_mix(layer, key, m, gain):
                t = has(dve, layer, key)
                do(tt_op(mixT[:, m:m + 2, :], v3(t, 2), bc(pp(layer, gain), [P, 2, T], 2), ALU.mult), mix_done)

            def rwkv_matrices(layer, c):
                if c:
                    need(dve, rk_off, layer, 7)
                for q, key in enumerate(PRODUCT_TILES):
                    t = has(dve, layer, (key, c))
                    for i, (dst, mask) in enumerate((((nm, m_gt[:]), (m2, m_lt[:])), ((mb, m_le), (mk, m_le)))[q // 2]):
                        do(tt_op(dst[:, q % 2::2, :], v3(t[:, i * T:(i + 1) * T], 2), bc(mask, [P, 2, P], 1), ALU.mult),
                           rk_mat if i else None)

            def rwkv_levels(layer, c):
                idb = bc(ident[:], [P, H, P], 1)
                need(dve, rk_off, layer, 7 * c + 1)
                do(tt_op(tm_, noff[:, 0], idb, ALU.add), rk_t)
                t = has(dve, layer, ("X", c, 0))
                do(tt_op(tt_, v3(t, H), idb, ALU.add), rk_tt)
                for l in range(1, 7):
                    t = has(dve, layer, ("TT", c, l))
                    do(tt_op(tt_, v3(t, H), tt_, ALU.add), rk_tt)
                    if l < 6:
                        t = has(dve, layer, ("T", c, l))
                        do(tt_op(tm_, v3(t, H), tm_, ALU.add), rk_t)

            def group_norm(layer, c):
                t = has(dve, layer, ("Y", c), 0, GW)
                y3 = t.rearrange("p (h e) -> p h e", h=H)
                g3 = gy[:, c, :].rearrange("p (h e) -> p h e", h=H)
                k3 = gsq.rearrange("p (h e) -> p h e", h=H)
                mean, var = gst[:, 0:4], gst[:, 4:8]
                do(dve.tensor_reduce(mean, y3, AX.X, ALU.add))
                do(ts(mean, mean, 1.0 / HD, None, ALU.mult))
                do(tt_op(g3, y3, bc(mean, [P, H, HD], 2), ALU.subtract))
                do(tt_op(k3, g3, g3, ALU.mult))
                do(dve.tensor_reduce(var, k3, AX.X, ALU.add))
                do(ts(var, var, 1.0 / HD, GN_EPS, ALU.mult, ALU.add), gn_in)
                need(dve, gn_rs, layer, c + 1)
                do(tt_op(g3, g3, bc(var, [P, H, HD], 2), ALU.mult), gn_y)

            def rwkv_out(layer):
                for c in range(TT):
                    t = has(dve, layer, ("yt", c), 0, 256)
                    for m in range(2):
                        do(ts(mixT[:, 4 + m, c * P:(c + 1) * P], t[:, m * P:(m + 1) * P], pp(layer, "ln_w", m, 1),
                              pp(layer, "ln_b", m, 1), ALU.mult, ALU.add), rk_yt if m else None)
                o = mixT[:, 4:6, :]
                do(tt_op(o, o, rw_b, ALU.add))
                do(tt_op(o, o, rw_g, ALU.mult), mix_done)

            def attention(layer):
                for tt, a, bias in ((0, a0, bias0), (1, a1, bias1)):
                    n = P * (tt + 1)
                    mx = amx[:, tt * H:(tt + 1) * H]
                    for key, _, hs in ATT_TILES[2 * tt:2 * tt + 2]:
                        t = has(dve, layer, key, 0, 2 * n)
                        do(stt(a[:, hs[0]::2, :], v3(t, 2), HD ** -0.5, bias[:, hs[0]::2, :], ALU.mult, ALU.add),
                           att_s)
                    do(dve.tensor_reduce(mx, a, AX.X, ALU.max))
                    do(tt_op(a, a, bc(mx, [P, H, n], 2), ALU.subtract), att_m)
                for tt, a, cnt in ((0, a0, cnt0), (1, a1, cnt1)):
                    n = P * (tt + 1)
                    mx = amx[:, tt * H:(tt + 1) * H]
                    need(dve, att_e, layer, tt + 1)
                    do(tt_op(a, a, bc(cnt[:], [P, H, n], 1), ALU.mult))
                    do(dve.tensor_reduce(mx, a, AX.X, ALU.add))
                    do(dve.reciprocal(mx, mx))
                    do(tt_op(a, a, bc(mx, [P, H, n], 2), ALU.mult), att_p)
                need(dve, att_y, layer, 1)
                do(ts(ssa, ssa, 1.0 / GW, EPS, ALU.mult, ALU.add), att_v)
                need(dve, att_rs2, layer, 1)
                t = has(dve, layer, "ya")
                for tt in range(TT):
                    do(ts(ya[:, tt, :], t[:, tt * T:(tt + 1) * T], ssa[:, tt:tt + 1], None, ALU.mult),
                       att_n if tt else None)
                to_mix(layer, "yat", 2, "att_out")

            def s5(layer):
                dve.wait_ge(tab.sem, layer + 1)

                def products(j, src, f):
                    b = j % 2
                    do(tt_op(p5[:, b, 0], src, bc(e_re[:, j, :], [P, 2, T], 1), ALU.mult))
                    do(tt_op(p5[:, b, 1], src, bc(e_im[:, j, :], [P, 2, T], 1), ALU.mult), f)

                for j in range(8):
                    t = has(dve, layer, ("bu", j))
                    if j >= 2:
                        need(dve, s5_z, layer, j - 1)
                    products(j, v3(t, 2), s5_in)
                for j in range(8):
                    need(dve, s5_z, layer, j + 1)
                    for i in range(2):
                        z = z5[:, j, i, :]
                        do(dve.tensor_tensor_scan(z, s5p[:, layer, 2, j:j + 1].to_broadcast([P, T]), z, 0.0,
                                                  ALU.mult, ALU.add))
                    if j == 0:
                        need(dve, s5_z, layer, 8)
                    if j >= 2:
                        need(dve, s5_h, layer, j - 1)
                    products(j, z5[:, j], s5_back)
                t = has(dve, layer, "y5")
                for m in range(2):
                    do(stt(y5[:, m, :], u5[:, m, :], pp(layer, "s5_d", m, 1), t[:, m * T:(m + 1) * T],
                           ALU.mult, ALU.add), s5_y if m else None)
                need(dve, s5_sig, layer, 1)
                do(tt_op(g5, g5, g5s, ALU.mult))
                do(tt_op(q5, g5, g5, ALU.mult), s5_sq)
                t = has(dve, layer, "o5", 0, 256)
                do(ts(y5[:, 0, :], t, 1.0 / GW, EPS, ALU.mult, ALU.add), s5_ss)
                need(dve, s5_rs, layer, 1)
                for m in range(2):
                    do(stt(mixT[:, 6 + m, :], g5[:, m, :], pp(layer, "s5_out", m, 1), y5[:, 0, :],
                           ALU.mult, ALU.mult), mix_done if m else None)

            def residual(q):
                return x[:, q // 2, (q % 2) * 512:(q % 2) * 512 + 512]

            def ffn(e, nb):
                for c in range(NC_):
                    dve.wait_ge(sil_ready.sem, NC_ * e + c + 1)
                    for b in range(nb):
                        ins = tt_op(av[:, b, :], sil[:, b, :], ps[:, b, FC:2 * FC], ALU.mult)
                    ins.then_inc(av_ready.sem, 1)
                    yield c

            constants()
            dve.wait_ge(par_sem, 16)
            pole_constants()
            do(dve.memset(ovf[:], 0), consts_dve)
            for layer in range(DEPTH):
                norm(layer, 1)
                do(dve.memset(rk[:, :, 0:1], 0.0))
                do(dve.memset(xbc[:, :, 0:CONV - 1], 0.0))
                rwkv_mix(layer)
                for m in range(2):
                    do(ts(kk[:, m, :], pf[:, 2 + m, :], pp(layer, "k_k", m, 1), None, ALU.mult))
                do(tt_op(kk2, kk, kk, ALU.mult), rk_sq)
                conv(layer)
                rwkv_decay(layer)
                rwkv_keys(layer)
                dt_first(layer)
                need(dve, ssd_sg, layer, 1)
                do(tt_op(cv, cv, sg, ALU.mult), ssd_xbc)
                do(tt_op(zv[:, :, 0:GW], zv[:, :, 0:GW], xd, ALU.mult))
                dt_rest(layer)
                need(dve, rk_exp, layer, 1)
                rwkv_hats(layer)
                ssd(layer)
                to_mix(layer, "syt", 0, "ssd_norm")
                need(dve, fm_out, layer, 9)
                do(tt_op(sq, qk, qk, ALU.mult), att_sq)
                for key, i in (("qs", 0), ("ks", 2)):
                    t = has(dve, layer, key)
                    do(ts(sq[:, i:i + 2, :], v3(t, 2), 1.0 / HD, EPS, ALU.mult, ALU.add), att_ss)
                need(dve, att_rs, layer, 1)
                do(stt(qk[:, 0:2, :], qk[:, 0:2, :], pp(layer, "q_gain"), sq[:, 0:2, :], ALU.mult, ALU.mult))
                do(stt(qk[:, 2:4, :], qk[:, 2:4, :], pp(layer, "k_gain"), sq[:, 2:4, :], ALU.mult, ALU.mult), att_qk)
                for c in range(TT):
                    rwkv_matrices(layer, c)
                    rwkv_levels(layer, c)
                    if c == 0:
                        t = has(dve, layer, "S", 0, 256)
                        for m in range(2):
                            do(stt(s0[:, m, :], t[:, m * P:(m + 1) * P], dec[:, m:m + 1], blk[:], ALU.mult, ALU.mult),
                               rk_s if m else None)
                    group_norm(layer, c)
                rwkv_out(layer)
                attention(layer)
                s5(layer)
                for q in range(4):
                    t = has(dve, layer, ("wo", q))
                    do(tt_op(residual(q), residual(q), t, ALU.add), x_mixed)
                norm(layer, 2)
                if layer == 0:
                    for c in ffn(0, 2):
                        pass
                    dve.wait_ge(y_done.sem, 2)
                    for q in range(4):
                        do(tt_op(residual(q), residual(q), ps[:, 4 + q, :], ALU.add), x_ffn)

            dve.wait_ge(router_s.sem, 1)
            lg3 = rlg.rearrange("p (a e) -> p a e", a=2)
            do(tt_op(lg3, v3(ps[:, 0, 0:16], 2), bc(pp(1, "router_b"), [P, 2, NE], 1), ALU.add))
            for a in range(2):
                le = bc(lg3[:, a, :], [P, NE, NE], 2)
                lj = bc(lg3[:, a, :], [P, NE, NE], 1)
                g4, q4 = (rt[:, o + 64 * a:o + 64 * a + 64].rearrange("p (e j) -> p e j", e=NE) for o in (256, 384))
                do(tt_op(q4, lj, le, ALU.is_equal))
                do(tt_op(q4, q4, tie[:], ALU.mult))
                do(tt_op(g4, lj, le, ALU.is_gt))
                do(tt_op(g4, g4, q4, ALU.add))
                do(dve.tensor_reduce(rrk[:, 8 * a:8 * a + 8], g4, AX.X, ALU.add))
                do(dve.tensor_reduce(rmx[:, a:a + 1], lg3[:, a, :], AX.X, ALU.max))
            sel = rt[:, 0:16]
            do(ts(sel, rrk, float(2), None, ALU.is_lt))
            do(dve.memset(rtab, 0.0))
            do(tt_op(rl.rearrange("p (a e) -> p a e", a=2), lg3, bc(rmx, [P, 2, NE], 2), ALU.subtract), router_d)
            dve.wait_ge(router_a.sem, 1)
            do(tt_op(rl, rl, sel, ALU.mult))
            do(dve.tensor_reduce(rmx, rl.rearrange("p (a e) -> p a e", a=2), AX.X, ALU.add))
            do(dve.reciprocal(rmx, rmx))
            for a in range(2):
                do(ts(rgate[:, a, 0:NE], rl[:, 8 * a:8 * a + 8], rmx[:, a:a + 1], None, ALU.mult))
                do(dve.tensor_copy(rsel[:, a, 0:NE], sel[:, 8 * a:8 * a + 8]))
            dve.wait_ge(router_s.sem, 2)
            for a in range(2):
                do(dve.tensor_copy(rpos[:, a, 0:NE], ps[:, 1, 8 * a:8 * a + 8]))
            do(dve.tensor_reduce(rmx[:, 0:1], ps[:, 1, 16:24], AX.X, ALU.max))
            do(ts(ovf[:], rmx[:, 0:1], float(P), None, ALU.is_gt), router_d)

            def choose(col, f):
                for a in range(2):
                    ts(G[:, a, :], iota[:], rpos[:, a, bass.ds(col, 1)], rsel[:, a, bass.ds(col, 1)],
                       ALU.is_equal, ALU.mult)
                    ins = ts(Gg[:, a, :], iota[:], rpos[:, a, bass.ds(col, 1)], rgate[:, a, bass.ds(col, 1)],
                             ALU.is_equal, ALU.mult)
                ins.then_inc(f.sem, 1)

            def add_pieces(ve):
                for q in range(4):
                    dve.wait_ge(sc_full.sem, 4 * ve + q + 1)
                    tt_op(residual(q), residual(q), ps[:, 1 + 2 * (q % 2), :], ALU.add).then_inc(x_added.sem, 1)

            def experts(first, ps_no):
                dve.memset(GT, 0.0).then_inc(gt_ready.sem, 1)
                for hf in range(2):
                    dve.memset(ys[:, hf * 512:(hf + 1) * 512], 0.0).then_inc(ys_ready.sem, 1)
                choose(0, g_ready)
                with dve.Fori(first, first + NE) as e:
                    ve = e - 1 + ps_no
                    for r in range(2):
                        dve.wait_ge(gat_full.sem, 2 * (e - 1) + r + 1)
                        tt_op(xgT[:, 4 * r:4 * r + 4, :], v3(ps[:, 6 + r, :], 4),
                              bc(pp(1, "ln_ffn", 4 * r, 4), [P, 4, P], 2), ALU.mult).then_inc(xg_ready.sem, 1)
                    add_pieces(ve)
                    dve.wait_ge(gt_full.sem, e)
                    dve.tensor_copy(GT, v3(ps[:, 2, 0:2 * P], 2)).then_inc(gt_ready.sem, 1)
                    for c in ffn(e, 1):
                        if c == 5:
                            choose(e - first + 1, g_ready)
                add_pieces(first + NE - 1 + ps_no)

            experts(1, 0)
            over = dve.value_load(ovf[0:1, 0:1])
            with dve.If(over > 0):
                do(ts(rpos, rpos, -float(P), None, ALU.add))
                experts(1 + NE, 1)



def kernel(**inputs):
    from concourse import bacc as _bacc
    from concourse.bass_utils import run_bass_kernel_spmd as _run

    a = {k: np.asarray(v) for k, v in inputs.items()}
    L = DEPTH

    def cols(v):
        return v.reshape(L, -1, P).transpose(0, 2, 1)

    def row(v):
        return np.broadcast_to(v[:, None, :], (L, P, v.shape[1]))

    def poles(v):
        return v.reshape(L, 8, P).transpose(0, 2, 1)

    moe_b = np.broadcast_to(a["moe_router_b"], (L, NE))
    parts = {
        "ln_mix": cols(a["ln_mix"]), "ln_ffn": cols(a["ln_ffn"]),
        "conv_w": a["ssd_conv_w"].reshape(L, CONV, 4, P).transpose(0, 3, 2, 1).reshape(L, P, 16),
        "conv_b": cols(a["ssd_conv_b"]), "ssd_norm": cols(a["ssd_norm"]), "att_out": cols(a["att_out_norm"]),
        "q_gain": np.concatenate([a["att_q_norm"]] * 2, axis=1)[:, :, None],
        "k_gain": np.concatenate([a["att_k_norm"]] * 2, axis=1)[:, :, None],
        "mu": cols(a["rwkv_mu"]), "w0": cols(a["rwkv_w0"]), "a0": cols(a["rwkv_a0"]), "k_k": cols(a["rwkv_k_k"]),
        "k_a": cols(a["rwkv_k_a"]), "r_k": cols(a["rwkv_r_k"]), "ln_w": cols(a["rwkv_ln_w"]),
        "ln_b": cols(a["rwkv_ln_b"]), "s5_d": cols(a["s5_d"]), "glu_b": cols(a["s5_glu_b"]),
        "s5_out": cols(a["s5_out_norm"]), "a_re": poles(a["s5_a_re"]), "a_im": poles(a["s5_a_im"]),
        "log_dt": poles(np.broadcast_to(a["s5_log_dt"][:, :, None], (L, 16, 64))),
        "dt_bias": row(a["ssd_dt_bias"]), "a_log": row(a["ssd_a_log"]), "ssd_d": row(a["ssd_d"]),
        "router_b": row(moe_b),
    }
    params = np.concatenate([parts[k] for k in PCOLS], axis=2)

    def b_rows(b):
        w = np.zeros((L, 2, 4, 2, 16, 2, 64), b.dtype)
        v = b.reshape(L, 2, 4, 2, 64, 16)
        for g in range(2):
            w[:, :, :, g, :, g, :] = v[:, :, :, g].transpose(0, 1, 2, 4, 3)
        return w.transpose(0, 2, 3, 4, 1, 5, 6).reshape(L, P, 256)

    def c_cols(c):
        return c.reshape(L, 8, 2, 16, 64).transpose(0, 2, 4, 1, 3).reshape(L, P, P)

    def k_rows(w):
        return w.reshape(L, -1, P, w.shape[2]).transpose(0, 2, 1, 3).reshape(L, P, -1)

    small = np.concatenate([
        np.concatenate([a["rwkv_w2"], a["rwkv_a2"]], axis=1), a["rwkv_g2"], k_rows(a["s5_glu_w"]),
        b_rows(a["s5_b_re"]), b_rows(a["s5_b_im"]), c_cols(a["s5_c_re"]), c_cols(a["s5_c_im"]),
        k_rows(np.broadcast_to(a["moe_router_w"], (L, D, NE)))], axis=2)

    w_in = a["w_in"]
    q0 = 772
    r0 = q0 + 768
    s0 = r0 + 1024
    starts = [r0 + P * i for i in range(8)] + [s0, s0 + P] + [P * i for i in range(4)] + [q0 + P * i for i in range(4)]
    mix = np.zeros((L, M_UNITS, P, MUNIT), w_in.dtype)
    tm = np.concatenate([w_in[:, :, 512:768], w_in[:, :, q0 + 512:q0 + 768], w_in[:, :, 768:772]], axis=2)
    fm_at = list(range(14)) + list(range(18, 22))
    for i, c in enumerate(starts):
        mix[:, fm_at[i], :, :D] = k_rows(w_in[:, :, c:c + P])
    for i in range(4):
        mix[:, 14 + i, :, :2 * TMW] = k_rows(tm[:, 2 * P * i:2 * P * (i + 1)])
    mix[:, 22:30, :, :D] = a["w_out"].reshape(L, 8, P, D)

    def gate_up(g, u):
        n = g.shape[0]
        w = np.stack([v.reshape(n, GUQ, GUK, P, NC_, FC) for v in (g, u)], axis=6)
        return np.ascontiguousarray(w.transpose(0, 4, 1, 3, 2, 6, 5)).reshape(n, GU_UNITS, P, GUK, 2 * FC)

    arrays = {
        "x": a["x"].reshape(T, D), "params": params, "small_w": small, "mix_w": mix,
        "gu_dense": gate_up(a["ffn_w_gate"], a["ffn_w_up"])[0], "d_dense": a["ffn_w_down"][0],
        "gu_moe": gate_up(a["moe_w_gate"][0], a["moe_w_up"][0]), "d_moe": a["moe_w_down"][0],
    }
    arrays = {k: np.ascontiguousarray(v) for k, v in arrays.items()}
    nc = _bacc.Bacc("TRN2", target_bir_lowering=False, num_devices=1)
    args = [nc.dram_tensor(f"in_{k}", v.shape, mybir.dt.from_np(v.dtype), kind="ExternalInput").ap()
            for k, v in arrays.items()]
    out = nc.dram_tensor("out_x", (T, D), F32, kind="ExternalOutput").ap()
    trunk(nc, *args, out)
    r = _run(nc, [{f"in_{k}": v for k, v in arrays.items()}], core_ids=[0])
    return r.results[0]["out_x"].reshape(1, T, D)
```

```python
from contextlib import ExitStack

import numpy as np

import concourse.bass as bass
from concourse import mybir

F32 = mybir.dt.float32
I32 = mybir.dt.int32
ALU = mybir.AluOpType
ACT = mybir.ActivationFunctionType
AX = mybir.AxisListType

P = 128
D = 1024
KT = D // P
T = 256
TT = T // P
GW = 256
HD = 64
H = GW // HD
DEPTH = 2
F = 2816
NE = 8
EPS = 1e-6
GN_EPS = 64e-5
DECAY = 0.606531
LOG2E_SLOPES = [2.0 ** (-8.0 / H * (h + 1)) for h in range(H)]
PATTERNS = ((128, 1), (512, 4), (2048, 16))
CONV = 4

FC = 256
NC_ = F // FC
GUK = 2
GUQ = KT // GUK
GU_UNITS = NC_ * GUQ
R_GU = 4
NF = F // P
D_UNITS = NF * 2
R_D = 4
R_M = 5
TMW = 2 * GW + H

PCOLS = {}
_at = 0
for _name, _n in (("ln_mix", 8), ("ln_ffn", 8), ("conv_w", 16), ("conv_b", 4), ("ssd_norm", 2), ("att_out", 2),
                  ("q_gain", 1), ("k_gain", 1), ("mu", 8), ("w0", 2), ("a0", 2), ("k_k", 2), ("k_a", 2),
                  ("r_k", 2), ("ln_w", 2), ("ln_b", 2), ("s5_d", 2), ("glu_b", 2), ("s5_out", 2),
                  ("a_re", 8), ("a_im", 8), ("log_dt", 8), ("dt_bias", 4), ("a_log", 4), ("ssd_d", 4),
                  ("router_b", 8)):
    PCOLS[_name] = (_at, _n)
    _at += _n
NPAR = _at
WCOLS = {}
_at = 0
for _name, _n in (("w2a2", 256), ("g2", 256), ("glu", 512), ("b_re", 256), ("b_im", 256), ("c_re", 128),
                  ("c_im", 128), ("router", 64)):
    WCOLS[_name] = (_at, _n)
    _at += _n
NSW = _at
ARENA = 11796 + 13 * 512 + 256 + 6144
MUNIT = 4 * 258
FM_ORDER = (4, 0, 1, 2, 3, 5, 6, 7, 8)
GROUPS = ("ssd", "att", "rwkv", "s5")
MIX_ORDER = ("s5", "ssd", "att", "rwkv")
WO_ORDER = [2 * GROUPS.index(g) + i for g in MIX_ORDER for i in range(2)]
UNITS = ([("fm", 2 * q + i) for q in FM_ORDER[:7] for i in range(2)] + [("tm", i) for i in range(4)]
         + [("fm", 2 * q + i) for q in FM_ORDER[7:] for i in range(2)] + [("wo", k) for k in WO_ORDER])
M_UNITS = len(UNITS)


class Flag:

    def __init__(self, nc, ctx, name, per):
        self.sem, self.per, self.n = ctx.enter_context(nc.semaphore(name)), per, 0

    def at(self, layer, i):
        return layer * self.per + i


class Chain:

    def __init__(self, eng, sem):
        self.eng, self.sem, self.n = eng, sem, 0

    def __call__(self, ins, flag=None):
        if flag is None:
            self.n += 1
            ins.then_inc(self.sem, 1)
            self.eng.wait_ge(self.sem, self.n)
        else:
            flag.n += 1
            ins.then_inc(flag.sem, 1)
            self.eng.wait_ge(flag.sem, flag.n)


def trunk(nc, x_in, params, small_w, mix_w, gu_dense, d_dense, gu_moe, d_moe, out):
    ctx = ExitStack()
    with ctx:
        def sb(name, shape, dt=F32):
            return ctx.enter_context(nc.sbuf_tensor(name, shape, dt))

        def flag(name, per=1):
            return Flag(nc, ctx, name, per)

        x = sb("x", [P, TT, D])
        par = sb("par", [P, DEPTH, NPAR])
        sw = sb("sw", [P, NSW])
        mring = sb("mring", [P, R_M, MUNIT])
        guring = sb("guring", [P, R_GU, GUK, 2 * FC])
        dring = sb("dring", [P, R_D, 512])
        ident = sb("ident", [P, P])
        ones = sb("ones", [P, P])
        blk = sb("blk", [P, P])
        m_gt = sb("m_gt", [P, P])
        m_lt = sb("m_lt", [P, P])
        m_leo = sb("m_leo", [P, T])
        m_le = m_leo[:, 0:P]
        lvl = sb("lvl", [P, 7, P])
        bias0 = sb("bias0", [P, H, P])
        bias1 = sb("bias1", [P, H, T])
        cnt0 = sb("cnt0", [P, P])
        cnt1 = sb("cnt1", [P, T])
        iota = sb("iota", [P, P])
        tie = sb("tie", [P, NE, NE])
        s5p = sb("s5p", [P, DEPTH, 6, 8])
        s5t = sb("s5t", [P, 10, DEPTH * 8])
        e_re = sb("e_re", [P, 8, T])
        e_im = sb("e_im", [P, 8, T])
        st = sb("st", [P, 128])
        xh = sb("xh", [P, TT, D])
        arena = sb("arena", [P, ARENA])
        at = [0]

        def flat(a):
            return a.rearrange("p m t -> p (m t)")

        def v3(a, m):
            return a.rearrange("p (m t) -> p m t", m=m)

        def take(n, reset=None):
            if reset is not None:
                at[0] = reset
            a = arena[:, at[0]:at[0] + n]
            at[0] += n
            assert at[0] <= ARENA, at[0]
            return a

        hT = v3(take(2048), KT)
        mixT = v3(take(2048), 8)
        zv = v3(take(1024), TT)
        rk_raw = take(8 * 257)
        rk = v3(rk_raw, 8)
        pf = v3(take(2048), 8)
        u5 = v3(take(512), 2)
        xbc = v3(take(4 * 259), 4)
        qk = v3(take(1024), 4)
        sA, cs, cp, eE, eX, eM, kk, kp, rw_g, rw_b, kk2, rsq = (v3(take(512), 2) for _ in range(12))
        gy = v3(take(512), TT)
        s0 = v3(take(256), 2)
        nm, m2, mb, mk = (v3(rk_raw[:, i * 512:(i + 1) * 512], H) for i in range(4))
        tm_, tt_, xs_ = (v3(flat(a), H) for a in (kk, cs, eM))
        zs, us = flat(kk2)[:, 0:256], flat(kk2)[:, 256:512]
        gsq = flat(rsq)[:, 0:256]
        xflat = xh[:, :, :].rearrange("p a d -> p (a d)")
        vt = v3(xflat[:, 0:512], TT)
        bkt = v3(xflat[:, 512:1024], 4)
        noff = xflat[:, 1024:2048].rearrange("p (b h t) -> p b h t", b=2, h=H)
        scratch = at[0]
        cv = v3(take(1024), 4)
        sg = v3(take(1024), 4)
        r0 = sg
        xs = v3(take(512), TT)
        xd = v3(take(512), TT)
        L0 = v3(take(1024), H)
        L1 = v3(take(512), H)
        sc0 = v3(take(512), 2)
        sc1 = v3(take(256), 2)
        r1 = v3(take(512), H)
        sq = v3(take(1024, scratch), 4)
        a1 = v3(take(1024), H)
        take(512)
        pt0 = v3(take(512), H)
        a0 = v3(take(512), H)
        pt1, pt2 = (v3(take(512), H) for _ in range(2))
        ya = v3(take(512), TT)
        z5 = take(4096, scratch).rearrange("p (j c t) -> p j c t", j=8, c=2)
        p5raw = take(2048)
        p5 = p5raw.rearrange("p (b s c t) -> p b s c t", b=2, s=2, c=2)
        y5, g5, q5, g5s = (v3(p5raw[:, i * 512:(i + 1) * 512], 2) for i in range(4))
        cpad_re = mixT[:, 0:4, :].rearrange("p m (a t) -> p (m a) t", a=2)
        cpad_im = mixT[:, 4:8, :].rearrange("p m (a t) -> p (m a) t", a=2)
        sil = v3(take(512, 2048), 2)
        av = v3(take(512), 2)
        avT = take(512).rearrange("p (b f s) -> p b f s", b=2, f=2)
        xgT = v3(take(1024), KT)
        ys = take(1024)
        G = v3(take(256), TT)
        Gg = v3(take(256), TT)
        GT = v3(take(256), TT)
        rt = take(1024)
        tab_tmp = sb("tab_tmp", [P, 512])
        c5 = sb("c5", [P, 3, P])
        sel_, rl, rlg, rrk, rmx = rt[:, 0:16], rt[:, 16:32], rt[:, 32:48], rt[:, 48:64], rt[:, 64:66]
        rtab = rt[:, 66:120]
        rgate, rsel, rpos = (v3(rtab[:, 18 * i:18 * i + 18], 2) for i in range(3))
        st_at = [0]

        def small_tile(n):
            st_at[0] += n
            return st[:, st_at[0] - n:st_at[0]]

        ssx, rsx, ssy, ssa, dec = (small_tile(2) for _ in range(5))
        ncm, ael = small_tile(4), small_tile(4)
        dtr, dta, dte, dtl, dtu, sa, gst, amx = (small_tile(8) for _ in range(8))
        dtr3 = v3(dtr, 2)
        pw = sb("pw", [P, 3, 8])
        S_AT = ("dt", "da", "r", "k", "r2", "mag", "sin", "cos")

        def S(name):
            return s5t[:, S_AT.index(name), :].rearrange("p (l j) -> p l j", l=DEPTH)

        def par3(name):
            a_, n_ = PCOLS[name]
            return par[:, :, a_:a_ + n_]

        ovf = sb("ovf", [P, 1], I32)
        it_x = sb("it_x", [P, P], I32)
        it_y = sb("it_y", [P, P], I32)
        it_d = sb("it_d", [P, 384], I32)

        ps = ctx.enter_context(nc.psum_tensor("ps", [P, 8, 512], F32))

        ch_act, ch_dve, ch_pool = (ctx.enter_context(nc.semaphore(n)) for n in ("act_chain", "dve_chain", "pool_chain"))
        x_in_sem = ctx.enter_context(nc.semaphore("x_loaded"))
        par_sem = ctx.enter_context(nc.semaphore("params_loaded"))
        sw_sem = ctx.enter_context(nc.semaphore("small_weights_loaded"))
        out_sem = ctx.enter_context(nc.semaphore("out_stored"))
        m_full = [ctx.enter_context(nc.semaphore(f"mix_weight_full{i}")) for i in range(R_M)]
        gu_full_s = [ctx.enter_context(nc.semaphore(f"gate_up_full{i}")) for i in range(R_GU)]
        d_full_s = [ctx.enter_context(nc.semaphore(f"down_full{i}")) for i in range(R_D)]
        bank_full = [ctx.enter_context(nc.semaphore(f"bank_full{i}")) for i in range(8)]

        ident_ready = flag("ident_ready")
        consts_pool = flag("consts_pool")
        consts_dve = flag("consts_dve")
        poles = flag("poles", 1)
        pole_a = flag("pole_a", 3)
        pole_d = flag("pole_d", 2)
        sumsq = flag("sumsq", 2)
        rs_in = flag("rs_in", 2)
        rs_out = flag("rs_out", 2)
        xh_ready = flag("xh_ready", 2)
        h_evac = flag("h_evac", 8)
        fm_out = flag("fm_out", 9)
        zv_out = flag("zv_out", 2)
        dt_out = flag("dt_out", 1)
        rk_mixed = flag("rk_mixed", 1)
        lora_in = flag("lora_in", 1)
        rk_act = flag("rk_act", 3)
        rk_cs = flag("rk_cs", 1)
        rk_exp = flag("rk_exp", 1)
        rk_sq = flag("rk_sq", 1)
        rk_ss = flag("rk_ss", 1)
        rk_rs = flag("rk_rs", 1)
        rk_hat = flag("rk_hat", 1)
        rk_bon = flag("rk_bon", 1)
        rk_bonus = flag("rk_bonus", 1)
        rk_tok = flag("rk_tok", 2)
        rk_mat = flag("rk_mat", 8)
        rk_off = flag("rk_off", 14)
        rk_x = flag("rk_x", 12)
        rk_tt = flag("rk_tt", 14)
        rk_t = flag("rk_t", 12)
        rk_z = flag("rk_z", 2)
        rk_u = flag("rk_u", 2)
        rk_s = flag("rk_s", 1)
        gn_in = flag("gn_in", 2)
        gn_rs = flag("gn_rs", 2)
        gn_y = flag("gn_y", 2)
        rk_yt = flag("rk_yt", 2)
        mix_done = flag("mix_done", 4)
        ssd_cv = flag("ssd_cv", 1)
        ssd_sg = flag("ssd_sg", 1)
        ssd_xbc = flag("ssd_xbc", 1)
        dt_a = flag("dt_a", 1)
        dt_b = flag("dt_b", 1)
        dt_c = flag("dt_c", 1)
        dt_d = flag("dt_d", 1)
        ssd_a = flag("ssd_a", 1)
        ssd_xs = flag("ssd_xs", 1)
        ssd_xd = flag("ssd_xd", 1)
        ssd_r = flag("ssd_r", 1)
        ssd_l = flag("ssd_l", 3)
        ssd_sc = flag("ssd_sc", 2)
        ssd_p = flag("ssd_p", 1)
        ssd_y = flag("ssd_y", 1)
        ssd_ss = flag("ssd_ss", 1)
        ssd_v = flag("ssd_v", 1)
        ssd_rs = flag("ssd_rs", 1)
        ssd_n = flag("ssd_n", 1)
        att_sq = flag("att_sq", 1)
        att_ss = flag("att_ss", 2)
        att_rs = flag("att_rs", 1)
        att_qk = flag("att_qk", 1)
        att_s = flag("att_s", 4)
        att_m = flag("att_m", 2)
        att_e = flag("att_e", 2)
        att_p = flag("att_p", 2)
        att_pt = flag("att_pt", 3)
        att_y = flag("att_y", 1)
        att_v = flag("att_v", 1)
        att_rs2 = flag("att_rs2", 1)
        att_n = flag("att_n", 1)
        tab = flag("tab", 1)
        s5_c = flag("s5_c", 1)
        s5_in = flag("s5_in", 8)
        s5_z = flag("s5_z", 8)
        s5_back = flag("s5_back", 8)
        s5_h = flag("s5_h", 8)
        s5_y = flag("s5_y", 1)
        s5_g = flag("s5_g", 1)
        s5_sig = flag("s5_sig", 1)
        s5_sq = flag("s5_sq", 1)
        s5_ss = flag("s5_ss", 1)
        s5_rs = flag("s5_rs", 1)
        wo_used = flag("wo_used", 7)
        x_mixed = flag("x_mixed", 4)
        gu_used = flag("gu_used", NC_ * (GUQ - 1))
        gu_done = flag("gu_done", NC_)
        gu_done0 = flag("gu_done0", NC_)
        av_ready = flag("av_ready", NC_)
        sil_ready = flag("sil_ready", NC_)
        t_full = flag("t_full", NC_)
        avT_ready = flag("avT_ready", NC_)
        d_used = flag("d_used", D_UNITS - 2)
        y_done = flag("y_done", 2)
        x_ffn = flag("x_ffn", 4)
        g_ready = flag("g_ready", 1)
        gat_full = flag("gat_full", 2)
        xg_ready = flag("xg_ready", 2)
        sc_full = flag("sc_full", 4)
        x_added = flag("x_added", 4)
        gt_full = flag("gt_full", 1)
        gt_ready = flag("gt_ready", 1)
        ys_ready = flag("ys_ready", 2)
        router_s = flag("router_s", 2)
        router_d = flag("router_d", 2)
        router_a = flag("router_a", 1)

        def need(eng, f, layer, i):
            eng.wait_ge(f.sem, f.at(layer, i))

        def pp(layer, name, i=0, n=None):
            a, m = PCOLS[name]
            return par[:, layer, a + i:a + i + (m if n is None else n)]

        def ww(name):
            a, m = WCOLS[name]
            return sw[:, a:a + m]

        def bc(a, shape, axis):
            return a.unsqueeze(axis).to_broadcast(shape)

        place, prev, uses = {}, {}, [0] * 8
        last_in = [None] * 8
        turn_of_banks = list(range(8))

        def fm_n(q):
            return FM_ORDER.index(q) + 1

        def mix_n(group):
            return MIX_ORDER.index(group) + 1

        def tile_(key, f, i):
            b = turn_of_banks.pop(0)
            turn_of_banks.append(b)
            prev[key] = last_in[b]
            place[key] = (b, uses[b])
            last_in[b] = (f, i)
            uses[b] += 1

        PRODUCT_TILES = ("NM2e", "NM2o", "MBKe", "MBKo")

        ATT_TILES = (("S0e", 0, (0, 2)), ("S0o", 0, (1, 3)), ("S1e", 1, (0, 2)), ("S1o", 1, (1, 3)))

        READER = {"lw": (rk_act, 1), "la": (rk_act, 2), "lg": (rk_act, 3), "kks": (rk_ss, 1), "zv0": (zv_out, 1),
                  "zv1": (zv_out, 2), "dt": (dt_out, 1), "bon": (rk_bonus, 1), "xt": (ssd_xs, 1), "dA": (ssd_l, 1),
                  "dB": (ssd_l, 2), "d1": (ssd_l, 3), "sc0": (ssd_sc, 1), "sc1": (ssd_sc, 2), "sy": (ssd_y, 1),
                  "vt": (rk_tok, 1), "bkt": (rk_tok, 2), "syt": (mix_done, mix_n("ssd")), "qs": (att_ss, 1),
                  "ks": (att_ss, 2), "P0": (att_pt, 1), "P1": (att_pt, 2), "P2": (att_pt, 3), "ya": (att_n, 1),
                  "yat": (mix_done, mix_n("att")), "y5": (s5_y, 1), "glu": (s5_sig, 1), "o5": (s5_ss, 1),
                  "S": (rk_s, 1), "S0e": (att_s, 1), "S0o": (att_s, 2), "S1e": (att_s, 3), "S1o": (att_s, 4)}
        for q in range(4):
            READER["h", q] = (h_evac, q + 1)
            READER["h2", q] = (h_evac, 4 + q + 1)
            READER["wo", q] = (x_mixed, q + 1)
        for q in range(9):
            READER["fm", q] = (fm_out, fm_n(q))
        for j in range(8):
            READER["bu", j] = (s5_in, j + 1)
        for c in range(TT):
            READER["Z", c] = (rk_z, c + 1)
            READER["U", c] = (rk_u, c + 1)
            READER["Y", c] = (gn_y, c + 1)
            READER["yt", c] = (rk_yt, c + 1)
            for q, n in enumerate(PRODUCT_TILES):
                READER[n, c] = (rk_mat, 4 * c + q + 1)
            for l in range(7):
                READER["X", c, l] = (rk_x, 6 * c + l) if l else (rk_tt, 7 * c + 1)
                READER["TT", c, l] = (rk_tt, 7 * c + l + 1)
                READER["T", c, l] = (rk_t, 6 * c + l + 1)

        def T_(c, l):
            return [("TT", c, l)] + ([("T", c, l)] if l < 6 else [])

        TILE_ORDER = (
            [("h", q) for q in range(4)] + [("fm", 4), ("fm", 0), ("fm", 1), ("bu", 0), ("bu", 1), ("fm", 2)]
            + [("bu", 2), ("bu", 3), ("bu", 4), ("fm", 3), ("bu", 5), ("bu", 6), ("bu", 7), "lw", "la", "lg", "kks"]
            + [("fm", 5), ("fm", 6), "bon", "vt", "bkt"] + [(n, 0) for n in PRODUCT_TILES]
            + ["y5", ("X", 0, 0), ("X", 0, 1)] + T_(0, 1) + ["zv0", ("X", 0, 2)] + T_(0, 2) + ["glu", "zv1", ("X", 0, 3)]
            + T_(0, 3) + ["dt", ("X", 0, 4), "o5"] + T_(0, 4) + [("fm", 7), ("X", 0, 5)] + T_(0, 5)
            + [("fm", 8), ("X", 0, 6)] + T_(0, 6) + [("Z", 0), "xt", ("U", 0), "S", ("Y", 0)]
            + [(n, 1) for n in PRODUCT_TILES] + ["dA", "dB", "d1", ("X", 1, 0), "sc0", "sc1", ("X", 1, 1), "qs"]
            + T_(1, 1) + ["ks", ("X", 1, 2), "sy"] + T_(1, 2) + [("X", 1, 3)] + T_(1, 3) + ["S0e", "S0o", ("X", 1, 4), "syt"]
            + T_(1, 4) + ["S1e", "S1o", ("X", 1, 5), "P0"] + T_(1, 5) + [("X", 1, 6)] + T_(1, 6)
            + ["P1", "P2", ("Z", 1), "ya", ("U", 1), ("Y", 1), ("yt", 0), "yat", ("wo", 0), ("wo", 1), ("wo", 2), ("wo", 3)]
            + [("yt", 1)] + [("h2", q) for q in range(4)])
        for key in TILE_ORDER:
            tile_(key, *READER[key])
            if key == ("wo", 3):
                turn_of_banks = [b for b in turn_of_banks if b not in [place["wo", q][0] for q in range(4)]]
        assert len(TILE_ORDER) == len(set(TILE_ORDER))
        taken = []

        def acquire(pe, layer, key):
            assert TILE_ORDER[len(taken) % len(TILE_ORDER)] == key, (TILE_ORDER[len(taken) % len(TILE_ORDER)], key)
            taken.append(key)
            if prev[key]:
                need(pe, prev[key][0], layer, prev[key][1])
            return ps[:, place[key][0], :]

        def filled(ins, key):
            ins.then_inc(bank_full[place[key][0]], 1)

        def has(eng, layer, key, i0=0, n=512):
            b, i = place[key]
            eng.wait_ge(bank_full[b], layer * uses[b] + i + 1)
            return ps[:, b, i0:i0 + n]

        unit_at = {u: i for i, u in enumerate(UNITS)}
        assert len(UNITS) == M_UNITS and M_UNITS % R_M == 0

        def unit_read(u):
            kind, i = u
            if kind == "fm":
                return fm_out, fm_n(i // 2)
            if kind == "tm":
                return dt_out, 1
            return (wo_used, WO_ORDER.index(i) + 1) if i != WO_ORDER[7] else (x_mixed, 4)

        def unit(pe, layer, u):
            i = unit_at[u]
            pe.wait_ge(m_full[i % R_M], 16 * (layer * (M_UNITS // R_M) + i // R_M + 1))
            return mring[:, i % R_M, :]

        def gu_read(e, q):
            if q % GUQ < GUQ - 1:
                return gu_used, e * gu_used.per + (q // GUQ) * (GUQ - 1) + q % GUQ + 1
            return gu_done, e * gu_done.per + q // GUQ + 1

        def d_read(e, q):
            if q < D_UNITS - 2:
                return d_used, e * d_used.per + q + 1
            return y_done, e * y_done.per + q - (D_UNITS - 2) + 1

        block = ctx.enter_context(nc.Block())

        @block.sync
        def _(sp):
            sp.dma_start(x[:], x_in.rearrange("(a p) d -> p a d", p=P)).then_inc(x_in_sem, 16)
            sp.dma_start(par[:], params.rearrange("l p n -> p l n")).then_inc(par_sem, 16)

            def small(layer):
                if layer:
                    need(sp, x_mixed, layer - 1, 4)
                sp.dma_start(sw[:], small_w[layer]).then_inc(sw_sem, 16)

            def mix_unit(layer, i):
                g = layer * M_UNITS + i
                if g >= R_M:
                    f, n = unit_read(UNITS[(i - R_M) % M_UNITS])
                    need(sp, f, (g - R_M) // M_UNITS, n)
                sp.dma_start(mring[:, i % R_M, :], mix_w[layer, i]).then_inc(m_full[i % R_M], 16)

            def gu_unit(e, q, src, first):
                if not first:
                    f, n = gu_read(e, q - R_GU) if q >= R_GU else gu_read(e - 1, GU_UNITS + q - R_GU)
                    sp.wait_ge(f.sem, n)
                sp.dma_start(guring[:, q % R_GU], src).then_inc(gu_full_s[q % R_GU], 16)

            def d_unit(e, q, src, first):
                if not first:
                    f, n = d_read(e, q - R_D) if q >= R_D else d_read(e - 1, D_UNITS + q - R_D)
                    sp.wait_ge(f.sem, n)
                sp.dma_start(dring[:, q % R_D], src).then_inc(d_full_s[q % R_D], 16)

            def ffn_stream(e, gu_src, d_src, q0, d0):
                dq = d0
                for c in range(NC_ + 1):
                    if c < NC_:
                        for q in range(GUQ * c, GUQ * c + GUQ):
                            if q >= q0:
                                gu_unit(e, q, gu_src(q), False)
                    if c >= 1:
                        for q in range(4 * (c - 1), 4 * c):
                            if q >= d0:
                                d_unit(e, q, d_src(q), False)

            def d_rows(w, q):
                return w[(q // 2) * P:(q // 2 + 1) * P, (q % 2) * 512:(q % 2) * 512 + 512]

            for i in range(R_M):
                mix_unit(0, i)
            small(0)
            for i in range(R_M, M_UNITS):
                mix_unit(0, i)
                if i == 12:
                    for q in range(R_GU):
                        gu_unit(0, q, gu_dense[q], True)
                    for q in range(R_D):
                        d_unit(0, q, d_rows(d_dense, q), True)
            small(1)
            ffn_stream(0, lambda q: gu_dense[q], lambda q: d_rows(d_dense, q), R_GU, R_D)
            for i in range(M_UNITS):
                mix_unit(1, i)

            def experts(first):
                with sp.Fori(first, first + NE) as e:
                    gw = gu_moe[bass.ds(e - first, 1)].rearrange("a q p k n -> (a q) p k n")
                    dw = d_moe[bass.ds(e - first, 1)].rearrange("a f d -> (a f) d")
                    ffn_stream(e, lambda q: gw[q], lambda q: d_rows(dw, q), 0, 0)

            experts(1)
            sp.wait_ge(router_d.sem, 2)
            over = sp.value_load(ovf[0:1, 0:1])
            with sp.If(over > 0):
                experts(1 + NE)
                sp.wait_ge(x_added.sem, 8 * NE + 8)
            sp.wait_ge(x_added.sem, 4 * NE + 4)
            sp.dma_start(out.rearrange("(a p) d -> p a d", p=P), x[:]).then_inc(out_sem, 16)
            sp.wait_ge(out_sem, 16)

        @block.tensor
        def _(pe):
            mm = pe.matmul

            def transposes(layer, key, srcs):
                t = acquire(pe, layer, key)
                for i, s in enumerate(srcs):
                    ins = pe.transpose(t[:, i * P:(i + 1) * P], s, ident[:])
                filled(ins, key)

            def norm_transpose(layer, name, n):
                need(pe, xh_ready, layer, n)
                for q in range(4):
                    transposes(layer, (name, q), [xh[:, q // 2, (4 * (q % 2) + i) * P:(4 * (q % 2) + i + 1) * P]
                                                  for i in range(4)])

            def fm(layer, q):
                t = acquire(pe, layer, ("fm", q))
                if q == FM_ORDER[0]:
                    need(pe, h_evac, layer, 4)
                for i in range(2):
                    w = unit(pe, layer, ("fm", 2 * q + i))
                    for k in range(KT):
                        ins = mm(t[:, i * T:(i + 1) * T], w[:, k * P:(k + 1) * P], hT[:, k, :],
                                 start=(k == 0), stop=(k == KT - 1))
                filled(ins, ("fm", q))

            def tm(layer, tt):
                t = acquire(pe, layer, f"zv{tt}")
                for k in range(KT):
                    w = unit(pe, layer, ("tm", k // 2))[:, (k % 2) * TMW:(k % 2) * TMW + 2 * GW]
                    ins = mm(t, hT[:, k, tt * P:(tt + 1) * P], w, start=(k == 0), stop=(k == KT - 1))
                filled(ins, f"zv{tt}")

            def tm_dt(layer):
                t = acquire(pe, layer, "dt")
                for tt in range(TT):
                    for k in range(KT):
                        w = unit(pe, layer, ("tm", k // 2))[:, (k % 2) * TMW + 2 * GW:(k % 2 + 1) * TMW]
                        ins = mm(t[:, tt * H:(tt + 1) * H], hT[:, k, tt * P:(tt + 1) * P], w,
                                 start=(k == 0), stop=(k == KT - 1))
                filled(ins, "dt")

            def lora(layer):
                need(pe, lora_in, layer, 1)
                pe.wait_ge(sw_sem, 16 * (layer + 1))
                for key, rows, src in (("lw", slice(0, 64), 6), ("la", slice(64, 128), 6), ("lg", slice(0, 128), 7)):
                    w = ww("g2") if key == "lg" else ww("w2a2")
                    t = acquire(pe, layer, key)
                    for m in range(2):
                        ins = mm(t[:, m * T:(m + 1) * T], w[rows, m * P:(m + 1) * P], pf[rows, src, :],
                                 start=True, stop=True)
                    filled(ins, key)

            def block_sum(layer, key, f, n, src):
                need(pe, f, layer, n)
                t = acquire(pe, layer, key)
                filled(mm(t, blk[:], src, start=True, stop=True), key)

            def head(h):
                return slice(HD * (h % 2), HD * (h % 2) + HD), h // 2

            def ssd_xt(layer):
                need(pe, ssd_xbc, layer, 1)
                transposes(layer, "xt", [cv[:, m, tt * P:(tt + 1) * P] for tt in range(TT) for m in range(2)])

            def ssd_decays(layer):
                need(pe, ssd_r, layer, 1)
                for key, h in (("dA", 0), ("dB", 2)):
                    t = acquire(pe, layer, key)
                    mm(t, m_gt[:], r0[:, h:h + 2, :], start=True, stop=False)
                    ins = mm(v3(t, 2)[:, :, P:T], ones[:], r1[:, h:h + 2, :], start=False, stop=True)
                    filled(ins, key)
                t = acquire(pe, layer, "d1")
                filled(mm(t, m_gt[:], r1, start=True, stop=True), "d1")

            def ssd_scores(layer):
                for g in range(2):
                    t = acquire(pe, layer, f"sc{g}")
                    rows = slice(64 * g, 64 * g + 64)
                    mm(t[:, 0:T], cv[rows, 2, 0:P], cv[rows, 3, :], start=True, stop=True)
                    filled(mm(t[:, T:T + P], cv[rows, 2, P:T], cv[rows, 3, P:T], start=True, stop=True), f"sc{g}")

            def ssd_output(layer):
                t = acquire(pe, layer, "sy")
                need(pe, ssd_p, layer, 1)
                for h in range(H):
                    c = slice(h * HD, (h + 1) * HD)
                    mm(t[:, h * HD:(h + 1) * HD], L0[:, h, 0:P], xd[:, 0, c], start=True, stop=True)
                    o = t[:, T + h * HD:T + (h + 1) * HD]
                    mm(o, L0[:, h, P:T], xd[:, 0, c], start=True, stop=False)
                    ins = mm(o, L1[:, h, :], xd[:, 1, c], start=False, stop=True)
                filled(ins, "sy")

            def att_sums(layer, key, i):
                need(pe, att_sq, layer, 1)
                t = acquire(pe, layer, key)
                filled(mm(t, blk[:], sq[:, i:i + 2, :], start=True, stop=True), key)

            def att_scores(layer, tt):
                need(pe, att_qk, layer, 1)
                for key, _, hs in ATT_TILES[2 * tt:2 * tt + 2]:
                    t = acquire(pe, layer, key)
                    n = P * (tt + 1)
                    for i, h in enumerate(hs):
                        rows, m = head(h)
                        ins = mm(t[:, i * n:(i + 1) * n], qk[rows, m, tt * P:(tt + 1) * P], qk[rows, 2 + m, 0:n],
                                 start=True, stop=True)
                    filled(ins, key)

            def att_turn(layer, key, n, a, j0):
                need(pe, att_p, layer, n)
                transposes(layer, key, [a[:, h, j0:j0 + P] for h in range(H)])

            def att_values(layer):
                t = acquire(pe, layer, "ya")
                need(pe, att_pt, layer, 3)
                for h in range(H):
                    c = slice(GW + h * HD, GW + (h + 1) * HD)
                    mm(t[:, h * HD:(h + 1) * HD], pt0[:, h, :], zv[:, 0, c], start=True, stop=True)
                    o = t[:, T + h * HD:T + (h + 1) * HD]
                    mm(o, pt1[:, h, :], zv[:, 0, c], start=True, stop=False)
                    ins = mm(o, pt2[:, h, :], zv[:, 1, c], start=False, stop=True)
                filled(ins, "ya")

            def token_to_feature(layer, key, f, n, src):
                need(pe, f, layer, n)
                transposes(layer, key, [src[:, tt, m * P:(m + 1) * P] for m in range(2) for tt in range(TT)])

            def rwkv_products(layer, c):
                ch = slice(c * P, (c + 1) * P)
                for q, key in enumerate(PRODUCT_TILES):
                    t = acquire(pe, layer, (key, c))
                    for i, (a, b) in enumerate((((eX, cp), (kp, eX)), ((cp, eE), (kp, eE)))[q // 2]):
                        for m in range(2):
                            rows, _ = head(q % 2)
                            ins = mm(t[:, (2 * i + m) * P:(2 * i + m + 1) * P], a[rows, m, ch], b[rows, m, ch],
                                     start=True, stop=True)
                    filled(ins, (key, c))

            def rwkv_x(layer, c, l):
                t = acquire(pe, layer, ("X", c, l))
                need(pe, rk_off, layer, 7 * c + l + 1)
                if l:
                    need(pe, rk_tt, layer, 7 * c + l)
                for h in range(H):
                    ins = mm(t[:, h * P:(h + 1) * P], noff[:, l % 2, h, :], tt_[:, h, :] if l else ident[:],
                             start=True, stop=True)
                filled(ins, ("X", c, l))

            def rwkv_t(layer, c, l):
                t = acquire(pe, layer, ("TT", c, l))
                need(pe, rk_x, layer, 6 * c + l)
                need(pe, rk_t, layer, 6 * c + l)
                for h in range(H):
                    ins = mm(t[:, h * P:(h + 1) * P], tm_[:, h, :], xs_[:, h, :], start=True, stop=True)
                filled(ins, ("TT", c, l))
                if l < 6:
                    t = acquire(pe, layer, ("T", c, l))
                    for h in range(H):
                        ins = mm(t[:, h * P:(h + 1) * P], xs_[:, h, :], tm_[:, h, :], start=True, stop=True)
                    filled(ins, ("T", c, l))

            def rwkv_z(layer, c):
                ch = slice(c * P, (c + 1) * P)
                t = acquire(pe, layer, ("Z", c))
                need(pe, rk_mat, layer, 4 * c + 2)
                if c:
                    need(pe, rk_s, layer, 1)
                for m in range(2):
                    if c:
                        mm(t[:, m * P:(m + 1) * P], eX[:, m, ch], s0[:, m, :], start=True, stop=False)
                    for h in (2 * m, 2 * m + 1):
                        ins = mm(t[:, h * HD:(h + 1) * HD], m2[:, h, :], vt[:, c, h * HD:(h + 1) * HD],
                                 start=(c == 0), stop=(c == 0 or h % 2 == 1))
                filled(ins, ("Z", c))

            def rwkv_u(layer, c):
                t = acquire(pe, layer, ("U", c))
                need(pe, rk_tt, layer, 7 * c + 7)
                need(pe, rk_z, layer, c + 1)
                for h in range(H):
                    ins = mm(t[:, h * HD:(h + 1) * HD], tt_[:, h, :], zs[:, h * HD:(h + 1) * HD], start=True, stop=True)
                filled(ins, ("U", c))

            def rwkv_state_y(layer, c):
                ch = slice(c * P, (c + 1) * P)
                need(pe, rk_u, layer, c + 1)
                if c == 0:
                    t = acquire(pe, layer, "S")
                    for m in range(2):
                        o = t[:, m * P:(m + 1) * P]
                        mm(o, bkt[:, m, :], us[:, m * P:(m + 1) * P], start=True, stop=False)
                        ins = mm(o, bkt[:, 2 + m, :], vt[:, 0, m * P:(m + 1) * P], start=False, stop=True)
                    filled(ins, "S")
                t = acquire(pe, layer, ("Y", c))
                need(pe, rk_mat, layer, 4 * c + 4)
                for m in range(2):
                    if c:
                        mm(t[:, m * P:(m + 1) * P], eE[:, m, ch], s0[:, m, :], start=True, stop=False)
                    for h in (2 * m, 2 * m + 1):
                        o = t[:, h * HD:(h + 1) * HD]
                        mm(o, mb[:, h, :], us[:, h * HD:(h + 1) * HD], start=(c == 0), stop=False)
                        ins = mm(o, mk[:, h, :], vt[:, c, h * HD:(h + 1) * HD], start=False,
                                 stop=(c == 0 or h % 2 == 1))
                filled(ins, ("Y", c))

            def rwkv_turn_y(layer, c):
                need(pe, gn_y, layer, c + 1)
                t = acquire(pe, layer, ("yt", c))
                for m in range(2):
                    ins = pe.transpose(t[:, m * P:(m + 1) * P], gy[:, c, m * P:(m + 1) * P], ident[:])
                filled(ins, ("yt", c))

            def s5_input(layer, js):
                for j in js:
                    t = acquire(pe, layer, ("bu", j))
                    if j == 0:
                        need(pe, fm_out, layer, fm_n(4))
                        pe.wait_ge(sw_sem, 16 * (layer + 1))
                    rows = slice(32 * (j % 4), 32 * (j % 4) + 32)
                    for i, w in enumerate((ww("b_re"), ww("b_im"))):
                        ins = mm(t[:, i * T:(i + 1) * T], w[rows, (j // 4) * P:(j // 4 + 1) * P], u5[rows, j // 4, :],
                                 start=True, stop=True)
                    filled(ins, ("bu", j))

            def s5_output(layer, t, js):
                for j in js:
                    if j == 0:
                        need(pe, s5_c, layer, 1)
                    need(pe, s5_h, layer, j + 1)
                    o = t[:, (j // 4) * T:(j // 4 + 1) * T]
                    mm(o, cpad_re[:, j, :], z5[:, j, 0, :], start=(j % 4 == 0), stop=False)
                    ins = mm(o, cpad_im[:, j, :], z5[:, j, 1, :], start=False, stop=(j % 4 == 3))
                    if j == 7:
                        filled(ins, "y5")

            def s5_glu(layer):
                t = acquire(pe, layer, "glu")
                need(pe, s5_g, layer, 1)
                w = v3(ww("glu"), 2)
                for m in range(2):
                    for k in range(2):
                        ins = mm(t[:, m * T:(m + 1) * T], w[:, k, m * P:(m + 1) * P], g5[:, k, :],
                                 start=(k == 0), stop=(k == 1))
                filled(ins, "glu")

            def s5_norm(layer):
                t = acquire(pe, layer, "o5")
                need(pe, s5_sq, layer, 1)
                for k in range(2):
                    ins = mm(t[:, 0:T], ones[:], q5[:, k, :], start=(k == 0), stop=(k == 1))
                filled(ins, "o5")

            def out_projection(layer, ts, group):
                need(pe, mix_done, layer, mix_n(group))
                for k in [2 * GROUPS.index(group) + i for i in range(2)]:
                    w = unit(pe, layer, ("wo", k))
                    last = k == WO_ORDER[7]
                    for q in range(4):
                        ins = mm(ts[q], mixT[:, k, (q // 2) * P:(q // 2 + 1) * P], w[:, (q % 2) * 512:(q % 2) * 512 + 512],
                                 start=(k == WO_ORDER[0]), stop=last)
                        if last:
                            filled(ins, ("wo", q))
                    if not last:
                        ins.then_inc(wo_used.sem, 1)

            def gu_slot(e, q):
                pe.wait_ge(gu_full_s[q % R_GU], 16 * (GU_UNITS // R_GU) * e + 16 * (q // R_GU + 1))
                return guring[:, q % R_GU]

            def d_slot(e, q):
                pe.wait_ge(d_full_s[q % R_D], 16 * (D_UNITS // R_D) * e + 16 * (q // R_D + 1))
                return dring[:, q % R_D]

            def ffn(e, src, nb):
                def gate_up(c, qs):
                    for q in qs:
                        u = GUQ * c + q
                        w = gu_slot(e, u)
                        if q == 0 and c:
                            pe.wait_ge(av_ready.sem, av_ready.per * e + c)
                        for b in range(nb):
                            for kk_ in range(GUK):
                                k = q * GUK + kk_
                                ins = mm(ps[:, b, :], src[:, k, b * P:(b + 1) * P], w[:, kk_, :],
                                         start=(k == 0), stop=(k == KT - 1))
                            if q == GUQ - 1:
                                ins.then_inc((gu_done if b == nb - 1 else gu_done0).sem, 1)
                        if q < GUQ - 1:
                            ins.then_inc(gu_used.sem, 1)

                def turn(c):
                    pe.wait_ge(av_ready.sem, av_ready.per * e + c + 1)
                    for b in range(nb):
                        for f in range(2):
                            ins = pe.transpose(ps[:, 2, (2 * b + f) * P:(2 * b + f + 1) * P],
                                               av[:, b, f * P:(f + 1) * P], ident[:])
                    ins.then_inc(t_full.sem, 1)

                def down(c):
                    pe.wait_ge(avT_ready.sem, avT_ready.per * e + c + 1)
                    for f in range(2):
                        for hf in range(2):
                            u = (2 * c + f) * 2 + hf
                            w = d_slot(e, u)
                            for b in range(nb):
                                ins = mm(ps[:, 4 + 2 * b + hf, :], avT[:, b, f, :], w,
                                         start=(c == 0 and f == 0), stop=(c == NC_ - 1 and f == 1))
                            ins.then_inc((d_used if u < D_UNITS - 2 else y_done).sem, 1)

                for c in range(NC_):
                    gate_up(c, range(0, GUQ // 2))
                    if c:
                        turn(c - 1)
                    gate_up(c, range(GUQ // 2, GUQ))
                    if c:
                        down(c - 1)
                turn(NC_ - 1)
                down(NC_ - 1)

            def router():
                need(pe, h_evac, 1, 8)
                w = v3(ww("router"), KT)
                for tt in range(TT):
                    for k in range(KT):
                        ins = mm(ps[:, 0, tt * NE:(tt + 1) * NE], hT[:, k, tt * P:(tt + 1) * P], w[:, k, :],
                                 start=(k == 0), stop=(k == KT - 1))
                ins.then_inc(router_s.sem, 1)
                pe.wait_ge(router_d.sem, 1)
                sel = rt[:, 0:16]
                mm(ps[:, 1, 0:8], m_lt[:], sel[:, 0:8], start=True, stop=True)
                mm(ps[:, 1, 8:16], ones[:], sel[:, 0:8], start=True, stop=False)
                mm(ps[:, 1, 8:16], m_lt[:], sel[:, 8:16], start=False, stop=True)
                mm(ps[:, 1, 16:24], ones[:], sel[:, 0:8], start=True, stop=False)
                mm(ps[:, 1, 16:24], ones[:], sel[:, 8:16], start=False, stop=True).then_inc(router_s.sem, 1)

            def scatter(ve):
                pe.wait_ge(ys_ready.sem, 2 * ve + 2)
                pe.wait_ge(gt_ready.sem, ve + 1)
                for q in range(4):
                    if q >= 2:
                        pe.wait_ge(x_added.sem, 4 * ve + q - 1)
                    mm(ps[:, 1 + 2 * (q % 2), :], GT[:, q // 2, :], ys[:, (q % 2) * 512:(q % 2) * 512 + 512],
                       start=True, stop=True).then_inc(sc_full.sem, 1)

            def experts(first, ps_no):
                with pe.Fori(first, first + NE) as e:
                    ve = e - 1 + ps_no
                    pe.wait_ge(g_ready.sem, ve + 1)
                    for r in range(2):
                        for i in range(4):
                            k = 4 * r + i
                            for tt in range(TT):
                                ins = mm(ps[:, 6 + r, i * P:(i + 1) * P], xh[:, tt, k * P:(k + 1) * P], G[:, tt, :],
                                         start=(tt == 0), stop=(tt == TT - 1))
                        ins.then_inc(gat_full.sem, 1)
                    scatter(ve)
                    for tt in range(TT):
                        ins = pe.transpose(ps[:, 2, tt * P:(tt + 1) * P], Gg[:, tt, :], ident[:])
                    ins.then_inc(gt_full.sem, 1)
                    pe.wait_ge(xg_ready.sem, 2 * (e - 1) + 2)
                    pe.wait_ge(gt_ready.sem, ve + 2)
                    ffn(e, xgT, 1)
                scatter(first + NE - 1 + ps_no)

            pe.wait_ge(ident_ready.sem, 1)
            for layer in range(DEPTH):
                norm_transpose(layer, "h", 1)
                fm(layer, 4)
                fm(layer, 0)
                fm(layer, 1)
                s5_input(layer, (0, 1))
                fm(layer, 2)
                s5_input(layer, (2, 3, 4))
                fm(layer, 3)
                s5_input(layer, (5, 6, 7))
                lora(layer)
                pe.wait_ge(consts_pool.sem, 1)
                block_sum(layer, "kks", rk_sq, 1, kk2)
                fm(layer, 5)
                fm(layer, 6)
                block_sum(layer, "bon", rk_bon, 1, kk2)
                need(pe, rk_hat, layer, 1)
                transposes(layer, "vt", [pf[:, 4 + m, c * P:(c + 1) * P] for c in range(TT) for m in range(2)])
                transposes(layer, "bkt", [a[:, m, 0:P] for a in (cp, kp) for m in range(2)])
                rwkv_products(layer, 0)
                y5_tile = acquire(pe, layer, "y5")
                s5_output(layer, y5_tile, range(0, 4))
                rwkv_x(layer, 0, 0)
                s5_output(layer, y5_tile, range(4, 6))
                rwkv_x(layer, 0, 1)
                s5_output(layer, y5_tile, range(6, 8))
                rwkv_t(layer, 0, 1)
                tm(layer, 0)
                rwkv_x(layer, 0, 2)
                rwkv_t(layer, 0, 2)
                s5_glu(layer)
                tm(layer, 1)
                rwkv_x(layer, 0, 3)
                rwkv_t(layer, 0, 3)
                tm_dt(layer)
                rwkv_x(layer, 0, 4)
                s5_norm(layer)
                rwkv_t(layer, 0, 4)
                fm(layer, 7)
                rwkv_x(layer, 0, 5)
                rwkv_t(layer, 0, 5)
                fm(layer, 8)
                rwkv_x(layer, 0, 6)
                rwkv_t(layer, 0, 6)
                need(pe, rk_tok, layer, 2)
                rwkv_z(layer, 0)
                ssd_xt(layer)
                rwkv_u(layer, 0)
                rwkv_state_y(layer, 0)
                rwkv_products(layer, 1)
                ssd_decays(layer)
                rwkv_x(layer, 1, 0)
                ssd_scores(layer)
                rwkv_x(layer, 1, 1)
                att_sums(layer, "qs", 0)
                rwkv_t(layer, 1, 1)
                att_sums(layer, "ks", 2)
                rwkv_x(layer, 1, 2)
                ssd_output(layer)
                rwkv_t(layer, 1, 2)
                rwkv_x(layer, 1, 3)
                rwkv_t(layer, 1, 3)
                att_scores(layer, 0)
                rwkv_x(layer, 1, 4)
                token_to_feature(layer, "syt", ssd_n, 1, xs)
                rwkv_t(layer, 1, 4)
                att_scores(layer, 1)
                rwkv_x(layer, 1, 5)
                att_turn(layer, "P0", 1, a0, 0)
                rwkv_t(layer, 1, 5)
                rwkv_x(layer, 1, 6)
                rwkv_t(layer, 1, 6)
                att_turn(layer, "P1", 2, a1, 0)
                att_turn(layer, "P2", 2, a1, P)
                rwkv_z(layer, 1)
                att_values(layer)
                rwkv_u(layer, 1)
                rwkv_state_y(layer, 1)
                rwkv_turn_y(layer, 0)
                token_to_feature(layer, "yat", att_n, 1, ya)
                ts = [acquire(pe, layer, ("wo", q)) for q in range(4)]
                out_projection(layer, ts, "s5")
                out_projection(layer, ts, "ssd")
                rwkv_turn_y(layer, 1)
                out_projection(layer, ts, "att")
                out_projection(layer, ts, "rwkv")
                norm_transpose(layer, "h2", 2)
                if layer == 0:
                    need(pe, h_evac, 0, 8)
                    ffn(0, hT, 2)
                else:
                    router()
                    experts(1, 0)
                    pe.wait_ge(router_d.sem, 2)
                    over = pe.value_load(ovf[0:1, 0:1])
                    with pe.If(over > 0):
                        experts(1 + NE, 1)

        @block.scalar
        def _(act):
            do = Chain(act, ch_act)
            A = act.activation

            def rsqrt(src, dst, f=None):
                do(A(dst, src, ACT.Ln))
                do(A(dst, dst, ACT.Exp, scale=-0.5), f)

            def norm(layer, n):
                if layer == 0 and n == 1:
                    act.wait_ge(x_in_sem, 16)
                elif n == 1:
                    need(act, x_ffn, layer - 1, 4)
                else:
                    need(act, x_mixed, layer, 4)
                for tt in range(TT):
                    ins = A(xh[:, tt, :], x[:, tt, :], ACT.Square, accum_out=ssx[:, tt:tt + 1])
                    do(ins, sumsq if tt == 1 else None)
                need(act, rs_in, layer, n)
                rsqrt(ssx, rsx, rs_out)

            def evac_fm(layer, q):
                t = has(act, layer, ("fm", q))
                dst = (rk[:, 2 * q:2 * q + 2, 1:1 + T] if q < 4 else u5 if q == 4 else
                       xbc[:, 2 * (q - 5):2 * (q - 5) + 2, CONV - 1:CONV - 1 + T] if q < 7 else
                       qk[:, 2 * (q - 7):2 * (q - 7) + 2, :])
                do(act.copy(dst, v3(t, 2)), fm_out)

            def bank_copy(layer, key, dst, f, n=512, m=None):
                t = has(act, layer, key, 0, n)
                do(act.copy(dst, v3(t, m) if m else t), f)

            def poles_act():
                do(A(S("dt"), par3("log_dt"), ACT.Exp), pole_a)
                act.wait_ge(pole_d.sem, 1)
                do(A(S("mag"), S("da"), ACT.Exp), pole_a)
                act.wait_ge(pole_d.sem, 2)
                do(A(S("sin"), S("r"), ACT.Sin))
                do(A(S("cos"), S("r2"), ACT.Sin), pole_a)

            def rwkv_x(layer, c, l):
                t = has(act, layer, ("X", c, l))
                do(act.copy(xs_, v3(t, H)), rk_x)

            LN_EXP = "natural_log_exp_and_others"
            act.preload_act_table_set(LN_EXP)
            act.wait_ge(par_sem, 16)
            for layer in range(DEPTH):
                act.preload_act_table_set(LN_EXP)
                norm(layer, 1)
                if layer == 0:
                    poles_act()
                for q in FM_ORDER[:5]:
                    evac_fm(layer, q)
                need(act, rk_mixed, layer, 1)
                do(A(pf[0:64, 6, :], pf[0:64, 6, :], ACT.Tanh))
                do(A(pf[:, 7, :], pf[:, 7, :], ACT.Sigmoid), lora_in)
                for key, dst, b in (("lw", rw_b, "w0"), ("la", sA, "a0")):
                    t = has(act, layer, key)
                    for m in range(2):
                        do(A(dst[:, m, :], t[:, m * T:(m + 1) * T], ACT.Sigmoid, bias=pp(layer, b, m, 1)),
                           rk_act if m else None)
                bank_copy(layer, "lg", rw_g, rk_act, m=2)
                act.preload_act_table_set(LN_EXP)
                need(act, rk_cs, layer, 1)
                for m in range(2):
                    for c in range(TT):
                        ch = slice(c * P, (c + 1) * P)
                        i = 2 * m + c
                        do(A(eE[:, m, ch], cs[:, m, ch], ACT.Exp, bias=ncm[:, i:i + 1]))
                        do(A(eX[:, m, ch], cp[:, m, ch], ACT.Exp, bias=ncm[:, i:i + 1]))
                        do(A(eM[:, m, ch], cs[:, m, ch], ACT.Exp, scale=-1.0, bias=cs[:, m, c * P + 63:c * P + 64]))
                do(A(dec, dec, ACT.Exp), rk_exp)
                need(act, rk_ss, layer, 1)
                rsqrt(rsq, rsq, rk_rs)
                evac_fm(layer, 5)
                evac_fm(layer, 6)
                bank_copy(layer, "vt", vt, rk_tok, m=2)
                bank_copy(layer, "bkt", bkt, rk_tok, m=4)
                rwkv_x(layer, 0, 1)
                need(act, s5_y, layer, 1)
                do(A(g5, y5, ACT.Gelu_apprx_tanh), s5_g)
                bank_copy(layer, "zv0", zv[:, 0, :], zv_out)
                rwkv_x(layer, 0, 2)
                t = has(act, layer, "glu")
                for m in range(2):
                    do(A(g5s[:, m, :], t[:, m * T:(m + 1) * T], ACT.Sigmoid, bias=pp(layer, "glu_b", m, 1)),
                       s5_sig if m else None)
                bank_copy(layer, "zv1", zv[:, 1, :], zv_out)
                rwkv_x(layer, 0, 3)
                need(act, ssd_cv, layer, 1)
                do(A(xd, zv[:, :, 0:GW], ACT.Sigmoid))
                do(A(sg, cv, ACT.Sigmoid), ssd_sg)
                act.preload_act_table_set(LN_EXP)
                rwkv_x(layer, 0, 4)
                need(act, s5_ss, layer, 1)
                rsqrt(y5[:, 0, :], y5[:, 0, :], s5_rs)
                need(act, dt_a, layer, 1)
                do(A(ael, pp(layer, "a_log"), ACT.Exp))
                do(A(dte, dta, ACT.Exp, scale=-1.0), dt_b)
                evac_fm(layer, 7)
                rwkv_x(layer, 0, 5)
                need(act, dt_c, layer, 1)
                do(A(dtl, dtu, ACT.Ln), dt_d)
                evac_fm(layer, 8)
                rwkv_x(layer, 0, 6)
                bank_copy(layer, ("Z", 0), zs, rk_z, 256)
                bank_copy(layer, "xt", xs, ssd_xs, m=2)
                bank_copy(layer, ("U", 0), us, rk_u, 256)
                need(act, gn_in, layer, 1)
                rsqrt(gst[:, 4:8], gst[:, 4:8], gn_rs)
                for key, dst in (("dA", L0[:, 0:2, :]), ("dB", L0[:, 2:4, :]), ("d1", L1)):
                    t = has(act, layer, key)
                    do(A(dst, v3(t, 4 if key == "d1" else 2), ACT.Exp), ssd_l)
                rwkv_x(layer, 1, 1)
                rwkv_x(layer, 1, 2)
                need(act, att_ss, layer, 2)
                rsqrt(sq, sq, att_rs)
                rwkv_x(layer, 1, 3)
                need(act, ssd_y, layer, 1)
                for tt in range(TT):
                    do(A(xd[:, tt, :], xs[:, tt, :], ACT.Square, accum_out=ssy[:, tt:tt + 1]), ssd_ss if tt else None)
                need(act, ssd_v, layer, 1)
                rsqrt(ssy, ssy, ssd_rs)
                rwkv_x(layer, 1, 4)
                need(act, att_m, layer, 1)
                do(A(a0, a0, ACT.Exp), att_e)
                rwkv_x(layer, 1, 5)
                need(act, att_m, layer, 2)
                do(A(a1, a1, ACT.Exp), att_e)
                rwkv_x(layer, 1, 6)
                bank_copy(layer, "P0", pt0, att_pt, m=4)
                bank_copy(layer, "P1", pt1, att_pt, m=4)
                bank_copy(layer, "P2", pt2, att_pt, m=4)
                bank_copy(layer, ("Z", 1), zs, rk_z, 256)
                bank_copy(layer, ("U", 1), us, rk_u, 256)
                t = has(act, layer, "ya")
                for tt in range(TT):
                    do(A(sq[:, tt, :], t[:, tt * T:(tt + 1) * T], ACT.Square, accum_out=ssa[:, tt:tt + 1]),
                       att_y if tt else None)
                need(act, att_v, layer, 1)
                rsqrt(ssa, ssa, att_rs2)
                need(act, gn_in, layer, 2)
                rsqrt(gst[:, 4:8], gst[:, 4:8], gn_rs)
                norm(layer, 2)

                def ffn(e, nb):
                    for c in range(NC_ + 1):
                        if c:
                            act.wait_ge(t_full.sem, NC_ * e + c)
                            act.copy(avT[:, 0:nb], ps[:, 2, 0:nb * 256].rearrange("p (b f s) -> p b f s", b=nb, f=2)) \
                                .then_inc(avT_ready.sem, 1)
                        if c < NC_:
                            for b in range(nb):
                                act.wait_ge((gu_done if b == nb - 1 else gu_done0).sem, NC_ * e + c + 1)
                                ins = A(sil[:, b, :], ps[:, b, 0:FC], ACT.Silu)
                            ins.then_inc(sil_ready.sem, 1)

                if layer == 0:
                    ffn(0, 2)
                    continue
                act.wait_ge(router_d.sem, 1)
                do(A(rl, rl, ACT.Exp), router_a)

                def experts(first, ps_no):
                    with act.Fori(first, first + NE) as e:
                        ffn(e, 1)
                        act.wait_ge(y_done.sem, 2 * e + 2)
                        for hf in range(2):
                            act.copy(ys[:, hf * 512:(hf + 1) * 512], ps[:, 4 + hf, :]).then_inc(ys_ready.sem, 1)

                act.wait_ge(router_d.sem, 2)
                experts(1, 0)
                act.wait_ge(router_d.sem, 2)
                over = act.value_load(ovf[0:1, 0:1])
                with act.If(over > 0):
                    experts(1 + NE, 1)

        @block.gpsimd
        def _(pool):
            do = Chain(pool, ch_pool)

            def fill_mask(dst, base, mult, pattern, op):
                do(pool.memset(dst, 1.0))
                do(pool.affine_select(out=dst, in_=dst, compare_op=op, fill=0.0, base=base,
                                      pattern=pattern, channel_multiplier=mult))

            do(pool.memset(ident[:], 0.0))
            do(pool.affine_select(out=ident[:], in_=ident[:], compare_op=ALU.not_equal, fill=1.0, base=0,
                                  pattern=[[-1, P]], channel_multiplier=1), ident_ready)
            do(pool.memset(ones[:], 1.0))
            do(pool.memset(blk[:], 0.0))
            do(pool.memset(blk[0:64, 0:64], 1.0))
            do(pool.memset(blk[64:128, 64:128], 1.0))
            fill_mask(m_gt[:], 0, 1, [[-1, P]], ALU.is_gt)
            fill_mask(m_lt[:], 0, -1, [[1, P]], ALU.is_gt)
            fill_mask(m_leo[:], 0, -1, [[1, T]], ALU.is_ge)
            do(pool.memset(tie[:], 1.0))
            do(pool.affine_select(out=tie[:], in_=tie[:], compare_op=ALU.is_gt, fill=0.0, base=0,
                                  pattern=[[1, NE], [-1, NE]], channel_multiplier=0))
            do(pool.iota(iota[:], pattern=[[1, P]], base=0, channel_multiplier=0, allow_small_or_imprecise_dtypes=True))
            do(pool.iota(it_x[:], pattern=[[1, P]], base=0, channel_multiplier=0))
            do(pool.iota(it_y[:], pattern=[[0, P]], base=0, channel_multiplier=1))
            do(pool.iota(it_d[:, 0:P], pattern=[[-1, P]], base=0, channel_multiplier=1))
            do(pool.iota(it_d[:, P:384], pattern=[[-1, T]], base=P, channel_multiplier=1), consts_pool)

            def tables(layer):
                pool.wait_ge(poles.sem, 1)
                if layer:
                    need(pool, s5_back, layer - 1, 8)
                do(pool.memset(e_re[:, :, 0:1], 1.0))
                do(pool.memset(e_im[:, :, 0:1], 0.0))
                do(pool.tensor_copy(pw[:, 0, :], s5p[:, layer, 0, :]))
                do(pool.tensor_copy(pw[:, 1, :], s5p[:, layer, 1, :]))
                k = 1
                while k < T:
                    nh = 2 if k == P else 1
                    for hh in range(nh):
                        js = slice(hh * (8 // nh), (hh + 1) * (8 // nh))
                        n = 8 // nh
                        tmp = tab_tmp[:, 0:n * k].rearrange("p (j t) -> p j t", j=n)
                        c_ = bc(pw[:, 0, js], [P, n, k], 2)
                        s_ = bc(pw[:, 1, js], [P, n, k], 2)
                        re, im = e_re[:, js, 0:k], e_im[:, js, 0:k]
                        do(pool.tensor_tensor(e_re[:, js, k:2 * k], re, c_, ALU.mult))
                        do(pool.tensor_tensor(tmp, im, s_, ALU.mult))
                        do(pool.tensor_tensor(e_re[:, js, k:2 * k], e_re[:, js, k:2 * k], tmp, ALU.subtract))
                        do(pool.tensor_tensor(e_im[:, js, k:2 * k], re, s_, ALU.mult))
                        do(pool.tensor_tensor(tmp, im, c_, ALU.mult))
                        do(pool.tensor_tensor(e_im[:, js, k:2 * k], e_im[:, js, k:2 * k], tmp, ALU.add))
                    k *= 2
                    if k < T:
                        do(pool.tensor_tensor(pw[:, 2, :], pw[:, 1, :], pw[:, 1, :], ALU.mult))
                        do(pool.tensor_tensor(pw[:, 1, :], pw[:, 0, :], pw[:, 1, :], ALU.mult))
                        do(pool.tensor_tensor(pw[:, 1, :], pw[:, 1, :], pw[:, 1, :], ALU.add))
                        do(pool.tensor_tensor(pw[:, 0, :], pw[:, 0, :], pw[:, 0, :], ALU.mult))
                        do(pool.tensor_tensor(pw[:, 0, :], pw[:, 0, :], pw[:, 2, :], ALU.subtract))
                do(pool.tensor_copy(pw[:, 2, :], pw[:, 0, :]), tab)

            def c_rows(layer):
                pool.wait_ge(sw_sem, 16 * (layer + 1))
                fr = bc(s5p[:, layer, 3, :], [P, 8, 16], 2)
                fi = bc(s5p[:, layer, 4, :], [P, 8, 16], 2)
                cr, ci = (v3(ww(n), 8) for n in ("c_re", "c_im"))
                o_re, o_im, tmp = (v3(c5[:, i, :], 8) for i in range(3))
                do(pool.tensor_tensor(o_re, cr, fr, ALU.mult))
                do(pool.tensor_tensor(tmp, ci, fi, ALU.mult))
                do(pool.tensor_tensor(o_re, o_re, tmp, ALU.subtract))
                do(pool.tensor_tensor(o_im, cr, fi, ALU.mult))
                do(pool.tensor_tensor(tmp, ci, fr, ALU.mult))
                do(pool.tensor_tensor(o_im, o_im, tmp, ALU.add))
                do(pool.tensor_scalar(o_im, o_im, -1.0, None, ALU.mult))
                need(pool, h_evac, layer, 4)
                do(pool.memset(cpad_re, 0.0))
                do(pool.memset(cpad_im, 0.0))
                for src, dst in ((o_re, cpad_re), (o_im, cpad_im)):
                    for j in range(8):
                        for g in range(2):
                            rows = slice(64 * g, 64 * g + 64)
                            c0 = 32 * (j % 4) + 16 * g
                            ins = pool.tensor_copy(dst[rows, j, c0:c0 + 16], src[rows, j, :])
                            last = j == 7 and g == 1
                            if last and dst is cpad_im:
                                do(ins, s5_c)
                            elif last:
                                do(ins)

            def masked_level(layer, c, l):
                if l == 0:
                    need(pool, rk_mat, layer, 4 * c + 2)
                    if c:
                        need(pool, rk_x, layer, 6)
                elif l == 2:
                    need(pool, rk_tt, layer, 7 * c + 1)
                elif l > 2:
                    need(pool, rk_x, layer, 6 * c + l - 2)
                do(pool.tensor_tensor(noff[:, l % 2], nm, bc(lvl[:, l, :], [P, H, P], 1), ALU.mult), rk_off)

            for layer in range(DEPTH):
                tables(layer)
                c_rows(layer)
                for j in range(8):
                    need(pool, s5_in, layer, j + 1)
                    b = j % 2
                    do(pool.tensor_tensor(z5[:, j, 0, :], p5[:, b, 0, 0, :], p5[:, b, 1, 1, :], ALU.add))
                    do(pool.tensor_tensor(z5[:, j, 1, :], p5[:, b, 0, 1, :], p5[:, b, 1, 0, :], ALU.subtract), s5_z)
                for j in range(8):
                    need(pool, s5_back, layer, j + 1)
                    b = j % 2
                    do(pool.tensor_tensor(z5[:, j, 0, :], p5[:, b, 0, 0, :], p5[:, b, 1, 1, :], ALU.subtract))
                    do(pool.tensor_tensor(z5[:, j, 1, :], p5[:, b, 1, 0, :], p5[:, b, 0, 1, :], ALU.add), s5_h)
                pool.wait_ge(consts_dve.sem, 1)
                for l in range(7):
                    masked_level(layer, 0, l)
                need(pool, ssd_a, layer, 1)
                for h0 in (0, 2):
                    do(pool.tensor_tensor(r0[:, h0:h0 + 2, :], bc(m_leo[:], [P, 2, T], 1),
                                          bc(sa[:, h0:h0 + 2], [P, 2, T], 2), ALU.mult))
                do(pool.tensor_tensor(r1, bc(m_le, [P, H, P], 1), bc(sa[:, 4:8], [P, H, P], 2), ALU.mult), ssd_r)
                for l in range(7):
                    masked_level(layer, 1, l)

        @block.vector
        def _(dve):
            do = Chain(dve, ch_dve)
            tt_op, ts, stt = dve.tensor_tensor, dve.tensor_scalar, dve.scalar_tensor_tensor

            def constants():
                dve.wait_ge(consts_pool.sem, 1)
                do(tt_op(it_x[:], it_x[:], it_y[:], ALU.bitwise_xor))
                for l in range(7):
                    do(ts(it_y[:], it_x[:], l, None, ALU.logical_shift_right))
                    do(stt(lvl[:, l, :], it_y[:], 1.0, m_gt[:], ALU.is_equal, ALU.mult))
                for cnt, bias, d in ((cnt0, bias0, it_d[:, 0:P]), (cnt1, bias1, it_d[:, P:384])):
                    n = d.shape[1]
                    c = cnt[:]
                    dist, w = flat(gy)[:, 0:n], flat(s0)[:, 0:n]
                    wi = flat(gy)[:, 256:256 + n].bitcast(I32)
                    do(dve.tensor_copy(dist, d))
                    do(dve.memset(c, 0.0))
                    for window, dil in PATTERNS:
                        do(ts(wi, d, dil - 1, None, ALU.bitwise_and))
                        do(ts(w, wi, 0.0, None, ALU.is_equal))
                        do(stt(w, dist, float(window), w, ALU.is_le, ALU.mult))
                        do(tt_op(c, c, w, ALU.add))
                    do(stt(c, dist, 0.0, c, ALU.is_ge, ALU.mult))
                    do(ts(w, c, 0.0, -1e30, ALU.is_equal, ALU.mult))
                    for h in range(H):
                        do(stt(bias[:, h, :], dist, -LOG2E_SLOPES[h], w, ALU.mult, ALU.add))

            def pole_constants():
                inv, magic = 1.0 / (2 * np.pi), 12582912.0
                c1 = 6.28125
                c2 = float(np.float32(np.float16(2 * np.pi - c1)))
                c3 = float(np.float32(2 * np.pi - c1 - c2))
                dve.wait_ge(pole_a.sem, 1)
                are, aim = par3("a_re"), par3("a_im")
                do(tt_op(S("da"), S("dt"), are, ALU.mult), pole_d)
                do(tt_op(S("r"), S("dt"), aim, ALU.mult))
                do(ts(S("k"), S("r"), inv, magic, ALU.mult, ALU.add))
                do(ts(S("k"), S("k"), -magic, None, ALU.add))
                for c_ in (c1, c2, c3):
                    do(stt(S("r"), S("k"), -c_, S("r"), ALU.mult, ALU.add))
                pi = float(np.nextafter(np.float32(np.pi), np.float32(0)))
                do(ts(S("r"), S("r"), pi, -pi, ALU.min, ALU.max))
                do(ts(S("r2"), S("r"), float(np.pi / 2), None, ALU.add))
                do(ts(S("k"), S("r2"), pi, None, ALU.is_gt))
                do(stt(S("r2"), S("k"), float(-2 * np.pi), S("r2"), ALU.mult, ALU.add))
                do(ts(S("r2"), S("r2"), pi, -pi, ALU.min, ALU.max), pole_d)
                dve.wait_ge(pole_a.sem, 3)
                do(dve.tensor_copy(s5p[:, :, 0, :], S("cos")))
                do(dve.tensor_copy(s5p[:, :, 1, :], S("sin")))
                do(dve.tensor_copy(s5p[:, :, 2, :], S("mag")))
                do(tt_op(S("cos"), S("cos"), S("mag"), ALU.mult))
                do(tt_op(S("sin"), S("sin"), S("mag"), ALU.mult))
                do(ts(S("cos"), S("cos"), -1.0, None, ALU.add))
                do(tt_op(S("k"), are, are, ALU.mult))
                do(tt_op(S("r"), aim, aim, ALU.mult))
                do(tt_op(S("k"), S("k"), S("r"), ALU.add))
                do(dve.reciprocal(S("k"), S("k")))
                do(tt_op(S("r"), S("cos"), are, ALU.mult))
                do(tt_op(S("r2"), S("sin"), aim, ALU.mult))
                do(tt_op(S("r"), S("r"), S("r2"), ALU.add))
                do(tt_op(s5p[:, :, 3, :], S("r"), S("k"), ALU.mult))
                do(tt_op(S("r"), S("sin"), are, ALU.mult))
                do(tt_op(S("r2"), S("cos"), aim, ALU.mult))
                do(tt_op(S("r"), S("r"), S("r2"), ALU.subtract))
                do(tt_op(s5p[:, :, 4, :], S("r"), S("k"), ALU.mult), poles)

            def norm(layer, n):
                need(dve, sumsq, layer, n)
                do(ts(ssx, ssx, 1.0 / D, EPS, ALU.mult, ALU.add), rs_in)
                need(dve, rs_out, layer, n)
                for tt in range(TT):
                    do(ts(xh[:, tt, :], x[:, tt, :], rsx[:, tt:tt + 1], None, ALU.mult), xh_ready if tt else None)
                g = pp(layer, "ln_mix" if n == 1 else "ln_ffn")
                for q in range(4):
                    t = has(dve, layer, ("h" if n == 1 else "h2", q))
                    k = 4 * (q % 2)
                    do(tt_op(hT[:, k:k + 4, (q // 2) * P:(q // 2 + 1) * P], v3(t, 4),
                             bc(g[:, k:k + 4], [P, 4, P], 2), ALU.mult), h_evac)

            def rwkv_mix(layer, q):
                need(dve, fm_out, layer, fm_n(q))
                m = slice(2 * q, 2 * q + 2)
                do(tt_op(pf[:, m, :], rk[:, m, 0:T], rk[:, m, 1:1 + T], ALU.subtract))
                for i in (2 * q, 2 * q + 1):
                    do(stt(pf[:, i, :], pf[:, i, :], pp(layer, "mu", i, 1), rk[:, i, 1:1 + T], ALU.mult, ALU.add),
                       rk_mixed if i == 7 else None)

            def conv(layer, ms):
                need(dve, fm_out, layer, fm_n(6))
                for m in ms:
                    w = [pp(layer, "conv_w", 4 * m + i, 1) for i in range(CONV)]
                    do(ts(cv[:, m, :], xbc[:, m, 0:T], w[0], pp(layer, "conv_b", m, 1), ALU.mult, ALU.add))
                    for i in range(1, CONV):
                        do(stt(cv[:, m, :], xbc[:, m, i:i + T], w[i], cv[:, m, :], ALU.mult, ALU.add),
                           ssd_cv if (m, i) == (3, CONV - 1) else None)

            def rwkv_decay(layer):
                need(dve, rk_act, layer, 1)
                do(ts(rw_b, rw_b, -DECAY, None, ALU.mult))
                for m in range(2):
                    for c in range(TT):
                        ch = slice(c * P, (c + 1) * P)
                        do(dve.tensor_tensor_scan(cs[:, m, ch], ones[:], rw_b[:, m, ch], 0.0, ALU.mult, ALU.add))
                do(tt_op(cp, cs, rw_b, ALU.subtract))
                do(ts(ncm.rearrange("p (m c) -> p m c", m=2), cs[:, :, 63:T:P], -1.0, None, ALU.mult))
                d3 = dec.rearrange("p (m c) -> p m c", c=1)
                do(tt_op(d3, cs[:, :, P - 1:P], cs[:, :, 63:64], ALU.subtract))
                do(tt_op(d3, d3, cs[:, :, P + 63:P + 64], ALU.add), rk_cs)

            def rwkv_keys(layer):
                need(dve, rk_act, layer, 2)
                for m in range(2):
                    do(ts(kp[:, m, :], sA[:, m, :], 1.0, pp(layer, "k_a", m, 1), ALU.subtract, ALU.mult))
                do(stt(kp, kp, 1.0, pf[:, 2:4, :], ALU.add, ALU.mult))
                t = has(dve, layer, "kks")
                do(ts(rsq, v3(t, 2), 1e-12, None, ALU.add), rk_ss)
                for m in range(2):
                    do(stt(kk2[:, m, :], pf[:, m, :], pp(layer, "r_k", m, 1), kp[:, m, :], ALU.mult, ALU.mult),
                       rk_bon if m else None)

            def rwkv_hats(layer):
                need(dve, rk_rs, layer, 1)
                do(tt_op(kk, kk, rsq, ALU.mult))
                do(stt(eX, kk, -1.0, eX, ALU.mult, ALU.mult))
                do(tt_op(cp, kk, sA, ALU.mult))
                do(tt_op(cp, cp, eM, ALU.mult))
                do(tt_op(kp, kp, eM, ALU.mult))
                t = has(dve, layer, "bon")
                do(tt_op(rw_b, v3(t, 2), pf[:, 4:6, :], ALU.mult), rk_bonus)
                do(tt_op(eE, eE, pf[:, 0:2, :], ALU.mult), rk_hat)

            def dt_first(layer):
                t = has(dve, layer, "dt", 0, 2 * H)
                do(tt_op(dtr3, v3(t, 2), bc(pp(layer, "dt_bias"), [P, 2, H], 1), ALU.add), dt_out)
                do(stt(dta, dtr, -1.0, dtr, ALU.mult, ALU.max), dt_a)

            def dt_rest(layer):
                need(dve, dt_b, layer, 1)
                do(ts(dtu, dte, 1.0, None, ALU.add), dt_c)
                do(stt(dta, dtu, -1.0, dte, ALU.add, ALU.subtract))
                do(dve.reciprocal(dte, dtu))
                do(tt_op(dta, dta, dte, ALU.mult))
                need(dve, dt_d, layer, 1)
                do(tt_op(dtl, dtl, dta, ALU.subtract))
                do(stt(dtr, dtr, 0.0, dtl, ALU.max, ALU.add))
                do(stt(sa.rearrange("p (a h) -> p a h", a=2), dtr3, -1.0, bc(ael, [P, 2, H], 1), ALU.mult, ALU.mult),
                   ssd_a)

            def heads(a):
                return a.rearrange("p a (h e) -> p (a h) e", h=H)

            def ssd_x(layer):
                need(dve, ssd_xs, layer, 1)
                do(tt_op(heads(xd), heads(xs), bc(dtr, [P, 2 * H, HD], 2), ALU.mult))

            def ssd_scores(layer):
                for g in range(2):
                    t = has(dve, layer, f"sc{g}")
                    do(tt_op(sc0[:, g, :], t[:, 0:T], m_leo[:], ALU.mult))
                    do(tt_op(sc1[:, g, :], t[:, T:T + P], m_le, ALU.mult), ssd_sc)

            def ssd_weights(layer):
                need(dve, ssd_l, layer, 3)
                for g in range(2):
                    do(tt_op(L0[:, 2 * g:2 * g + 2, :], L0[:, 2 * g:2 * g + 2, :], bc(sc0[:, g, :], [P, 2, T], 1),
                             ALU.mult))
                    do(tt_op(L1[:, 2 * g:2 * g + 2, :], L1[:, 2 * g:2 * g + 2, :], bc(sc1[:, g, :], [P, 2, P], 1),
                             ALU.mult), ssd_p if g else None)

            def ssd_gate(layer):
                for tt in range(TT):
                    a = xs[:, tt, :].rearrange("p (h e) -> p h e", h=H)
                    do(tt_op(a, a, bc(pp(layer, "ssd_d"), [P, H, HD], 2), ALU.mult))
                t = has(dve, layer, "sy")
                do(tt_op(xs, v3(t, 2), xs, ALU.add))
                do(tt_op(xs, xs, zv[:, :, 0:GW], ALU.mult), ssd_y)

            def ssd_norm(layer):
                need(dve, ssd_ss, layer, 1)
                do(ts(ssy, ssy, 1.0 / GW, EPS, ALU.mult, ALU.add), ssd_v)
                need(dve, ssd_rs, layer, 1)
                for tt in range(TT):
                    do(ts(xs[:, tt, :], xs[:, tt, :], ssy[:, tt:tt + 1], None, ALU.mult), ssd_n if tt else None)

            def to_mix(layer, key, m, gain):
                t = has(dve, layer, key)
                do(tt_op(mixT[:, m:m + 2, :], v3(t, 2), bc(pp(layer, gain), [P, 2, T], 2), ALU.mult), mix_done)

            def rwkv_matrices(layer, c):
                if c:
                    need(dve, rk_off, layer, 7)
                for q, key in enumerate(PRODUCT_TILES):
                    t = has(dve, layer, (key, c))
                    for i, (dst, mask) in enumerate((((nm, m_gt[:]), (m2, m_lt[:])), ((mb, m_le), (mk, m_le)))[q // 2]):
                        do(tt_op(dst[:, q % 2::2, :], v3(t[:, i * T:(i + 1) * T], 2), bc(mask, [P, 2, P], 1), ALU.mult),
                           rk_mat if i else None)

            def rwkv_level(layer, c, l):
                idb = bc(ident[:], [P, H, P], 1)
                if l == 0:
                    need(dve, rk_off, layer, 7 * c + 1)
                    do(tt_op(tm_, noff[:, 0], idb, ALU.add), rk_t)
                    t = has(dve, layer, ("X", c, 0))
                    do(tt_op(tt_, v3(t, H), idb, ALU.add), rk_tt)
                    return
                t = has(dve, layer, ("TT", c, l))
                do(tt_op(tt_, v3(t, H), tt_, ALU.add), rk_tt)
                if l < 6:
                    t = has(dve, layer, ("T", c, l))
                    do(tt_op(tm_, v3(t, H), tm_, ALU.add), rk_t)

            def group_norm(layer, c):
                t = has(dve, layer, ("Y", c), 0, GW)
                y3 = t.rearrange("p (h e) -> p h e", h=H)
                g3 = gy[:, c, :].rearrange("p (h e) -> p h e", h=H)
                k3 = gsq.rearrange("p (h e) -> p h e", h=H)
                mean, var = gst[:, 0:4], gst[:, 4:8]
                do(dve.tensor_reduce(mean, y3, AX.X, ALU.add))
                do(ts(mean, mean, 1.0 / HD, None, ALU.mult))
                do(tt_op(g3, y3, bc(mean, [P, H, HD], 2), ALU.subtract))
                do(tt_op(k3, g3, g3, ALU.mult))
                do(dve.tensor_reduce(var, k3, AX.X, ALU.add))
                do(ts(var, var, 1.0 / HD, GN_EPS, ALU.mult, ALU.add), gn_in)
                need(dve, gn_rs, layer, c + 1)
                do(tt_op(g3, g3, bc(var, [P, H, HD], 2), ALU.mult), gn_y)

            def rwkv_out(layer, c):
                t = has(dve, layer, ("yt", c), 0, 256)
                ch = slice(c * P, (c + 1) * P)
                for m in range(2):
                    do(ts(mixT[:, 4 + m, ch], t[:, m * P:(m + 1) * P], pp(layer, "ln_w", m, 1),
                          pp(layer, "ln_b", m, 1), ALU.mult, ALU.add), rk_yt if m else None)
                o = mixT[:, 4:6, ch]
                do(tt_op(o, o, rw_b[:, :, ch], ALU.add))
                do(tt_op(o, o, rw_g[:, :, ch], ALU.mult), mix_done if c else None)

            def att_squares(layer):
                need(dve, fm_out, layer, 9)
                do(tt_op(sq, qk, qk, ALU.mult), att_sq)

            def att_sums(layer):
                for key, i in (("qs", 0), ("ks", 2)):
                    t = has(dve, layer, key)
                    do(ts(sq[:, i:i + 2, :], v3(t, 2), 1.0 / HD, EPS, ALU.mult, ALU.add), att_ss)

            def att_norm(layer):
                need(dve, att_rs, layer, 1)
                do(stt(qk[:, 0:2, :], qk[:, 0:2, :], pp(layer, "q_gain"), sq[:, 0:2, :], ALU.mult, ALU.mult))
                do(stt(qk[:, 2:4, :], qk[:, 2:4, :], pp(layer, "k_gain"), sq[:, 2:4, :], ALU.mult, ALU.mult), att_qk)

            def att_scores(layer, tt):
                a, bias = ((a0, bias0), (a1, bias1))[tt]
                n = P * (tt + 1)
                mx = amx[:, tt * H:(tt + 1) * H]
                for key, _, hs in ATT_TILES[2 * tt:2 * tt + 2]:
                    t = has(dve, layer, key, 0, 2 * n)
                    do(stt(a[:, hs[0]::2, :], v3(t, 2), HD ** -0.5, bias[:, hs[0]::2, :], ALU.mult, ALU.add), att_s)
                do(dve.tensor_reduce(mx, a, AX.X, ALU.max))
                do(tt_op(a, a, bc(mx, [P, H, n], 2), ALU.subtract), att_m)

            def att_softmax(layer, tt):
                a, cnt = ((a0, cnt0), (a1, cnt1))[tt]
                n = P * (tt + 1)
                mx = amx[:, tt * H:(tt + 1) * H]
                need(dve, att_e, layer, tt + 1)
                do(tt_op(a, a, bc(cnt[:], [P, H, n], 1), ALU.mult))
                do(dve.tensor_reduce(mx, a, AX.X, ALU.add))
                do(dve.reciprocal(mx, mx))
                do(tt_op(a, a, bc(mx, [P, H, n], 2), ALU.mult), att_p)

            def att_out(layer):
                need(dve, att_y, layer, 1)
                do(ts(ssa, ssa, 1.0 / GW, EPS, ALU.mult, ALU.add), att_v)
                need(dve, att_rs2, layer, 1)
                t = has(dve, layer, "ya")
                for tt in range(TT):
                    do(ts(ya[:, tt, :], t[:, tt * T:(tt + 1) * T], ssa[:, tt:tt + 1], None, ALU.mult),
                       att_n if tt else None)

            def s5_products(j, src, f):
                b = j % 2
                do(tt_op(p5[:, b, 0], src, bc(e_re[:, j, :], [P, 2, T], 1), ALU.mult))
                do(tt_op(p5[:, b, 1], src, bc(e_im[:, j, :], [P, 2, T], 1), ALU.mult), f)

            def s5_input(layer, js):
                for j in js:
                    if j == 0:
                        dve.wait_ge(tab.sem, layer + 1)
                    t = has(dve, layer, ("bu", j))
                    if j >= 2:
                        need(dve, s5_z, layer, j - 1)
                    s5_products(j, v3(t, 2), s5_in)

            def s5_scan(layer, js):
                for j in js:
                    need(dve, s5_z, layer, j + 1)
                    for i in range(2):
                        z = z5[:, j, i, :]
                        do(dve.tensor_tensor_scan(z, s5p[:, layer, 2, j:j + 1].to_broadcast([P, T]), z, 0.0,
                                                  ALU.mult, ALU.add))

            def s5_rotate_back(layer, js):
                for j in js:
                    if j == 0:
                        need(dve, s5_z, layer, 8)
                    if j >= 2:
                        need(dve, s5_h, layer, j - 1)
                    s5_products(j, z5[:, j], s5_back)

            def s5_skip(layer):
                t = has(dve, layer, "y5")
                for m in range(2):
                    do(stt(y5[:, m, :], u5[:, m, :], pp(layer, "s5_d", m, 1), t[:, m * T:(m + 1) * T],
                           ALU.mult, ALU.add), s5_y if m else None)

            def s5_gate(layer):
                need(dve, s5_sig, layer, 1)
                do(tt_op(g5, g5, g5s, ALU.mult))
                do(tt_op(q5, g5, g5, ALU.mult), s5_sq)

            def s5_sums(layer):
                t = has(dve, layer, "o5", 0, 256)
                do(ts(y5[:, 0, :], t, 1.0 / GW, EPS, ALU.mult, ALU.add), s5_ss)

            def s5_out(layer):
                need(dve, s5_rs, layer, 1)
                for m in range(2):
                    do(stt(mixT[:, 6 + m, :], g5[:, m, :], pp(layer, "s5_out", m, 1), y5[:, 0, :],
                           ALU.mult, ALU.mult), mix_done if m else None)

            def residual(q):
                return x[:, q // 2, (q % 2) * 512:(q % 2) * 512 + 512]

            def ffn(e, nb):
                for c in range(NC_):
                    dve.wait_ge(sil_ready.sem, NC_ * e + c + 1)
                    for b in range(nb):
                        ins = tt_op(av[:, b, :], sil[:, b, :], ps[:, b, FC:2 * FC], ALU.mult)
                    ins.then_inc(av_ready.sem, 1)
                    yield c

            dve.wait_ge(par_sem, 16)
            for layer in range(DEPTH):
                norm(layer, 1)
                if layer == 0:
                    pole_constants()
                    constants()
                    do(dve.memset(ovf[:], 0), consts_dve)
                do(dve.memset(rk[:, :, 0:1], 0.0))
                do(dve.memset(xbc[:, :, 0:CONV - 1], 0.0))
                rwkv_mix(layer, 0)
                rwkv_mix(layer, 1)
                s5_input(layer, (0, 1))
                rwkv_mix(layer, 2)
                s5_input(layer, (2, 3, 4))
                rwkv_mix(layer, 3)
                for m in range(2):
                    do(ts(kk[:, m, :], pf[:, 2 + m, :], pp(layer, "k_k", m, 1), None, ALU.mult))
                do(tt_op(kk2, kk, kk, ALU.mult), rk_sq)
                s5_input(layer, (5, 6, 7))
                rwkv_decay(layer)
                rwkv_keys(layer)
                s5_scan(layer, range(8))
                s5_rotate_back(layer, (0, 1))
                need(dve, rk_exp, layer, 1)
                rwkv_hats(layer)
                s5_rotate_back(layer, range(2, 8))
                rwkv_matrices(layer, 0)
                rwkv_level(layer, 0, 0)
                s5_skip(layer)
                rwkv_level(layer, 0, 1)
                conv(layer, (0, 1))
                rwkv_level(layer, 0, 2)
                conv(layer, (2, 3))
                rwkv_level(layer, 0, 3)
                s5_gate(layer)
                rwkv_level(layer, 0, 4)
                s5_sums(layer)
                dt_first(layer)
                need(dve, ssd_sg, layer, 1)
                do(tt_op(cv, cv, sg, ALU.mult), ssd_xbc)
                s5_out(layer)
                rwkv_level(layer, 0, 5)
                do(tt_op(zv[:, :, 0:GW], zv[:, :, 0:GW], xd, ALU.mult))
                dt_rest(layer)
                rwkv_level(layer, 0, 6)
                t = has(dve, layer, "S", 0, 256)
                for m in range(2):
                    do(stt(s0[:, m, :], t[:, m * P:(m + 1) * P], dec[:, m:m + 1], blk[:], ALU.mult, ALU.mult),
                       rk_s if m else None)
                group_norm(layer, 0)
                rwkv_matrices(layer, 1)
                rwkv_level(layer, 1, 0)
                ssd_x(layer)
                ssd_scores(layer)
                ssd_weights(layer)
                att_squares(layer)
                rwkv_level(layer, 1, 1)
                att_sums(layer)
                rwkv_level(layer, 1, 2)
                ssd_gate(layer)
                att_norm(layer)
                rwkv_level(layer, 1, 3)
                att_scores(layer, 0)
                ssd_norm(layer)
                rwkv_level(layer, 1, 4)
                att_scores(layer, 1)
                att_softmax(layer, 0)
                to_mix(layer, "syt", 0, "ssd_norm")
                rwkv_level(layer, 1, 5)
                att_softmax(layer, 1)
                rwkv_level(layer, 1, 6)
                att_out(layer)
                group_norm(layer, 1)
                rwkv_out(layer, 0)
                to_mix(layer, "yat", 2, "att_out")
                rwkv_out(layer, 1)
                for q in range(4):
                    t = has(dve, layer, ("wo", q))
                    do(tt_op(residual(q), residual(q), t, ALU.add), x_mixed)
                norm(layer, 2)
                if layer == 0:
                    for c in ffn(0, 2):
                        pass
                    dve.wait_ge(y_done.sem, 2)
                    for q in range(4):
                        do(tt_op(residual(q), residual(q), ps[:, 4 + q, :], ALU.add), x_ffn)

            dve.wait_ge(router_s.sem, 1)
            lg3 = rlg.rearrange("p (a e) -> p a e", a=2)
            do(tt_op(lg3, v3(ps[:, 0, 0:16], 2), bc(pp(1, "router_b"), [P, 2, NE], 1), ALU.add))
            for a in range(2):
                le = bc(lg3[:, a, :], [P, NE, NE], 2)
                lj = bc(lg3[:, a, :], [P, NE, NE], 1)
                g4, q4 = (rt[:, o + 64 * a:o + 64 * a + 64].rearrange("p (e j) -> p e j", e=NE) for o in (256, 384))
                do(tt_op(q4, lj, le, ALU.is_equal))
                do(tt_op(q4, q4, tie[:], ALU.mult))
                do(tt_op(g4, lj, le, ALU.is_gt))
                do(tt_op(g4, g4, q4, ALU.add))
                do(dve.tensor_reduce(rrk[:, 8 * a:8 * a + 8], g4, AX.X, ALU.add))
                do(dve.tensor_reduce(rmx[:, a:a + 1], lg3[:, a, :], AX.X, ALU.max))
            sel = rt[:, 0:16]
            do(ts(sel, rrk, float(2), None, ALU.is_lt))
            do(dve.memset(rtab, 0.0))
            do(tt_op(rl.rearrange("p (a e) -> p a e", a=2), lg3, bc(rmx, [P, 2, NE], 2), ALU.subtract), router_d)
            dve.wait_ge(router_a.sem, 1)
            do(tt_op(rl, rl, sel, ALU.mult))
            do(dve.tensor_reduce(rmx, rl.rearrange("p (a e) -> p a e", a=2), AX.X, ALU.add))
            do(dve.reciprocal(rmx, rmx))
            for a in range(2):
                do(ts(rgate[:, a, 0:NE], rl[:, 8 * a:8 * a + 8], rmx[:, a:a + 1], None, ALU.mult))
                do(dve.tensor_copy(rsel[:, a, 0:NE], sel[:, 8 * a:8 * a + 8]))
            dve.wait_ge(router_s.sem, 2)
            for a in range(2):
                do(dve.tensor_copy(rpos[:, a, 0:NE], ps[:, 1, 8 * a:8 * a + 8]))
            do(dve.tensor_reduce(rmx[:, 0:1], ps[:, 1, 16:24], AX.X, ALU.max))
            do(ts(ovf[:], rmx[:, 0:1], float(P), None, ALU.is_gt), router_d)

            def choose(col, f):
                for a in range(2):
                    ts(G[:, a, :], iota[:], rpos[:, a, bass.ds(col, 1)], rsel[:, a, bass.ds(col, 1)],
                       ALU.is_equal, ALU.mult)
                    ins = ts(Gg[:, a, :], iota[:], rpos[:, a, bass.ds(col, 1)], rgate[:, a, bass.ds(col, 1)],
                             ALU.is_equal, ALU.mult)
                ins.then_inc(f.sem, 1)

            def add_pieces(ve):
                for q in range(4):
                    dve.wait_ge(sc_full.sem, 4 * ve + q + 1)
                    tt_op(residual(q), residual(q), ps[:, 1 + 2 * (q % 2), :], ALU.add).then_inc(x_added.sem, 1)

            def experts(first, ps_no):
                dve.memset(GT, 0.0).then_inc(gt_ready.sem, 1)
                for hf in range(2):
                    dve.memset(ys[:, hf * 512:(hf + 1) * 512], 0.0).then_inc(ys_ready.sem, 1)
                choose(0, g_ready)
                with dve.Fori(first, first + NE) as e:
                    ve = e - 1 + ps_no
                    for r in range(2):
                        dve.wait_ge(gat_full.sem, 2 * (e - 1) + r + 1)
                        tt_op(xgT[:, 4 * r:4 * r + 4, :], v3(ps[:, 6 + r, :], 4),
                              bc(pp(1, "ln_ffn", 4 * r, 4), [P, 4, P], 2), ALU.mult).then_inc(xg_ready.sem, 1)
                    add_pieces(ve)
                    dve.wait_ge(gt_full.sem, e)
                    dve.tensor_copy(GT, v3(ps[:, 2, 0:2 * P], 2)).then_inc(gt_ready.sem, 1)
                    for c in ffn(e, 1):
                        if c == 5:
                            choose(e - first + 1, g_ready)
                add_pieces(first + NE - 1 + ps_no)

            experts(1, 0)
            over = dve.value_load(ovf[0:1, 0:1])
            with dve.If(over > 0):
                do(ts(rpos, rpos, -float(P), None, ALU.add))
                experts(1 + NE, 1)



def kernel(**inputs):
    from concourse import bacc as _bacc
    from concourse.bass_utils import run_bass_kernel_spmd as _run

    a = {k: np.asarray(v) for k, v in inputs.items()}
    L = DEPTH

    def cols(v):
        return v.reshape(L, -1, P).transpose(0, 2, 1)

    def row(v):
        return np.broadcast_to(v[:, None, :], (L, P, v.shape[1]))

    def poles(v):
        return v.reshape(L, 8, P).transpose(0, 2, 1)

    moe_b = np.broadcast_to(a["moe_router_b"], (L, NE))
    parts = {
        "ln_mix": cols(a["ln_mix"]), "ln_ffn": cols(a["ln_ffn"]),
        "conv_w": a["ssd_conv_w"].reshape(L, CONV, 4, P).transpose(0, 3, 2, 1).reshape(L, P, 16),
        "conv_b": cols(a["ssd_conv_b"]), "ssd_norm": cols(a["ssd_norm"]), "att_out": cols(a["att_out_norm"]),
        "q_gain": np.concatenate([a["att_q_norm"]] * 2, axis=1)[:, :, None],
        "k_gain": np.concatenate([a["att_k_norm"]] * 2, axis=1)[:, :, None],
        "mu": cols(a["rwkv_mu"]), "w0": cols(a["rwkv_w0"]), "a0": cols(a["rwkv_a0"]), "k_k": cols(a["rwkv_k_k"]),
        "k_a": cols(a["rwkv_k_a"]), "r_k": cols(a["rwkv_r_k"]), "ln_w": cols(a["rwkv_ln_w"]),
        "ln_b": cols(a["rwkv_ln_b"]), "s5_d": cols(a["s5_d"]), "glu_b": cols(a["s5_glu_b"]),
        "s5_out": cols(a["s5_out_norm"]), "a_re": poles(a["s5_a_re"]), "a_im": poles(a["s5_a_im"]),
        "log_dt": poles(np.broadcast_to(a["s5_log_dt"][:, :, None], (L, 16, 64))),
        "dt_bias": row(a["ssd_dt_bias"]), "a_log": row(a["ssd_a_log"]), "ssd_d": row(a["ssd_d"]),
        "router_b": row(moe_b),
    }
    params = np.concatenate([parts[k] for k in PCOLS], axis=2)

    def b_rows(b):
        w = np.zeros((L, 2, 4, 2, 16, 2, 64), b.dtype)
        v = b.reshape(L, 2, 4, 2, 64, 16)
        for g in range(2):
            w[:, :, :, g, :, g, :] = v[:, :, :, g].transpose(0, 1, 2, 4, 3)
        return w.transpose(0, 2, 3, 4, 1, 5, 6).reshape(L, P, 256)

    def c_cols(c):
        return c.reshape(L, 8, 2, 16, 64).transpose(0, 2, 4, 1, 3).reshape(L, P, P)

    def k_rows(w):
        return w.reshape(L, -1, P, w.shape[2]).transpose(0, 2, 1, 3).reshape(L, P, -1)

    small = np.concatenate([
        np.concatenate([a["rwkv_w2"], a["rwkv_a2"]], axis=1), a["rwkv_g2"], k_rows(a["s5_glu_w"]),
        b_rows(a["s5_b_re"]), b_rows(a["s5_b_im"]), c_cols(a["s5_c_re"]), c_cols(a["s5_c_im"]),
        k_rows(np.broadcast_to(a["moe_router_w"], (L, D, NE)))], axis=2)

    w_in = a["w_in"]
    q0 = 772
    r0 = q0 + 768
    s0 = r0 + 1024
    starts = [r0 + P * i for i in range(8)] + [s0, s0 + P] + [P * i for i in range(4)] + [q0 + P * i for i in range(4)]
    mix = np.zeros((L, M_UNITS, P, MUNIT), w_in.dtype)
    w_out = a["w_out"].reshape(L, 8, P, D)
    tm = np.concatenate([w_in[:, :, 512:768], w_in[:, :, q0 + 512:q0 + 768], w_in[:, :, 768:772]], axis=2)
    for at, (kind, i) in enumerate(UNITS):
        if kind == "fm":
            mix[:, at, :, :D] = k_rows(w_in[:, :, starts[i]:starts[i] + P])
        elif kind == "tm":
            mix[:, at, :, :2 * TMW] = k_rows(tm[:, 2 * P * i:2 * P * (i + 1)])
        else:
            mix[:, at, :, :D] = w_out[:, i]

    def gate_up(g, u):
        n = g.shape[0]
        w = np.stack([v.reshape(n, GUQ, GUK, P, NC_, FC) for v in (g, u)], axis=6)
        return np.ascontiguousarray(w.transpose(0, 4, 1, 3, 2, 6, 5)).reshape(n, GU_UNITS, P, GUK, 2 * FC)

    arrays = {
        "x": a["x"].reshape(T, D), "params": params, "small_w": small, "mix_w": mix,
        "gu_dense": gate_up(a["ffn_w_gate"], a["ffn_w_up"])[0], "d_dense": a["ffn_w_down"][0],
        "gu_moe": gate_up(a["moe_w_gate"][0], a["moe_w_up"][0]), "d_moe": a["moe_w_down"][0],
    }
    arrays = {k: np.ascontiguousarray(v) for k, v in arrays.items()}
    nc = _bacc.Bacc("TRN2", target_bir_lowering=False, num_devices=1)
    args = [nc.dram_tensor(f"in_{k}", v.shape, mybir.dt.from_np(v.dtype), kind="ExternalInput").ap()
            for k, v in arrays.items()]
    out = nc.dram_tensor("out_x", (T, D), F32, kind="ExternalOutput").ap()
    trunk(nc, *args, out)
    r = _run(nc, [{f"in_{k}": v for k, v in arrays.items()}], core_ids=[0])
    return r.results[0]["out_x"].reshape(1, T, D)
```

```python
from contextlib import ExitStack

import numpy as np

import concourse.bass as bass
from concourse import mybir

F32 = mybir.dt.float32
I32 = mybir.dt.int32
ALU = mybir.AluOpType
ACT = mybir.ActivationFunctionType
AX = mybir.AxisListType

P = 128
D = 1024
KT = D // P
T = 256
TT = T // P
GW = 256
HD = 64
H = GW // HD
DEPTH = 2
F = 2816
NE = 8
EPS = 1e-6
GN_EPS = 64e-5
DECAY = 0.606531
LOG2E_SLOPES = [2.0 ** (-8.0 / H * (h + 1)) for h in range(H)]
PATTERNS = ((128, 1), (512, 4), (2048, 16))
CONV = 4

FC = 256
NC_ = F // FC
GUK = 2
GUQ = KT // GUK
GU_UNITS = NC_ * GUQ
R_GU = 4
NF = F // P
D_UNITS = NF
R_D = 2
R_M = 5
TMW = 2 * GW + H

PCOLS = {}
_at = 0
for _name, _n in (("ln_mix", 8), ("ln_ffn", 8), ("conv_w", 16), ("conv_b", 4), ("ssd_norm", 2), ("att_out", 2),
                  ("q_gain", 1), ("k_gain", 1), ("mu", 8), ("w0", 2), ("a0", 2), ("k_k", 2), ("k_a", 2),
                  ("r_k", 2), ("ln_w", 2), ("ln_b", 2), ("s5_d", 2), ("glu_b", 2), ("s5_out", 2),
                  ("a_re", 8), ("a_im", 8), ("log_dt", 8), ("dt_bias", 4), ("a_log", 4), ("ssd_d", 4),
                  ("router_b", 8)):
    PCOLS[_name] = (_at, _n)
    _at += _n
NPAR = _at
WCOLS = {}
_at = 0
for _name, _n in (("w2a2", 256), ("g2", 256), ("glu", 512), ("b_re", 256), ("b_im", 256), ("c_re", 128),
                  ("c_im", 128), ("router", 64)):
    WCOLS[_name] = (_at, _n)
    _at += _n
NSW = _at
ARENA = 11796 + 13 * 512 + 256 + 6144
MUNIT = 4 * 258
FM_ORDER = (4, 0, 1, 2, 3, 5, 6, 7, 8)
GROUPS = ("ssd", "att", "rwkv", "s5")
MIX_ORDER = ("s5", "ssd", "att", "rwkv")
WO_ORDER = [2 * GROUPS.index(g) + i for g in MIX_ORDER for i in range(2)]
UNITS = ([("fm", 2 * q + i) for q in FM_ORDER[:8] for i in range(2)] + [("tm", i) for i in range(4)]
         + [("fm", 2 * q + i) for q in FM_ORDER[8:] for i in range(2)] + [("wo", k) for k in WO_ORDER])
M_UNITS = len(UNITS)


class Flag:

    def __init__(self, nc, ctx, name, per):
        self.sem, self.per, self.n = ctx.enter_context(nc.semaphore(name)), per, 0

    def at(self, layer, i):
        return layer * self.per + i


class Chain:

    def __init__(self, eng, sem):
        self.eng, self.sem, self.n = eng, sem, 0

    def __call__(self, ins, flag=None):
        if flag is None:
            self.n += 1
            ins.then_inc(self.sem, 1)
            self.eng.wait_ge(self.sem, self.n)
        else:
            flag.n += 1
            ins.then_inc(flag.sem, 1)
            self.eng.wait_ge(flag.sem, flag.n)


def trunk(nc, x_in, params, small_w, mix_w, gu_dense, d_dense, gu_moe, d_moe, out):
    ctx = ExitStack()
    with ctx:
        def sb(name, shape, dt=F32):
            return ctx.enter_context(nc.sbuf_tensor(name, shape, dt))

        def flag(name, per=1):
            return Flag(nc, ctx, name, per)

        x = sb("x", [P, TT, D])
        par = sb("par", [P, DEPTH, NPAR])
        sw = sb("sw", [P, NSW])
        mring = sb("mring", [P, R_M, MUNIT])
        guring = sb("guring", [P, R_GU, GUK, 2 * FC])
        dring = sb("dring", [P, R_D, D])
        ident = sb("ident", [P, P])
        ones = sb("ones", [P, P])
        blk = sb("blk", [P, P])
        m_gt = sb("m_gt", [P, P])
        m_lt = sb("m_lt", [P, P])
        m_leo = sb("m_leo", [P, T])
        m_le = m_leo[:, 0:P]
        lvl = sb("lvl", [P, 7, P])
        bias0 = sb("bias0", [P, H, P])
        bias1 = sb("bias1", [P, H, T])
        cnt0 = sb("cnt0", [P, P])
        cnt1 = sb("cnt1", [P, T])
        iota = sb("iota", [P, P])
        tie = sb("tie", [P, NE, NE])
        s5p = sb("s5p", [P, DEPTH, 6, 8])
        s5t = sb("s5t", [P, 10, DEPTH * 8])
        e_re = sb("e_re", [P, 8, T])
        e_im = sb("e_im", [P, 8, T])
        st = sb("st", [P, 128])
        xh = sb("xh", [P, TT, D])
        arena = sb("arena", [P, ARENA])
        at = [0]

        def flat(a):
            return a.rearrange("p m t -> p (m t)")

        def v3(a, m):
            return a.rearrange("p (m t) -> p m t", m=m)

        def take(n, reset=None):
            if reset is not None:
                at[0] = reset
            a = arena[:, at[0]:at[0] + n]
            at[0] += n
            assert at[0] <= ARENA, at[0]
            return a

        hT = v3(take(2048), KT)
        MIX_AT = at[0]
        mixT = v3(take(2048), 8)
        zv = v3(take(1024), TT)
        rk_raw = take(8 * 257)
        rk = v3(rk_raw, 8)
        pf = v3(take(2048), 8)
        u5 = v3(take(512), 2)
        xbc = v3(take(4 * 259), 4)
        qk = v3(take(1024), 4)
        sA, cs, cp, eE, eX, eM, kk, kp, rw_g, rw_b, kk2, rsq = (v3(take(512), 2) for _ in range(12))
        gy = v3(take(512), TT)
        s0 = v3(take(256), 2)
        nm, m2, mb, mk = (v3(rk_raw[:, i * 512:(i + 1) * 512], H) for i in range(4))
        tm_, tt_, xs_ = (v3(flat(a), H) for a in (kk, cs, eM))
        zs, us = flat(kk2)[:, 0:256], flat(kk2)[:, 256:512]
        gsq = flat(rsq)[:, 0:256]
        xflat = xh[:, :, :].rearrange("p a d -> p (a d)")
        vt = v3(xflat[:, 0:512], TT)
        bkt = v3(xflat[:, 512:1024], 4)
        noff = xflat[:, 1024:2048].rearrange("p (b h t) -> p b h t", b=2, h=H)
        scratch = at[0]
        cv = v3(take(1024), 4)
        sg = v3(take(1024), 4)
        r0 = sg
        xs = v3(take(512), TT)
        xd = v3(take(512), TT)
        L0 = v3(take(1024), H)
        L1 = v3(take(512), H)
        sc0 = v3(take(512), 2)
        sc1 = v3(take(256), 2)
        r1 = v3(take(512), H)
        pt0 = v3(take(512, scratch + 2560), H)
        take(512)
        pt1, pt2 = (v3(take(512), H) for _ in range(2))
        ya = v3(take(512), TT)
        sq = v3(arena[:, 0:1024], 4)
        a1 = v3(arena[:, 0:1024], H)
        a0 = v3(arena[:, 1024:1536], H)
        z5 = take(4096, scratch).rearrange("p (j c t) -> p j c t", j=8, c=2)
        p5raw = take(2048)
        p5 = p5raw.rearrange("p (b s c t) -> p b s c t", b=2, s=2, c=2)
        y5, g5, q5, g5s = (v3(p5raw[:, i * 512:(i + 1) * 512], 2) for i in range(4))
        cpad_re = mixT[:, 0:4, :].rearrange("p m (a t) -> p (m a) t", a=2)
        cpad_im = mixT[:, 4:8, :].rearrange("p m (a t) -> p (m a) t", a=2)
        sil = v3(take(512, 2048), 2)
        av = v3(take(512), 2)
        avT = take(512).rearrange("p (b f s) -> p b f s", b=2, f=2)
        xgT = v3(take(1024), KT)
        ys = take(1024)
        G = v3(take(256), TT)
        Gg = v3(take(256), TT)
        GT = v3(take(256), TT)
        rt = take(1024)
        tab_tmp = sb("tab_tmp", [P, 512])
        tab_tmp_v = flat(gy)
        c5 = sb("c5", [P, 3, P])
        sel_, rl, rlg, rrk, rmx = rt[:, 0:16], rt[:, 16:32], rt[:, 32:48], rt[:, 48:64], rt[:, 64:66]
        rtab = rt[:, 66:120]
        rgate, rsel, rpos = (v3(rtab[:, 18 * i:18 * i + 18], 2) for i in range(3))
        st_at = [0]

        def small_tile(n):
            st_at[0] += n
            return st[:, st_at[0] - n:st_at[0]]

        ssx, rsx, ssy, ssa, dec = (small_tile(2) for _ in range(5))
        ncm, ael = small_tile(4), small_tile(4)
        dtr, dta, dte, dtl, dtu, sa, gst, amx = (small_tile(8) for _ in range(8))
        dtr3 = v3(dtr, 2)
        pw = sb("pw", [P, 3, 4])
        pw_v = sb("pw_v", [P, 3, 4])
        S_AT = ("dt", "da", "r", "k", "r2", "mag", "sin", "cos")

        def S(name):
            return s5t[:, S_AT.index(name), :].rearrange("p (l j) -> p l j", l=DEPTH)

        def par3(name):
            a_, n_ = PCOLS[name]
            return par[:, :, a_:a_ + n_]

        ovf = sb("ovf", [P, 1], I32)
        it_x = sb("it_x", [P, P], I32)
        it_y = sb("it_y", [P, P], I32)
        it_d = sb("it_d", [P, 384], I32)

        ps = ctx.enter_context(nc.psum_tensor("ps", [P, 8, 512], F32))

        ch_act, ch_dve, ch_pool = (ctx.enter_context(nc.semaphore(n)) for n in ("act_chain", "dve_chain", "pool_chain"))
        x_in_sem = [ctx.enter_context(nc.semaphore(f"x_loaded{tt}")) for tt in range(TT)]
        par_sem = ctx.enter_context(nc.semaphore("params_loaded"))
        sw_sem = ctx.enter_context(nc.semaphore("small_weights_loaded"))
        out_sem = ctx.enter_context(nc.semaphore("out_stored"))
        m_full = [ctx.enter_context(nc.semaphore(f"mix_weight_full{i}")) for i in range(R_M)]
        gu_full_s = [ctx.enter_context(nc.semaphore(f"gate_up_full{i}")) for i in range(R_GU)]
        d_full_s = [ctx.enter_context(nc.semaphore(f"down_full{i}")) for i in range(R_D)]
        bank_full = [ctx.enter_context(nc.semaphore(f"bank_full{i}")) for i in range(8)]

        ident_ready = flag("ident_ready")
        consts_pool = flag("consts_pool")
        consts_dve = flag("consts_dve")
        poles = flag("poles", 1)
        pole_a = flag("pole_a", 3)
        pole_d = flag("pole_d", 2)
        sumsq = flag("sumsq", 4)
        rs_in = flag("rs_in", 4)
        rs_out = flag("rs_out", 4)
        xh_ready = flag("xh_ready", 4)
        h_evac = flag("h_evac", 8)
        fm_out = flag("fm_out", 9)
        zv_out = flag("zv_out", 2)
        dt_out = flag("dt_out", 1)
        rk_mixed = flag("rk_mixed", 1)
        lora_in = flag("lora_in", 1)
        rk_act = flag("rk_act", 3)
        rk_cs = flag("rk_cs", 1)
        rk_exp = flag("rk_exp", 1)
        rk_sq = flag("rk_sq", 1)
        rk_ss = flag("rk_ss", 1)
        rk_rs = flag("rk_rs", 1)
        rk_hat = flag("rk_hat", 1)
        rk_bon = flag("rk_bon", 1)
        rk_bonus = flag("rk_bonus", 1)
        rk_tok = flag("rk_tok", 2)
        rk_mat = flag("rk_mat", 8)
        rk_off = flag("rk_off", 14)
        rk_x = flag("rk_x", 12)
        rk_tt = flag("rk_tt", 14)
        rk_t = flag("rk_t", 12)
        rk_z = flag("rk_z", 2)
        rk_u = flag("rk_u", 2)
        rk_s = flag("rk_s", 1)
        gn_x = flag("gn_x", 2)
        gn_in = flag("gn_in", 2)
        gn_rs = flag("gn_rs", 2)
        gn_y = flag("gn_y", 2)
        rk_yt = flag("rk_yt", 2)
        mix_done = flag("mix_done", 4)
        ssd_cv = flag("ssd_cv", 1)
        ssd_sg = flag("ssd_sg", 1)
        ssd_xbc = flag("ssd_xbc", 1)
        dt_a = flag("dt_a", 1)
        dt_b = flag("dt_b", 1)
        dt_c = flag("dt_c", 1)
        dt_d = flag("dt_d", 1)
        ssd_a = flag("ssd_a", 1)
        ssd_xs = flag("ssd_xs", 1)
        ssd_r = flag("ssd_r", 1)
        ssd_l = flag("ssd_l", 3)
        ssd_sc = flag("ssd_sc", 2)
        ssd_p = flag("ssd_p", 1)
        ssd_y = flag("ssd_y", 1)
        ssd_ss = flag("ssd_ss", 1)
        ssd_v = flag("ssd_v", 1)
        ssd_rs = flag("ssd_rs", 1)
        ssd_n = flag("ssd_n", 1)
        att_sq = flag("att_sq", 1)
        att_ss = flag("att_ss", 2)
        att_rs = flag("att_rs", 1)
        att_qk = flag("att_qk", 1)
        att_s = flag("att_s", 4)
        att_m = flag("att_m", 2)
        att_e = flag("att_e", 2)
        att_p = flag("att_p", 2)
        att_pt = flag("att_pt", 3)
        att_y = flag("att_y", 1)
        att_v = flag("att_v", 1)
        att_rs2 = flag("att_rs2", 1)
        att_n = flag("att_n", 1)
        tab = flag("tab", 1)
        s5_c = flag("s5_c", 1)
        s5_in = flag("s5_in", 8)
        s5_z = flag("s5_z", 8)
        s5_back = flag("s5_back", 8)
        s5_h = flag("s5_h", 8)
        s5_y = flag("s5_y", 1)
        s5_g = flag("s5_g", 1)
        s5_sig = flag("s5_sig", 1)
        s5_sq = flag("s5_sq", 1)
        s5_ss = flag("s5_ss", 1)
        s5_rs = flag("s5_rs", 1)
        wo_used = flag("wo_used", 6)
        x_mixed = flag("x_mixed", 4)
        gu_used = flag("gu_used", NC_ * (GUQ - 1))
        gu_done = flag("gu_done", NC_)
        gu_done0 = flag("gu_done0", NC_)
        av_ready = flag("av_ready", NC_)
        sil_ready = flag("sil_ready", NC_)
        t_full = flag("t_full", NC_)
        avT_ready = flag("avT_ready", NC_)
        d_used = flag("d_used", D_UNITS - 1)
        y_done = flag("y_done", 2)
        y_first = flag("y_first", 1)
        x_ffn = flag("x_ffn", 4)
        g_ready = flag("g_ready", 1)
        gat_full = flag("gat_full", 2)
        xg_ready = flag("xg_ready", 2)
        sc_full = flag("sc_full", 4)
        x_added = flag("x_added", 4)
        gt_full = flag("gt_full", 1)
        gt_ready = flag("gt_ready", 1)
        ys_ready = flag("ys_ready", 2)
        router_s = flag("router_s", 2)
        router_d = flag("router_d", 2)
        router_a = flag("router_a", 1)
        router_m = flag("router_m", 1)

        def need(eng, f, layer, i):
            eng.wait_ge(f.sem, f.at(layer, i))

        def pp(layer, name, i=0, n=None):
            a, m = PCOLS[name]
            return par[:, layer, a + i:a + i + (m if n is None else n)]

        def ww(name):
            a, m = WCOLS[name]
            return sw[:, a:a + m]

        def bc(a, shape, axis):
            return a.unsqueeze(axis).to_broadcast(shape)

        place, prev, uses = {}, {}, [0] * 8
        last_in = [None] * 8
        turn_of_banks = list(range(8))

        def fm_n(q):
            return FM_ORDER.index(q) + 1

        def mix_n(group):
            return MIX_ORDER.index(group) + 1

        def tile_(key, f, i):
            b = turn_of_banks.pop(0)
            turn_of_banks.append(b)
            prev[key] = last_in[b]
            place[key] = (b, uses[b])
            last_in[b] = (f, i)
            uses[b] += 1

        PRODUCT_TILES = ("NM2e", "NM2o", "MBKe", "MBKo")

        ATT_TILES = (("S0e", 0, (0, 2)), ("S0o", 0, (1, 3)), ("S1e", 1, (0, 2)), ("S1o", 1, (1, 3)))

        READER = {"lw": (rk_act, 1), "la": (rk_act, 2), "lg": (rk_act, 3), "kks": (rk_ss, 1), "zv0": (zv_out, 1),
                  "zv1": (zv_out, 2), "dt": (dt_out, 1), "bon": (rk_bonus, 1), "xt": (ssd_xs, 1), "dA": (ssd_l, 1),
                  "dB": (ssd_l, 2), "d1": (ssd_l, 3), "sc0": (ssd_sc, 1), "sc1": (ssd_sc, 2), "sy": (ssd_y, 1),
                  "vt": (rk_tok, 1), "bkt": (rk_tok, 2), "syt": (mix_done, mix_n("ssd")), "qs": (att_ss, 1),
                  "ks": (att_ss, 2), "P0": (att_pt, 1), "P1": (att_pt, 2), "P2": (att_pt, 3), "ya": (att_n, 1),
                  "yat": (mix_done, mix_n("att")), "y5": (s5_y, 1), "glu": (s5_sig, 1), "o5": (s5_ss, 1),
                  "S": (rk_s, 1), "S0e": (att_s, 1), "S0o": (att_s, 2), "S1e": (att_s, 3), "S1o": (att_s, 4)}
        for q in range(4):
            READER["h", q] = (h_evac, q + 1)
            READER["h2", q] = (h_evac, 4 + q + 1)
            READER["wo", q] = (x_mixed, q + 1)
        for q in range(9):
            READER["fm", q] = (fm_out, fm_n(q))
        for j in range(8):
            READER["bu", j] = (s5_in, j + 1)
        for c in range(TT):
            READER["Z", c] = (rk_z, c + 1)
            READER["U", c] = (rk_u, c + 1)
            READER["Y", c] = (gn_x, c + 1)
            READER["yt", c] = (rk_yt, c + 1)
            for q, n in enumerate(PRODUCT_TILES):
                READER[n, c] = (rk_mat, 4 * c + q + 1)
            for l in range(7):
                READER["X", c, l] = (rk_x, 6 * c + l) if l else (rk_tt, 7 * c + 1)
                READER["TT", c, l] = (rk_tt, 7 * c + l + 1)
                READER["T", c, l] = (rk_t, 6 * c + l + 1)

        def T_(c, l):
            return [("TT", c, l)] + ([("T", c, l)] if l < 6 else [])

        TILE_ORDER = (
            [("h", q) for q in range(4)] + [("fm", 4), ("fm", 0), ("fm", 1), ("bu", 0), ("bu", 1), ("fm", 2)]
            + [("bu", 2), ("bu", 3), ("bu", 4), ("fm", 3), ("bu", 5), ("bu", 6), ("bu", 7), ("fm", 5)]
            + ["lw", "la", "lg", "kks", ("fm", 6), "bon", ("fm", 7), "vt", "bkt"] + [(n, 0) for n in PRODUCT_TILES]
            + ["zv0", ("X", 0, 0), "y5", ("X", 0, 1)] + T_(0, 1) + [("X", 0, 2), "zv1"] + T_(0, 2) + ["glu", ("X", 0, 3), "dt"]
            + T_(0, 3) + ["o5", ("X", 0, 4)] + T_(0, 4) + [("X", 0, 5), ("fm", 8)] + T_(0, 5)
            + [("X", 0, 6), "xt"] + T_(0, 6) + ["qs", "ks", ("Z", 0), "sc0", "sc1", ("U", 0), "dA", "dB", "d1", "S", ("Y", 0)]
            + [(n, 1) for n in PRODUCT_TILES] + ["S0e", "S0o", ("X", 1, 0), "S1e", "S1o", ("X", 1, 1)]
            + T_(1, 1) + ["sy", ("X", 1, 2), ("yt", 0)] + T_(1, 2) + [("wo", q) for q in range(4)]
            + [("X", 1, 3)] + T_(1, 3) + ["P0", ("X", 1, 4), "syt"] + T_(1, 4) + ["P1", ("X", 1, 5), "P2"]
            + T_(1, 5) + [("X", 1, 6), "ya"] + T_(1, 6) + [("Z", 1), ("U", 1), "yat", ("Y", 1), ("yt", 1)]
            + [("h2", q) for q in range(4)])
        for key in TILE_ORDER:
            tile_(key, *READER[key])
            if key == ("wo", 3):
                turn_of_banks = [b for b in turn_of_banks if b not in [place["wo", q][0] for q in range(4)]]
        assert len(TILE_ORDER) == len(set(TILE_ORDER))
        taken = []

        def acquire(pe, layer, key):
            assert TILE_ORDER[len(taken) % len(TILE_ORDER)] == key, (TILE_ORDER[len(taken) % len(TILE_ORDER)], key)
            taken.append(key)
            if prev[key]:
                need(pe, prev[key][0], layer, prev[key][1])
            return ps[:, place[key][0], :]

        def filled(ins, key):
            ins.then_inc(bank_full[place[key][0]], 1)

        def has(eng, layer, key, i0=0, n=512):
            b, i = place[key]
            eng.wait_ge(bank_full[b], layer * uses[b] + i + 1)
            return ps[:, b, i0:i0 + n]

        unit_at = {u: i for i, u in enumerate(UNITS)}
        assert len(UNITS) == M_UNITS and M_UNITS % R_M == 0

        def unit_used(sp, layer, u):
            kind, i = u
            if kind == "wo" and i not in WO_ORDER[6:]:
                need(sp, wo_used, layer, WO_ORDER.index(i) + 1)
            else:
                has(sp, layer, ("fm", i // 2) if kind == "fm" else "dt" if kind == "tm" else ("wo", 3))

        def unit(pe, layer, u):
            i = unit_at[u]
            pe.wait_ge(m_full[i % R_M], 16 * (layer * (M_UNITS // R_M) + i // R_M + 1))
            return mring[:, i % R_M, :]

        def gu_read(e, q):
            if q % GUQ < GUQ - 1:
                return gu_used, e * gu_used.per + (q // GUQ) * (GUQ - 1) + q % GUQ + 1
            return gu_done, e * gu_done.per + q // GUQ + 1

        def d_read(e, q):
            if q < D_UNITS - 1:
                return d_used, e * d_used.per + q + 1
            return y_done, e * y_done.per + 2

        def rotation_tables(do, eng, layer, j0, n, tmp_, pw):
            tt_op = eng.tensor_tensor
            js = slice(j0, j0 + n)
            do(eng.memset(e_re[:, js, 0:1], 1.0))
            do(eng.memset(e_im[:, js, 0:1], 0.0))
            do(eng.tensor_copy(pw[:, 0, 0:n], s5p[:, layer, 0, js]))
            do(eng.tensor_copy(pw[:, 1, 0:n], s5p[:, layer, 1, js]))
            k = 1
            while k < T:
                tmp = tmp_[:, 0:n * k].rearrange("p (j t) -> p j t", j=n)
                c_ = bc(pw[:, 0, 0:n], [P, n, k], 2)
                s_ = bc(pw[:, 1, 0:n], [P, n, k], 2)
                re, im = e_re[:, js, 0:k], e_im[:, js, 0:k]
                do(tt_op(e_re[:, js, k:2 * k], re, c_, ALU.mult))
                do(tt_op(tmp, im, s_, ALU.mult))
                do(tt_op(e_re[:, js, k:2 * k], e_re[:, js, k:2 * k], tmp, ALU.subtract))
                do(tt_op(e_im[:, js, k:2 * k], re, s_, ALU.mult))
                do(tt_op(tmp, im, c_, ALU.mult))
                do(tt_op(e_im[:, js, k:2 * k], e_im[:, js, k:2 * k], tmp, ALU.add))
                k *= 2
                if k < T:
                    do(tt_op(pw[:, 2, 0:n], pw[:, 1, 0:n], pw[:, 1, 0:n], ALU.mult))
                    do(tt_op(pw[:, 1, 0:n], pw[:, 0, 0:n], pw[:, 1, 0:n], ALU.mult))
                    do(tt_op(pw[:, 1, 0:n], pw[:, 1, 0:n], pw[:, 1, 0:n], ALU.add))
                    do(tt_op(pw[:, 0, 0:n], pw[:, 0, 0:n], pw[:, 0, 0:n], ALU.mult))
                    do(tt_op(pw[:, 0, 0:n], pw[:, 0, 0:n], pw[:, 2, 0:n], ALU.subtract))

        LAST_BANKS = (1, 3, 6, 7)

        block = ctx.enter_context(nc.Block())

        @block.sync
        def _(sp):
            sp.dma_start(par[:], params.rearrange("l p n -> p l n")).then_inc(par_sem, 16)
            for tt in range(TT):
                sp.dma_start(x[:, tt, :], x_in[tt * P:(tt + 1) * P, :]).then_inc(x_in_sem[tt], 16)

            def small(layer):
                if layer:
                    need(sp, x_mixed, layer - 1, 4)
                sp.dma_start(sw[:], small_w[layer]).then_inc(sw_sem, 16)

            def mix_unit(layer, i):
                g = layer * M_UNITS + i
                if g >= R_M:
                    unit_used(sp, (g - R_M) // M_UNITS, UNITS[(i - R_M) % M_UNITS])
                sp.dma_start(mring[:, i % R_M, :], mix_w[layer, i]).then_inc(m_full[i % R_M], 16)

            def gu_unit(e, q, src, first):
                if not first:
                    f, n = gu_read(e, q - R_GU) if q >= R_GU else gu_read(e - 1, GU_UNITS + q - R_GU)
                    sp.wait_ge(f.sem, n)
                sp.dma_start(guring[:, q % R_GU], src).then_inc(gu_full_s[q % R_GU], 16)

            def d_unit(e, q, src, first):
                if not first:
                    f, n = d_read(e, q - R_D) if q >= R_D else d_read(e - 1, D_UNITS + q - R_D)
                    sp.wait_ge(f.sem, n)
                sp.dma_start(dring[:, q % R_D], src).then_inc(d_full_s[q % R_D], 16)

            def ffn_stream(e, gu_src, d_src, q0, d0):
                for c in range(NC_ + 1):
                    if c < NC_:
                        for q in range(GUQ * c, GUQ * c + GUQ):
                            if q >= q0:
                                gu_unit(e, q, gu_src(q), False)
                    if c >= 1:
                        for q in range(2 * (c - 1), 2 * c):
                            if q >= d0:
                                d_unit(e, q, d_src(q), False)

            def d_rows(w, q):
                return w[q * P:(q + 1) * P, :]

            for i in range(R_M):
                mix_unit(0, i)
            small(0)
            for i in range(R_M, M_UNITS):
                mix_unit(0, i)
                if i == 12:
                    for q in range(R_GU):
                        gu_unit(0, q, gu_dense[q], True)
                    for q in range(R_D):
                        d_unit(0, q, d_rows(d_dense, q), True)
            small(1)
            ffn_stream(0, lambda q: gu_dense[q], lambda q: d_rows(d_dense, q), R_GU, R_D)
            for i in range(M_UNITS):
                mix_unit(1, i)

            def experts(first):
                with sp.Fori(first, first + NE) as e:
                    gw = gu_moe[bass.ds(e - first, 1)].rearrange("a q p k n -> (a q) p k n")
                    dw = d_moe[bass.ds(e - first, 1)].rearrange("a f d -> (a f) d")
                    ffn_stream(e, lambda q: gw[q], lambda q: d_rows(dw, q), 0, 0)

            experts(1)
            sp.wait_ge(router_d.sem, 2)
            over = sp.value_load(ovf[0:1, 0:1])
            with sp.If(over > 0):
                experts(1 + NE)
                sp.wait_ge(x_added.sem, 8 * NE + 8)
            for tt in range(TT):
                sp.wait_ge(x_added.sem, 4 * NE + 2 * tt + 2)
                sp.dma_start(out[tt * P:(tt + 1) * P, :], x[:, tt, :]).then_inc(out_sem, 16)
            sp.wait_ge(out_sem, 16 * TT)

        @block.tensor
        def _(pe):
            mm = pe.matmul

            def transposes(layer, key, srcs):
                t = acquire(pe, layer, key)
                for i, s in enumerate(srcs):
                    ins = pe.transpose(t[:, i * P:(i + 1) * P], s, ident[:])
                filled(ins, key)

            def norm_transpose(layer, name, n):
                for q in range(4):
                    if q % 2 == 0:
                        need(pe, xh_ready, layer, 2 * (n - 1) + q // 2 + 1)
                    transposes(layer, (name, q), [xh[:, q // 2, (4 * (q % 2) + i) * P:(4 * (q % 2) + i + 1) * P]
                                                  for i in range(4)])

            def fm(layer, q):
                t = acquire(pe, layer, ("fm", q))
                if q == FM_ORDER[0]:
                    need(pe, h_evac, layer, 4)
                for i in range(2):
                    w = unit(pe, layer, ("fm", 2 * q + i))
                    for k in range(KT):
                        ins = mm(t[:, i * T:(i + 1) * T], w[:, k * P:(k + 1) * P], hT[:, k, :],
                                 start=(k == 0), stop=(k == KT - 1))
                filled(ins, ("fm", q))

            def tm(layer, tt):
                t = acquire(pe, layer, f"zv{tt}")
                for k in range(KT):
                    w = unit(pe, layer, ("tm", k // 2))[:, (k % 2) * TMW:(k % 2) * TMW + 2 * GW]
                    ins = mm(t, hT[:, k, tt * P:(tt + 1) * P], w, start=(k == 0), stop=(k == KT - 1))
                filled(ins, f"zv{tt}")

            def tm_dt(layer):
                t = acquire(pe, layer, "dt")
                for tt in range(TT):
                    for k in range(KT):
                        w = unit(pe, layer, ("tm", k // 2))[:, (k % 2) * TMW + 2 * GW:(k % 2 + 1) * TMW]
                        ins = mm(t[:, tt * H:(tt + 1) * H], hT[:, k, tt * P:(tt + 1) * P], w,
                                 start=(k == 0), stop=(k == KT - 1))
                filled(ins, "dt")

            def lora(layer):
                need(pe, lora_in, layer, 1)
                pe.wait_ge(sw_sem, 16 * (layer + 1))
                for key, rows, src in (("lw", slice(0, 64), 6), ("la", slice(64, 128), 6), ("lg", slice(0, 128), 7)):
                    w = ww("g2") if key == "lg" else ww("w2a2")
                    t = acquire(pe, layer, key)
                    for m in range(2):
                        ins = mm(t[:, m * T:(m + 1) * T], w[rows, m * P:(m + 1) * P], pf[rows, src, :],
                                 start=True, stop=True)
                    filled(ins, key)

            def block_sum(layer, key, f, n, src):
                need(pe, f, layer, n)
                t = acquire(pe, layer, key)
                filled(mm(t, blk[:], src, start=True, stop=True), key)

            def head(h):
                return slice(HD * (h % 2), HD * (h % 2) + HD), h // 2

            def ssd_xt(layer):
                need(pe, ssd_xbc, layer, 1)
                transposes(layer, "xt", [cv[:, m, tt * P:(tt + 1) * P] for tt in range(TT) for m in range(2)])

            def ssd_decays(layer):
                need(pe, ssd_r, layer, 1)
                for key, h in (("dA", 0), ("dB", 2)):
                    t = acquire(pe, layer, key)
                    mm(t, m_gt[:], r0[:, h:h + 2, :], start=True, stop=False)
                    ins = mm(v3(t, 2)[:, :, P:T], ones[:], r1[:, h:h + 2, :], start=False, stop=True)
                    filled(ins, key)
                t = acquire(pe, layer, "d1")
                filled(mm(t, m_gt[:], r1, start=True, stop=True), "d1")

            def ssd_scores(layer):
                for g in range(2):
                    t = acquire(pe, layer, f"sc{g}")
                    rows = slice(64 * g, 64 * g + 64)
                    mm(t[:, 0:T], cv[rows, 2, 0:P], cv[rows, 3, :], start=True, stop=True)
                    filled(mm(t[:, T:T + P], cv[rows, 2, P:T], cv[rows, 3, P:T], start=True, stop=True), f"sc{g}")

            def ssd_output(layer):
                t = acquire(pe, layer, "sy")
                need(pe, ssd_p, layer, 1)
                for h in range(H):
                    c = slice(h * HD, (h + 1) * HD)
                    mm(t[:, h * HD:(h + 1) * HD], L0[:, h, 0:P], xd[:, 0, c], start=True, stop=True)
                    o = t[:, T + h * HD:T + (h + 1) * HD]
                    mm(o, L0[:, h, P:T], xd[:, 0, c], start=True, stop=False)
                    ins = mm(o, L1[:, h, :], xd[:, 1, c], start=False, stop=True)
                filled(ins, "sy")

            def att_sums(layer, key, i):
                need(pe, att_sq, layer, 1)
                t = acquire(pe, layer, key)
                filled(mm(t, blk[:], sq[:, i:i + 2, :], start=True, stop=True), key)

            def att_scores(layer, tt):
                need(pe, att_qk, layer, 1)
                for key, _, hs in ATT_TILES[2 * tt:2 * tt + 2]:
                    t = acquire(pe, layer, key)
                    n = P * (tt + 1)
                    for i, h in enumerate(hs):
                        rows, m = head(h)
                        ins = mm(t[:, i * n:(i + 1) * n], qk[rows, m, tt * P:(tt + 1) * P], qk[rows, 2 + m, 0:n],
                                 start=True, stop=True)
                    filled(ins, key)

            def att_turn(layer, key, n, a, j0):
                need(pe, att_p, layer, n)
                transposes(layer, key, [a[:, h, j0:j0 + P] for h in range(H)])

            def att_values(layer):
                t = acquire(pe, layer, "ya")
                need(pe, att_pt, layer, 3)
                for h in range(H):
                    c = slice(GW + h * HD, GW + (h + 1) * HD)
                    mm(t[:, h * HD:(h + 1) * HD], pt0[:, h, :], zv[:, 0, c], start=True, stop=True)
                    o = t[:, T + h * HD:T + (h + 1) * HD]
                    mm(o, pt1[:, h, :], zv[:, 0, c], start=True, stop=False)
                    ins = mm(o, pt2[:, h, :], zv[:, 1, c], start=False, stop=True)
                filled(ins, "ya")

            def token_to_feature(layer, key, f, n, src):
                need(pe, f, layer, n)
                transposes(layer, key, [src[:, tt, m * P:(m + 1) * P] for m in range(2) for tt in range(TT)])

            def rwkv_products(layer, c):
                ch = slice(c * P, (c + 1) * P)
                for q, key in enumerate(PRODUCT_TILES):
                    t = acquire(pe, layer, (key, c))
                    for i, (a, b) in enumerate((((eX, cp), (kp, eX)), ((cp, eE), (kp, eE)))[q // 2]):
                        for m in range(2):
                            rows, _ = head(q % 2)
                            ins = mm(t[:, (2 * i + m) * P:(2 * i + m + 1) * P], a[rows, m, ch], b[rows, m, ch],
                                     start=True, stop=True)
                    filled(ins, (key, c))

            def rwkv_x(layer, c, l):
                t = acquire(pe, layer, ("X", c, l))
                need(pe, rk_off, layer, 7 * c + l + 1)
                if l:
                    need(pe, rk_tt, layer, 7 * c + l)
                for h in range(H):
                    ins = mm(t[:, h * P:(h + 1) * P], noff[:, l % 2, h, :], tt_[:, h, :] if l else ident[:],
                             start=True, stop=True)
                filled(ins, ("X", c, l))

            def rwkv_t(layer, c, l):
                t = acquire(pe, layer, ("TT", c, l))
                need(pe, rk_x, layer, 6 * c + l)
                need(pe, rk_t, layer, 6 * c + l)
                for h in range(H):
                    ins = mm(t[:, h * P:(h + 1) * P], tm_[:, h, :], xs_[:, h, :], start=True, stop=True)
                filled(ins, ("TT", c, l))
                if l < 6:
                    t = acquire(pe, layer, ("T", c, l))
                    for h in range(H):
                        ins = mm(t[:, h * P:(h + 1) * P], xs_[:, h, :], tm_[:, h, :], start=True, stop=True)
                    filled(ins, ("T", c, l))

            def rwkv_z(layer, c):
                ch = slice(c * P, (c + 1) * P)
                t = acquire(pe, layer, ("Z", c))
                need(pe, rk_mat, layer, 4 * c + 2)
                if c:
                    need(pe, rk_s, layer, 1)
                for m in range(2):
                    if c:
                        mm(t[:, m * P:(m + 1) * P], eX[:, m, ch], s0[:, m, :], start=True, stop=False)
                    for h in (2 * m, 2 * m + 1):
                        ins = mm(t[:, h * HD:(h + 1) * HD], m2[:, h, :], vt[:, c, h * HD:(h + 1) * HD],
                                 start=(c == 0), stop=(c == 0 or h % 2 == 1))
                filled(ins, ("Z", c))

            def rwkv_u(layer, c):
                t = acquire(pe, layer, ("U", c))
                need(pe, rk_tt, layer, 7 * c + 7)
                need(pe, rk_z, layer, c + 1)
                for h in range(H):
                    ins = mm(t[:, h * HD:(h + 1) * HD], tt_[:, h, :], zs[:, h * HD:(h + 1) * HD], start=True, stop=True)
                filled(ins, ("U", c))

            def rwkv_state_y(layer, c):
                ch = slice(c * P, (c + 1) * P)
                need(pe, rk_u, layer, c + 1)
                if c == 0:
                    t = acquire(pe, layer, "S")
                    for m in range(2):
                        o = t[:, m * P:(m + 1) * P]
                        mm(o, bkt[:, m, :], us[:, m * P:(m + 1) * P], start=True, stop=False)
                        ins = mm(o, bkt[:, 2 + m, :], vt[:, 0, m * P:(m + 1) * P], start=False, stop=True)
                    filled(ins, "S")
                t = acquire(pe, layer, ("Y", c))
                need(pe, rk_mat, layer, 4 * c + 4)
                for m in range(2):
                    if c:
                        mm(t[:, m * P:(m + 1) * P], eE[:, m, ch], s0[:, m, :], start=True, stop=False)
                    for h in (2 * m, 2 * m + 1):
                        o = t[:, h * HD:(h + 1) * HD]
                        mm(o, mb[:, h, :], us[:, h * HD:(h + 1) * HD], start=(c == 0), stop=False)
                        ins = mm(o, mk[:, h, :], vt[:, c, h * HD:(h + 1) * HD], start=False,
                                 stop=(c == 0 or h % 2 == 1))
                filled(ins, ("Y", c))

            def rwkv_turn_y(layer, c):
                need(pe, gn_y, layer, c + 1)
                t = acquire(pe, layer, ("yt", c))
                for m in range(2):
                    ins = pe.transpose(t[:, m * P:(m + 1) * P], gy[:, c, m * P:(m + 1) * P], ident[:])
                filled(ins, ("yt", c))

            def s5_input(layer, js):
                for j in js:
                    t = acquire(pe, layer, ("bu", j))
                    if j == 0:
                        need(pe, fm_out, layer, fm_n(4))
                        pe.wait_ge(sw_sem, 16 * (layer + 1))
                    rows = slice(32 * (j % 4), 32 * (j % 4) + 32)
                    for i, w in enumerate((ww("b_re"), ww("b_im"))):
                        ins = mm(t[:, i * T:(i + 1) * T], w[rows, (j // 4) * P:(j // 4 + 1) * P], u5[rows, j // 4, :],
                                 start=True, stop=True)
                    filled(ins, ("bu", j))

            def s5_output(layer, t, js):
                for j in js:
                    if j == 0:
                        need(pe, s5_c, layer, 1)
                    need(pe, s5_h, layer, j + 1)
                    o = t[:, (j // 4) * T:(j // 4 + 1) * T]
                    mm(o, cpad_re[:, j, :], z5[:, j, 0, :], start=(j % 4 == 0), stop=False)
                    ins = mm(o, cpad_im[:, j, :], z5[:, j, 1, :], start=False, stop=(j % 4 == 3))
                    if j == 7:
                        filled(ins, "y5")

            def s5_glu(layer):
                t = acquire(pe, layer, "glu")
                need(pe, s5_g, layer, 1)
                w = v3(ww("glu"), 2)
                for m in range(2):
                    for k in range(2):
                        ins = mm(t[:, m * T:(m + 1) * T], w[:, k, m * P:(m + 1) * P], g5[:, k, :],
                                 start=(k == 0), stop=(k == 1))
                filled(ins, "glu")

            def s5_norm(layer):
                t = acquire(pe, layer, "o5")
                need(pe, s5_sq, layer, 1)
                for k in range(2):
                    ins = mm(t[:, 0:T], ones[:], q5[:, k, :], start=(k == 0), stop=(k == 1))
                filled(ins, "o5")

            def out_projection(layer, ts, group, units):
                need(pe, mix_done, layer, mix_n(group))
                for k in [2 * GROUPS.index(group) + i for i in units]:
                    w = unit(pe, layer, ("wo", k))
                    for q in range(4):
                        ins = mm(ts[q], mixT[:, k, (q // 2) * P:(q // 2 + 1) * P], w[:, (q % 2) * 512:(q % 2) * 512 + 512],
                                 start=(k == WO_ORDER[0]), stop=False)
                    ins.then_inc(wo_used.sem, 1)

            def last_projection(layer, ts):
                need(pe, mix_done, layer, 4)
                ws = [unit(pe, layer, ("wo", k)) for k in WO_ORDER[6:]]
                for q in range(4):
                    for i, k in enumerate(WO_ORDER[6:]):
                        ins = mm(ts[q], mixT[:, k, (q // 2) * P:(q // 2 + 1) * P],
                                 ws[i][:, (q % 2) * 512:(q % 2) * 512 + 512], start=False, stop=(i == 1))
                    filled(ins, ("wo", q))

            def gu_slot(e, q):
                pe.wait_ge(gu_full_s[q % R_GU], 16 * (GU_UNITS // R_GU) * e + 16 * (q // R_GU + 1))
                return guring[:, q % R_GU]

            def d_slot(e, q):
                pe.wait_ge(d_full_s[q % R_D], 16 * (D_UNITS // R_D) * e + 16 * (q // R_D + 1))
                return dring[:, q % R_D]

            def nothing():
                pass

            def ffn(e, src, nb, in_first=nothing, between=nothing, after_first=nothing, before_last=nothing):
                def gate_up(c, qs):
                    for q in qs:
                        u = GUQ * c + q
                        w = gu_slot(e, u)
                        if q == 0 and c:
                            pe.wait_ge(av_ready.sem, av_ready.per * e + c)
                        for b in range(nb):
                            for kk_ in range(GUK):
                                k = q * GUK + kk_
                                ins = mm(ps[:, b, :], src[:, k, b * P:(b + 1) * P], w[:, kk_, :],
                                         start=(k == 0), stop=(k == KT - 1))
                            if q == GUQ - 1:
                                ins.then_inc((gu_done if b == nb - 1 else gu_done0).sem, 1)
                        if q < GUQ - 1:
                            ins.then_inc(gu_used.sem, 1)

                def turn(c):
                    pe.wait_ge(av_ready.sem, av_ready.per * e + c + 1)
                    for b in range(nb):
                        for f in range(2):
                            ins = pe.transpose(ps[:, 2, (2 * b + f) * P:(2 * b + f + 1) * P],
                                               av[:, b, f * P:(f + 1) * P], ident[:])
                    ins.then_inc(t_full.sem, 1)

                def down(c):
                    pe.wait_ge(avT_ready.sem, avT_ready.per * e + c + 1)
                    ws = {}
                    split = nb == 2 and c == NC_ - 1
                    for bs in ((0,), (1,)) if split else (range(nb),):
                        for f in range(2):
                            u = 2 * c + f
                            if f not in ws:
                                ws[f] = d_slot(e, u)
                            for hf in range(2):
                                for b in bs:
                                    ins = mm(ps[:, 4 + 2 * b + hf, :], avT[:, b, f, :],
                                             ws[f][:, hf * 512:(hf + 1) * 512],
                                             start=(c == 0 and f == 0), stop=(c == NC_ - 1 and f == 1))
                                if u == D_UNITS - 1 and bs[-1] == nb - 1:
                                    ins.then_inc(y_done.sem, 1)
                            if u < D_UNITS - 1 and bs[-1] == nb - 1:
                                ins.then_inc(d_used.sem, 1)
                        if split and bs == (0,):
                            ins.then_inc(y_first.sem, 1)

                for c in range(NC_):
                    gate_up(c, range(0, GUQ // 2))
                    if c == 0:
                        in_first()
                    if c == 1:
                        after_first()
                    if c:
                        turn(c - 1)
                    gate_up(c, range(GUQ // 2, GUQ))
                    if c == 0:
                        between()
                    if c:
                        down(c - 1)
                before_last()
                turn(NC_ - 1)
                down(NC_ - 1)

            def router():
                w = v3(ww("router"), KT)
                for tt in range(TT):
                    need(pe, h_evac, 1, 6 + 2 * tt)
                    for k in range(KT):
                        ins = mm(ps[:, 0, tt * NE:(tt + 1) * NE], hT[:, k, tt * P:(tt + 1) * P], w[:, k, :],
                                 start=(k == 0), stop=(k == KT - 1))
                ins.then_inc(router_s.sem, 1)
                pe.wait_ge(router_d.sem, 1)
                sel = rt[:, 0:16]
                mm(ps[:, 1, 0:8], m_lt[:], sel[:, 0:8], start=True, stop=True)
                mm(ps[:, 1, 8:16], ones[:], sel[:, 0:8], start=True, stop=False)
                mm(ps[:, 1, 8:16], m_lt[:], sel[:, 8:16], start=False, stop=True)
                mm(ps[:, 5, 0:8], ones[:], sel[:, 0:8], start=True, stop=False)
                mm(ps[:, 5, 0:8], ones[:], sel[:, 8:16], start=False, stop=True).then_inc(router_s.sem, 1)

            def scatter(ve, qs, banks=(1, 3, 1, 3)):
                for q in qs:
                    if q == 0:
                        pe.wait_ge(ys_ready.sem, 2 * ve + 2)
                        pe.wait_ge(gt_ready.sem, ve + 1)
                    if banks[q] in banks[:q]:
                        pe.wait_ge(x_added.sem, 4 * ve + q - 1)
                    mm(ps[:, banks[q], :], GT[:, q // 2, :], ys[:, (q % 2) * 512:(q % 2) * 512 + 512],
                       start=True, stop=True).then_inc(sc_full.sem, 1)

            def gather(v):
                pe.wait_ge(g_ready.sem, v + 1)
                for r in range(2):
                    for i in range(4):
                        k = 4 * r + i
                        for tt in range(TT):
                            ins = mm(ps[:, 6 + r, i * P:(i + 1) * P], xh[:, tt, k * P:(k + 1) * P], G[:, tt, :],
                                     start=(tt == 0), stop=(tt == TT - 1))
                    ins.then_inc(gat_full.sem, 1)

            def experts(first, ps_no):
                def expert(e, last):
                    ve = e - 1 + ps_no
                    for tt in range(TT):
                        ins = pe.transpose(ps[:, 2, tt * P:(tt + 1) * P], Gg[:, tt, :], ident[:])
                    ins.then_inc(gt_full.sem, 1)
                    pe.wait_ge(xg_ready.sem, 2 * (e - 1) + 2)
                    ffn(e, xgT, 1, in_first=lambda: scatter(ve, (0, 1)), between=lambda: scatter(ve, (2, 3)),
                        after_first=lambda: pe.wait_ge(gt_ready.sem, ve + 2),
                        before_last=lambda: None if last else gather(ve + 1))

                gather(first - 1 + ps_no)
                with pe.Fori(first, first + NE - 1) as e:
                    expert(e, False)
                expert(first + NE - 1, True)
                scatter(first + NE - 1 + ps_no, range(4), LAST_BANKS)

            pe.wait_ge(ident_ready.sem, 1)
            for layer in range(DEPTH):
                norm_transpose(layer, "h", 1)
                fm(layer, 4)
                fm(layer, 0)
                fm(layer, 1)
                s5_input(layer, (0, 1))
                fm(layer, 2)
                s5_input(layer, (2, 3, 4))
                fm(layer, 3)
                s5_input(layer, (5, 6, 7))
                fm(layer, 5)
                lora(layer)
                pe.wait_ge(consts_pool.sem, 1)
                block_sum(layer, "kks", rk_sq, 1, kk2)
                fm(layer, 6)
                block_sum(layer, "bon", rk_bon, 1, kk2)
                fm(layer, 7)
                need(pe, rk_hat, layer, 1)
                transposes(layer, "vt", [pf[:, 4 + m, c * P:(c + 1) * P] for c in range(TT) for m in range(2)])
                transposes(layer, "bkt", [a[:, m, 0:P] for a in (cp, kp) for m in range(2)])
                rwkv_products(layer, 0)
                tm(layer, 0)
                rwkv_x(layer, 0, 0)
                y5_tile = acquire(pe, layer, "y5")
                s5_output(layer, y5_tile, range(0, 4))
                rwkv_x(layer, 0, 1)
                s5_output(layer, y5_tile, range(4, 6))
                rwkv_t(layer, 0, 1)
                s5_output(layer, y5_tile, range(6, 8))
                rwkv_x(layer, 0, 2)
                tm(layer, 1)
                rwkv_t(layer, 0, 2)
                s5_glu(layer)
                rwkv_x(layer, 0, 3)
                tm_dt(layer)
                rwkv_t(layer, 0, 3)
                s5_norm(layer)
                rwkv_x(layer, 0, 4)
                rwkv_t(layer, 0, 4)
                rwkv_x(layer, 0, 5)
                fm(layer, 8)
                rwkv_t(layer, 0, 5)
                rwkv_x(layer, 0, 6)
                ssd_xt(layer)
                rwkv_t(layer, 0, 6)
                att_sums(layer, "qs", 0)
                att_sums(layer, "ks", 2)
                need(pe, rk_tok, layer, 2)
                rwkv_z(layer, 0)
                ssd_scores(layer)
                rwkv_u(layer, 0)
                ssd_decays(layer)
                rwkv_state_y(layer, 0)
                rwkv_products(layer, 1)
                att_scores(layer, 0)
                rwkv_x(layer, 1, 0)
                att_scores(layer, 1)
                rwkv_x(layer, 1, 1)
                rwkv_t(layer, 1, 1)
                ssd_output(layer)
                rwkv_x(layer, 1, 2)
                rwkv_turn_y(layer, 0)
                rwkv_t(layer, 1, 2)
                ts = [acquire(pe, layer, ("wo", q)) for q in range(4)]
                out_projection(layer, ts, "s5", (0,))
                rwkv_x(layer, 1, 3)
                rwkv_t(layer, 1, 3)
                att_turn(layer, "P0", 1, a0, 0)
                out_projection(layer, ts, "s5", (1,))
                rwkv_x(layer, 1, 4)
                token_to_feature(layer, "syt", ssd_n, 1, xs)
                rwkv_t(layer, 1, 4)
                att_turn(layer, "P1", 2, a1, 0)
                rwkv_x(layer, 1, 5)
                att_turn(layer, "P2", 2, a1, P)
                rwkv_t(layer, 1, 5)
                out_projection(layer, ts, "ssd", (0,))
                rwkv_x(layer, 1, 6)
                att_values(layer)
                rwkv_t(layer, 1, 6)
                rwkv_z(layer, 1)
                out_projection(layer, ts, "ssd", (1,))
                rwkv_u(layer, 1)
                token_to_feature(layer, "yat", att_n, 1, ya)
                rwkv_state_y(layer, 1)
                out_projection(layer, ts, "att", (0,))
                rwkv_turn_y(layer, 1)
                out_projection(layer, ts, "att", (1,))
                last_projection(layer, ts)
                norm_transpose(layer, "h2", 2)
                if layer == 0:
                    need(pe, h_evac, 0, 8)
                    ffn(0, hT, 2)
                else:
                    router()
                    experts(1, 0)
                    pe.wait_ge(router_d.sem, 2)
                    over = pe.value_load(ovf[0:1, 0:1])
                    with pe.If(over > 0):
                        experts(1 + NE, 1)

        @block.scalar
        def _(act):
            do = Chain(act, ch_act)
            A = act.activation

            def rsqrt(src, dst, f=None):
                do(A(dst, src, ACT.Ln))
                do(A(dst, dst, ACT.Exp, scale=-0.5), f)

            def norm(layer, n):
                for tt in range(TT):
                    if layer == 0 and n == 1:
                        act.wait_ge(x_in_sem[tt], 16)
                    elif n == 1:
                        need(act, x_ffn, layer - 1, 2 * tt + 2)
                    else:
                        need(act, x_mixed, layer, 2 * tt + 2)
                    i = 2 * (n - 1) + tt + 1
                    do(A(xh[:, tt, :], x[:, tt, :], ACT.Square, accum_out=ssx[:, tt:tt + 1]), sumsq)
                    need(act, rs_in, layer, i)
                    rsqrt(ssx[:, tt:tt + 1], rsx[:, tt:tt + 1], rs_out)

            def evac_fm(layer, q):
                t = has(act, layer, ("fm", q))
                dst = (rk[:, 2 * q:2 * q + 2, 1:1 + T] if q < 4 else u5 if q == 4 else
                       xbc[:, 2 * (q - 5):2 * (q - 5) + 2, CONV - 1:CONV - 1 + T] if q < 7 else
                       qk[:, 2 * (q - 7):2 * (q - 7) + 2, :])
                do(act.copy(dst, v3(t, 2)), fm_out)

            def bank_copy(layer, key, dst, f, n=512, m=None):
                t = has(act, layer, key, 0, n)
                do(act.copy(dst, v3(t, m) if m else t), f)

            def poles_act():
                act.wait_ge(pole_d.sem, 1)
                do(A(S("mag"), S("da"), ACT.Exp), pole_a)
                act.wait_ge(pole_d.sem, 2)
                do(A(S("sin"), S("r"), ACT.Sin))
                do(A(S("cos"), S("r2"), ACT.Sin), pole_a)

            def rwkv_x(layer, c, l):
                t = has(act, layer, ("X", c, l))
                do(act.copy(xs_, v3(t, H)), rk_x)

            LN_EXP = "natural_log_exp_and_others"
            act.preload_act_table_set(LN_EXP)
            act.wait_ge(par_sem, 16)
            do(A(S("dt"), par3("log_dt"), ACT.Exp), pole_a)
            for layer in range(DEPTH):
                act.preload_act_table_set(LN_EXP)
                norm(layer, 1)
                if layer == 0:
                    poles_act()
                for q in FM_ORDER[:5]:
                    evac_fm(layer, q)
                act.preload_act_table_set("sigmoid_and_others")
                need(act, rk_mixed, layer, 1)
                do(A(pf[0:64, 6, :], pf[0:64, 6, :], ACT.Tanh))
                do(A(pf[:, 7, :], pf[:, 7, :], ACT.Sigmoid), lora_in)
                for key, dst, b in (("lw", rw_b, "w0"), ("la", sA, "a0")):
                    t = has(act, layer, key)
                    for m in range(2):
                        do(A(dst[:, m, :], t[:, m * T:(m + 1) * T], ACT.Sigmoid, bias=pp(layer, b, m, 1)),
                           rk_act if m else None)
                bank_copy(layer, "lg", rw_g, rk_act, m=2)
                act.preload_act_table_set(LN_EXP)
                need(act, rk_cs, layer, 1)
                for m in range(2):
                    for c in range(TT):
                        ch = slice(c * P, (c + 1) * P)
                        i = 2 * m + c
                        do(A(eE[:, m, ch], cs[:, m, ch], ACT.Exp, bias=ncm[:, i:i + 1]))
                        do(A(eX[:, m, ch], cp[:, m, ch], ACT.Exp, bias=ncm[:, i:i + 1]))
                        do(A(eM[:, m, ch], cs[:, m, ch], ACT.Exp, scale=-1.0, bias=cs[:, m, c * P + 63:c * P + 64]))
                do(A(dec, dec, ACT.Exp), rk_exp)
                need(act, rk_ss, layer, 1)
                rsqrt(rsq, rsq, rk_rs)
                evac_fm(layer, 5)
                evac_fm(layer, 6)
                evac_fm(layer, 7)
                bank_copy(layer, "vt", vt, rk_tok, m=2)
                bank_copy(layer, "bkt", bkt, rk_tok, m=4)
                bank_copy(layer, "zv0", zv[:, 0, :], zv_out)
                rwkv_x(layer, 0, 1)
                act.preload_act_table_set("gelu_apprx_tanh_and_others")
                need(act, s5_y, layer, 1)
                do(A(g5, y5, ACT.Gelu_apprx_tanh), s5_g)
                act.preload_act_table_set("sigmoid_and_others")
                rwkv_x(layer, 0, 2)
                bank_copy(layer, "zv1", zv[:, 1, :], zv_out)
                t = has(act, layer, "glu")
                for m in range(2):
                    do(A(g5s[:, m, :], t[:, m * T:(m + 1) * T], ACT.Sigmoid, bias=pp(layer, "glu_b", m, 1)),
                       s5_sig if m else None)
                rwkv_x(layer, 0, 3)
                need(act, ssd_cv, layer, 1)
                do(A(xd, zv[:, :, 0:GW], ACT.Sigmoid))
                do(A(sg, cv, ACT.Sigmoid), ssd_sg)
                act.preload_act_table_set(LN_EXP)
                need(act, s5_ss, layer, 1)
                rsqrt(y5[:, 0, :], y5[:, 0, :], s5_rs)
                rwkv_x(layer, 0, 4)
                need(act, dt_a, layer, 1)
                do(A(ael, pp(layer, "a_log"), ACT.Exp))
                do(A(dte, dta, ACT.Exp, scale=-1.0), dt_b)
                rwkv_x(layer, 0, 5)
                need(act, dt_c, layer, 1)
                do(A(dtl, dtu, ACT.Ln), dt_d)
                evac_fm(layer, 8)
                rwkv_x(layer, 0, 6)
                bank_copy(layer, "xt", xs, ssd_xs, m=2)
                bank_copy(layer, ("Z", 0), zs, rk_z, 256)
                bank_copy(layer, ("U", 0), us, rk_u, 256)
                need(act, att_ss, layer, 2)
                rsqrt(sq, sq, att_rs)
                for key, dst in (("dA", L0[:, 0:2, :]), ("dB", L0[:, 2:4, :]), ("d1", L1)):
                    t = has(act, layer, key)
                    do(A(dst, v3(t, 4 if key == "d1" else 2), ACT.Exp), ssd_l)
                need(act, gn_in, layer, 1)
                rsqrt(gst[:, 4:8], gst[:, 4:8], gn_rs)
                rwkv_x(layer, 1, 1)
                need(act, att_m, layer, 1)
                do(A(a0, a0, ACT.Exp), att_e)
                rwkv_x(layer, 1, 2)
                need(act, att_m, layer, 2)
                do(A(a1, a1, ACT.Exp), att_e)
                rwkv_x(layer, 1, 3)
                need(act, ssd_y, layer, 1)
                for tt in range(TT):
                    do(A(xd[:, tt, :], xs[:, tt, :], ACT.Square, accum_out=ssy[:, tt:tt + 1]), ssd_ss if tt else None)
                need(act, ssd_v, layer, 1)
                rsqrt(ssy, ssy, ssd_rs)
                bank_copy(layer, "P0", pt0, att_pt, m=4)
                rwkv_x(layer, 1, 4)
                rwkv_x(layer, 1, 5)
                bank_copy(layer, "P1", pt1, att_pt, m=4)
                bank_copy(layer, "P2", pt2, att_pt, m=4)
                rwkv_x(layer, 1, 6)
                t = has(act, layer, "ya")
                for tt in range(TT):
                    do(A(sq[:, tt, :], t[:, tt * T:(tt + 1) * T], ACT.Square, accum_out=ssa[:, tt:tt + 1]),
                       att_y if tt else None)
                need(act, att_v, layer, 1)
                rsqrt(ssa, ssa, att_rs2)
                bank_copy(layer, ("Z", 1), zs, rk_z, 256)
                bank_copy(layer, ("U", 1), us, rk_u, 256)
                need(act, gn_in, layer, 2)
                rsqrt(gst[:, 4:8], gst[:, 4:8], gn_rs)
                norm(layer, 2)

                def ffn(e, nb):
                    for c in range(NC_ + 1):
                        if c:
                            act.wait_ge(t_full.sem, NC_ * e + c)
                            act.copy(avT[:, 0:nb], ps[:, 2, 0:nb * 256].rearrange("p (b f s) -> p b f s", b=nb, f=2)) \
                                .then_inc(avT_ready.sem, 1)
                        if c < NC_:
                            for b in range(nb):
                                act.wait_ge((gu_done if b == nb - 1 else gu_done0).sem, NC_ * e + c + 1)
                                ins = A(sil[:, b, :], ps[:, b, 0:FC], ACT.Silu)
                            ins.then_inc(sil_ready.sem, 1)

                if layer == 0:
                    ffn(0, 2)
                    continue
                act.wait_ge(router_m.sem, 1)
                do(A(rl, rl, ACT.Exp), router_a)

                def experts(first, ps_no):
                    with act.Fori(first, first + NE) as e:
                        ffn(e, 1)
                        act.wait_ge(y_done.sem, 2 * e + 2)
                        for hf in range(2):
                            act.copy(ys[:, hf * 512:(hf + 1) * 512], ps[:, 4 + hf, :]).then_inc(ys_ready.sem, 1)

                experts(1, 0)
                act.wait_ge(router_d.sem, 2)
                over = act.value_load(ovf[0:1, 0:1])
                with act.If(over > 0):
                    experts(1 + NE, 1)

        @block.gpsimd
        def _(pool):
            do = Chain(pool, ch_pool)

            def fill_mask(dst, base, mult, pattern, op):
                do(pool.memset(dst, 1.0))
                do(pool.affine_select(out=dst, in_=dst, compare_op=op, fill=0.0, base=base,
                                      pattern=pattern, channel_multiplier=mult))

            do(pool.memset(ident[:], 0.0))
            do(pool.affine_select(out=ident[:], in_=ident[:], compare_op=ALU.not_equal, fill=1.0, base=0,
                                  pattern=[[-1, P]], channel_multiplier=1), ident_ready)
            do(pool.memset(ones[:], 1.0))
            do(pool.memset(blk[:], 0.0))
            do(pool.memset(blk[0:64, 0:64], 1.0))
            do(pool.memset(blk[64:128, 64:128], 1.0))
            fill_mask(m_gt[:], 0, 1, [[-1, P]], ALU.is_gt)
            fill_mask(m_lt[:], 0, -1, [[1, P]], ALU.is_gt)
            fill_mask(m_leo[:], 0, -1, [[1, T]], ALU.is_ge)
            do(pool.memset(tie[:], 1.0))
            do(pool.affine_select(out=tie[:], in_=tie[:], compare_op=ALU.is_gt, fill=0.0, base=0,
                                  pattern=[[1, NE], [-1, NE]], channel_multiplier=0))
            do(pool.iota(iota[:], pattern=[[1, P]], base=0, channel_multiplier=0, allow_small_or_imprecise_dtypes=True))
            do(pool.iota(it_x[:], pattern=[[1, P]], base=0, channel_multiplier=0))
            do(pool.iota(it_y[:], pattern=[[0, P]], base=0, channel_multiplier=1))
            do(pool.iota(it_d[:, 0:P], pattern=[[-1, P]], base=0, channel_multiplier=1))
            do(pool.iota(it_d[:, P:384], pattern=[[-1, T]], base=P, channel_multiplier=1), consts_pool)

            def c_clear(layer):
                need(pool, h_evac, layer, 4)
                do(pool.memset(cpad_re, 0.0))
                do(pool.memset(cpad_im, 0.0))

            def c_rows(layer):
                pool.wait_ge(sw_sem, 16 * (layer + 1))
                fr = bc(s5p[:, layer, 3, :], [P, 8, 16], 2)
                fi = bc(s5p[:, layer, 4, :], [P, 8, 16], 2)
                cr, ci = (v3(ww(n), 8) for n in ("c_re", "c_im"))
                o_re, o_im, tmp = (v3(c5[:, i, :], 8) for i in range(3))
                do(pool.tensor_tensor(o_re, cr, fr, ALU.mult))
                do(pool.tensor_tensor(tmp, ci, fi, ALU.mult))
                do(pool.tensor_tensor(o_re, o_re, tmp, ALU.subtract))
                do(pool.tensor_tensor(o_im, cr, fi, ALU.mult))
                do(pool.tensor_tensor(tmp, ci, fr, ALU.mult))
                do(pool.tensor_tensor(o_im, o_im, tmp, ALU.add))
                do(pool.tensor_scalar(o_im, o_im, -1.0, None, ALU.mult))
                for i, src in enumerate((o_re, o_im)):
                    for a in range(2):
                        for g in range(2):
                            rows = slice(64 * g, 64 * g + 64)
                            at0 = 1024 * i + 512 * a + 16 * g
                            dst = arena[rows, MIX_AT + at0:MIX_AT + at0 + 4 * (P + 32)] \
                                .rearrange("p (q s) -> p q s", q=4)[:, :, 0:16]
                            do(pool.tensor_copy(dst, src[rows, 4 * a:4 * a + 4, :]), s5_c if i + a + g == 3 else None)

            def masked_level(layer, c, l):
                if l == 0:
                    need(pool, rk_mat, layer, 4 * c + 2)
                    if c:
                        need(pool, rk_x, layer, 6)
                elif l == 2:
                    need(pool, rk_tt, layer, 7 * c + 1)
                elif l > 2:
                    need(pool, rk_x, layer, 6 * c + l - 2)
                do(pool.tensor_tensor(noff[:, l % 2], nm, bc(lvl[:, l, :], [P, H, P], 1), ALU.mult), rk_off)

            for layer in range(DEPTH):
                if layer == 0:
                    c_clear(layer)
                    pool.wait_ge(poles.sem, 1)
                    rotation_tables(do, pool, layer, 4, 4, tab_tmp, pw)
                else:
                    need(pool, s5_back, layer - 1, 8)
                    rotation_tables(do, pool, layer, 0, 4, tab_tmp, pw)
                    rotation_tables(do, pool, layer, 4, 4, tab_tmp, pw)
                do(pool.memset(tab_tmp[:, 0:1], 0.0), tab)
                if layer:
                    c_clear(layer)
                    c_rows(layer)
                for j in range(8):
                    need(pool, s5_in, layer, j + 1)
                    b = j % 2
                    do(pool.tensor_tensor(z5[:, j, 0, :], p5[:, b, 0, 0, :], p5[:, b, 1, 1, :], ALU.add))
                    do(pool.tensor_tensor(z5[:, j, 1, :], p5[:, b, 0, 1, :], p5[:, b, 1, 0, :], ALU.subtract), s5_z)
                if layer == 0:
                    c_rows(layer)
                for j in range(8):
                    need(pool, s5_back, layer, j + 1)
                    b = j % 2
                    do(pool.tensor_tensor(z5[:, j, 0, :], p5[:, b, 0, 0, :], p5[:, b, 1, 1, :], ALU.subtract))
                    do(pool.tensor_tensor(z5[:, j, 1, :], p5[:, b, 1, 0, :], p5[:, b, 0, 1, :], ALU.add), s5_h)
                    if j == 1:
                        pool.wait_ge(consts_dve.sem, 1)
                        masked_level(layer, 0, 0)
                        masked_level(layer, 0, 1)
                for l in range(2, 7):
                    masked_level(layer, 0, l)
                need(pool, ssd_a, layer, 1)
                for h0 in (0, 2):
                    do(pool.tensor_tensor(r0[:, h0:h0 + 2, :], bc(m_leo[:], [P, 2, T], 1),
                                          bc(sa[:, h0:h0 + 2], [P, 2, T], 2), ALU.mult))
                do(pool.tensor_tensor(r1, bc(m_le, [P, H, P], 1), bc(sa[:, 4:8], [P, H, P], 2), ALU.mult), ssd_r)
                for l in range(7):
                    masked_level(layer, 1, l)

        @block.vector
        def _(dve):
            do = Chain(dve, ch_dve)
            tt_op, ts, stt = dve.tensor_tensor, dve.tensor_scalar, dve.scalar_tensor_tensor

            def level_masks():
                dve.wait_ge(consts_pool.sem, 1)
                do(tt_op(it_x[:], it_x[:], it_y[:], ALU.bitwise_xor))
                for l in range(7):
                    do(ts(it_y[:], it_x[:], l, None, ALU.logical_shift_right))
                    do(stt(lvl[:, l, :], it_y[:], 1.0, m_gt[:], ALU.is_equal, ALU.mult),
                       consts_dve if l == 6 else None)

            def distance_masks(tt):
                cnt, bias, d = ((cnt0, bias0, it_d[:, 0:P]), (cnt1, bias1, it_d[:, P:384]))[tt]
                n = d.shape[1]
                c = cnt[:]
                dist, w = flat(gy)[:, 0:n], flat(s0)[:, 0:n]
                wi = flat(gy)[:, 256:256 + n].bitcast(I32)
                do(dve.tensor_copy(dist, d))
                do(dve.memset(c, 0.0))
                for window, dil in PATTERNS:
                    do(ts(wi, d, dil - 1, None, ALU.bitwise_and))
                    do(ts(w, wi, 0.0, None, ALU.is_equal))
                    do(stt(w, dist, float(window), w, ALU.is_le, ALU.mult))
                    do(tt_op(c, c, w, ALU.add))
                do(stt(c, dist, 0.0, c, ALU.is_ge, ALU.mult))
                do(ts(w, c, 0.0, -1e30, ALU.is_equal, ALU.mult))
                for h in range(H):
                    do(stt(bias[:, h, :], dist, -LOG2E_SLOPES[h], w, ALU.mult, ALU.add))

            def pole_angles():
                inv, magic = 1.0 / (2 * np.pi), 12582912.0
                c1 = 6.28125
                c2 = float(np.float32(np.float16(2 * np.pi - c1)))
                c3 = float(np.float32(2 * np.pi - c1 - c2))
                dve.wait_ge(pole_a.sem, 1)
                are, aim = par3("a_re"), par3("a_im")
                do(tt_op(S("da"), S("dt"), are, ALU.mult), pole_d)
                do(tt_op(S("r"), S("dt"), aim, ALU.mult))
                do(ts(S("k"), S("r"), inv, magic, ALU.mult, ALU.add))
                do(ts(S("k"), S("k"), -magic, None, ALU.add))
                for c_ in (c1, c2, c3):
                    do(stt(S("r"), S("k"), -c_, S("r"), ALU.mult, ALU.add))
                pi = float(np.nextafter(np.float32(np.pi), np.float32(0)))
                do(ts(S("r"), S("r"), pi, -pi, ALU.min, ALU.max))
                do(ts(S("r2"), S("r"), float(np.pi / 2), None, ALU.add))
                do(ts(S("k"), S("r2"), pi, None, ALU.is_gt))
                do(stt(S("r2"), S("k"), float(-2 * np.pi), S("r2"), ALU.mult, ALU.add))
                do(ts(S("r2"), S("r2"), pi, -pi, ALU.min, ALU.max), pole_d)

            def pole_factors():
                are, aim = par3("a_re"), par3("a_im")
                dve.wait_ge(pole_a.sem, 3)
                do(dve.tensor_copy(s5p[:, :, 0, :], S("cos")))
                do(dve.tensor_copy(s5p[:, :, 1, :], S("sin")))
                do(dve.tensor_copy(s5p[:, :, 2, :], S("mag")))
                do(tt_op(S("cos"), S("cos"), S("mag"), ALU.mult))
                do(tt_op(S("sin"), S("sin"), S("mag"), ALU.mult))
                do(ts(S("cos"), S("cos"), -1.0, None, ALU.add))
                do(tt_op(S("k"), are, are, ALU.mult))
                do(tt_op(S("r"), aim, aim, ALU.mult))
                do(tt_op(S("k"), S("k"), S("r"), ALU.add))
                do(dve.reciprocal(S("k"), S("k")))
                do(tt_op(S("r"), S("cos"), are, ALU.mult))
                do(tt_op(S("r2"), S("sin"), aim, ALU.mult))
                do(tt_op(S("r"), S("r"), S("r2"), ALU.add))
                do(tt_op(s5p[:, :, 3, :], S("r"), S("k"), ALU.mult))
                do(tt_op(S("r"), S("sin"), are, ALU.mult))
                do(tt_op(S("r2"), S("cos"), aim, ALU.mult))
                do(tt_op(S("r"), S("r"), S("r2"), ALU.subtract))
                do(tt_op(s5p[:, :, 4, :], S("r"), S("k"), ALU.mult), poles)

            def norm(layer, n, add=None):
                def mean_square(tt):
                    need(dve, sumsq, layer, 2 * (n - 1) + tt + 1)
                    do(ts(ssx[:, tt:tt + 1], ssx[:, tt:tt + 1], 1.0 / D, EPS, ALU.mult, ALU.add), rs_in)

                def scale(tt):
                    need(dve, rs_out, layer, 2 * (n - 1) + tt + 1)
                    do(ts(xh[:, tt, :], x[:, tt, :], rsx[:, tt:tt + 1], None, ALU.mult), xh_ready)

                if add:
                    for q in range(3):
                        add(q)
                mean_square(0)
                if add:
                    add(3)
                scale(0)
                mean_square(1)
                scale(1)
                g = pp(layer, "ln_mix" if n == 1 else "ln_ffn")
                for q in range(4):
                    t = has(dve, layer, ("h" if n == 1 else "h2", q))
                    k = 4 * (q % 2)
                    do(tt_op(hT[:, k:k + 4, (q // 2) * P:(q // 2 + 1) * P], v3(t, 4),
                             bc(g[:, k:k + 4], [P, 4, P], 2), ALU.mult), h_evac)

            def rwkv_mix(layer, q):
                need(dve, fm_out, layer, fm_n(q))
                m = slice(2 * q, 2 * q + 2)
                do(tt_op(pf[:, m, :], rk[:, m, 0:T], rk[:, m, 1:1 + T], ALU.subtract))
                for i in (2 * q, 2 * q + 1):
                    do(stt(pf[:, i, :], pf[:, i, :], pp(layer, "mu", i, 1), rk[:, i, 1:1 + T], ALU.mult, ALU.add),
                       rk_mixed if i == 7 else None)

            def conv(layer, ms):
                need(dve, fm_out, layer, fm_n(6))
                for m in ms:
                    w = [pp(layer, "conv_w", 4 * m + i, 1) for i in range(CONV)]
                    do(ts(cv[:, m, :], xbc[:, m, 0:T], w[0], pp(layer, "conv_b", m, 1), ALU.mult, ALU.add))
                    for i in range(1, CONV):
                        do(stt(cv[:, m, :], xbc[:, m, i:i + T], w[i], cv[:, m, :], ALU.mult, ALU.add),
                           ssd_cv if (m, i) == (3, CONV - 1) else None)

            def rwkv_decay(layer):
                need(dve, rk_act, layer, 1)
                do(ts(rw_b, rw_b, -DECAY, None, ALU.mult))
                for m in range(2):
                    for c in range(TT):
                        ch = slice(c * P, (c + 1) * P)
                        do(dve.tensor_tensor_scan(cs[:, m, ch], ones[:], rw_b[:, m, ch], 0.0, ALU.mult, ALU.add))
                do(tt_op(cp, cs, rw_b, ALU.subtract))
                do(ts(ncm.rearrange("p (m c) -> p m c", m=2), cs[:, :, 63:T:P], -1.0, None, ALU.mult))
                d3 = dec.rearrange("p (m c) -> p m c", c=1)
                do(tt_op(d3, cs[:, :, P - 1:P], cs[:, :, 63:64], ALU.subtract))
                do(tt_op(d3, d3, cs[:, :, P + 63:P + 64], ALU.add), rk_cs)

            def rwkv_keys(layer):
                need(dve, rk_act, layer, 2)
                for m in range(2):
                    do(ts(kp[:, m, :], sA[:, m, :], 1.0, pp(layer, "k_a", m, 1), ALU.subtract, ALU.mult))
                do(stt(kp, kp, 1.0, pf[:, 2:4, :], ALU.add, ALU.mult))
                t = has(dve, layer, "kks")
                do(ts(rsq, v3(t, 2), 1e-12, None, ALU.add), rk_ss)
                for m in range(2):
                    do(stt(kk2[:, m, :], pf[:, m, :], pp(layer, "r_k", m, 1), kp[:, m, :], ALU.mult, ALU.mult),
                       rk_bon if m else None)

            def rwkv_hats(layer):
                need(dve, rk_rs, layer, 1)
                do(tt_op(kk, kk, rsq, ALU.mult))
                do(stt(eX, kk, -1.0, eX, ALU.mult, ALU.mult))
                do(tt_op(cp, kk, sA, ALU.mult))
                do(tt_op(cp, cp, eM, ALU.mult))
                do(tt_op(kp, kp, eM, ALU.mult))
                t = has(dve, layer, "bon")
                do(tt_op(rw_b, v3(t, 2), pf[:, 4:6, :], ALU.mult), rk_bonus)
                do(tt_op(eE, eE, pf[:, 0:2, :], ALU.mult), rk_hat)

            def dt_first(layer):
                t = has(dve, layer, "dt", 0, 2 * H)
                do(tt_op(dtr3, v3(t, 2), bc(pp(layer, "dt_bias"), [P, 2, H], 1), ALU.add), dt_out)
                do(stt(dta, dtr, -1.0, dtr, ALU.mult, ALU.max), dt_a)

            def dt_rest(layer):
                need(dve, dt_b, layer, 1)
                do(ts(dtu, dte, 1.0, None, ALU.add), dt_c)
                do(stt(dta, dtu, -1.0, dte, ALU.add, ALU.subtract))
                do(dve.reciprocal(dte, dtu))
                do(tt_op(dta, dta, dte, ALU.mult))
                need(dve, dt_d, layer, 1)
                do(tt_op(dtl, dtl, dta, ALU.subtract))
                do(stt(dtr, dtr, 0.0, dtl, ALU.max, ALU.add))
                do(stt(sa.rearrange("p (a h) -> p a h", a=2), dtr3, -1.0, bc(ael, [P, 2, H], 1), ALU.mult, ALU.mult),
                   ssd_a)

            def heads(a):
                return a.rearrange("p a (h e) -> p (a h) e", h=H)

            def ssd_x(layer):
                need(dve, ssd_xs, layer, 1)
                do(tt_op(heads(xd), heads(xs), bc(dtr, [P, 2 * H, HD], 2), ALU.mult))

            def ssd_scores(layer):
                for g in range(2):
                    t = has(dve, layer, f"sc{g}")
                    do(tt_op(sc0[:, g, :], t[:, 0:T], m_leo[:], ALU.mult))
                    do(tt_op(sc1[:, g, :], t[:, T:T + P], m_le, ALU.mult), ssd_sc)

            def ssd_weights(layer):
                need(dve, ssd_l, layer, 3)
                for g in range(2):
                    do(tt_op(L0[:, 2 * g:2 * g + 2, :], L0[:, 2 * g:2 * g + 2, :], bc(sc0[:, g, :], [P, 2, T], 1),
                             ALU.mult))
                    do(tt_op(L1[:, 2 * g:2 * g + 2, :], L1[:, 2 * g:2 * g + 2, :], bc(sc1[:, g, :], [P, 2, P], 1),
                             ALU.mult), ssd_p if g else None)

            def ssd_gate(layer):
                for tt in range(TT):
                    a = xs[:, tt, :].rearrange("p (h e) -> p h e", h=H)
                    do(tt_op(a, a, bc(pp(layer, "ssd_d"), [P, H, HD], 2), ALU.mult))
                t = has(dve, layer, "sy")
                do(tt_op(xs, v3(t, 2), xs, ALU.add))
                do(tt_op(xs, xs, zv[:, :, 0:GW], ALU.mult), ssd_y)

            def ssd_norm(layer):
                need(dve, ssd_ss, layer, 1)
                do(ts(ssy, ssy, 1.0 / GW, EPS, ALU.mult, ALU.add), ssd_v)
                need(dve, ssd_rs, layer, 1)
                for tt in range(TT):
                    do(ts(xs[:, tt, :], xs[:, tt, :], ssy[:, tt:tt + 1], None, ALU.mult), ssd_n if tt else None)

            def to_mix(layer, key, m, gain):
                t = has(dve, layer, key)
                do(tt_op(mixT[:, m:m + 2, :], v3(t, 2), bc(pp(layer, gain), [P, 2, T], 2), ALU.mult), mix_done)

            def rwkv_matrices(layer, c):
                if c:
                    need(dve, rk_off, layer, 7)
                for q, key in enumerate(PRODUCT_TILES):
                    t = has(dve, layer, (key, c))
                    for i, (dst, mask) in enumerate((((nm, m_gt[:]), (m2, m_lt[:])), ((mb, m_le), (mk, m_le)))[q // 2]):
                        do(tt_op(dst[:, q % 2::2, :], v3(t[:, i * T:(i + 1) * T], 2), bc(mask, [P, 2, P], 1), ALU.mult),
                           rk_mat if i else None)

            def rwkv_level(layer, c, l):
                idb = bc(ident[:], [P, H, P], 1)
                if l == 0:
                    need(dve, rk_off, layer, 7 * c + 1)
                    do(tt_op(tm_, noff[:, 0], idb, ALU.add), rk_t)
                    t = has(dve, layer, ("X", c, 0))
                    do(tt_op(tt_, v3(t, H), idb, ALU.add), rk_tt)
                    return
                t = has(dve, layer, ("TT", c, l))
                do(tt_op(tt_, v3(t, H), tt_, ALU.add), rk_tt)
                if l < 6:
                    t = has(dve, layer, ("T", c, l))
                    do(tt_op(tm_, v3(t, H), tm_, ALU.add), rk_t)

            def group_centre(layer, c):
                t = has(dve, layer, ("Y", c), 0, GW)
                y3 = t.rearrange("p (h e) -> p h e", h=H)
                g3 = gy[:, c, :].rearrange("p (h e) -> p h e", h=H)
                mean = gst[:, 0:4]
                do(dve.tensor_reduce(mean, y3, AX.X, ALU.add))
                do(ts(mean, mean, 1.0 / HD, None, ALU.mult))
                do(tt_op(g3, y3, bc(mean, [P, H, HD], 2), ALU.subtract), gn_x)

            def group_variance(layer, c):
                g3 = gy[:, c, :].rearrange("p (h e) -> p h e", h=H)
                k3 = gsq.rearrange("p (h e) -> p h e", h=H)
                var = gst[:, 4:8]
                do(tt_op(k3, g3, g3, ALU.mult))
                do(dve.tensor_reduce(var, k3, AX.X, ALU.add))
                do(ts(var, var, 1.0 / HD, GN_EPS, ALU.mult, ALU.add), gn_in)

            def group_scale(layer, c):
                g3 = gy[:, c, :].rearrange("p (h e) -> p h e", h=H)
                var = gst[:, 4:8]
                need(dve, gn_rs, layer, c + 1)
                do(tt_op(g3, g3, bc(var, [P, H, HD], 2), ALU.mult), gn_y)

            def rwkv_out(layer, c):
                t = has(dve, layer, ("yt", c), 0, 256)
                ch = slice(c * P, (c + 1) * P)
                for m in range(2):
                    do(ts(mixT[:, 4 + m, ch], t[:, m * P:(m + 1) * P], pp(layer, "ln_w", m, 1),
                          pp(layer, "ln_b", m, 1), ALU.mult, ALU.add), rk_yt if m else None)
                o = mixT[:, 4:6, ch]
                do(tt_op(o, o, rw_b[:, :, ch], ALU.add))
                do(tt_op(o, o, rw_g[:, :, ch], ALU.mult), mix_done if c else None)

            def att_squares(layer):
                need(dve, fm_out, layer, 9)
                do(tt_op(sq, qk, qk, ALU.mult), att_sq)

            def att_sums(layer):
                for key, i in (("qs", 0), ("ks", 2)):
                    t = has(dve, layer, key)
                    do(ts(sq[:, i:i + 2, :], v3(t, 2), 1.0 / HD, EPS, ALU.mult, ALU.add), att_ss)

            def att_norm(layer):
                need(dve, att_rs, layer, 1)
                do(stt(qk[:, 0:2, :], qk[:, 0:2, :], pp(layer, "q_gain"), sq[:, 0:2, :], ALU.mult, ALU.mult))
                do(stt(qk[:, 2:4, :], qk[:, 2:4, :], pp(layer, "k_gain"), sq[:, 2:4, :], ALU.mult, ALU.mult), att_qk)

            def att_scores(layer, tt):
                a, bias = ((a0, bias0), (a1, bias1))[tt]
                n = P * (tt + 1)
                for key, _, hs in ATT_TILES[2 * tt:2 * tt + 2]:
                    t = has(dve, layer, key, 0, 2 * n)
                    do(stt(a[:, hs[0]::2, :], v3(t, 2), HD ** -0.5, bias[:, hs[0]::2, :], ALU.mult, ALU.add), att_s)

            def att_maximum(layer, tt):
                a = (a0, a1)[tt]
                n = P * (tt + 1)
                mx = amx[:, tt * H:(tt + 1) * H]
                do(dve.tensor_reduce(mx, a, AX.X, ALU.max))
                do(tt_op(a, a, bc(mx, [P, H, n], 2), ALU.subtract), att_m)

            def att_softmax(layer, tt):
                a, cnt = ((a0, cnt0), (a1, cnt1))[tt]
                n = P * (tt + 1)
                mx = amx[:, tt * H:(tt + 1) * H]
                need(dve, att_e, layer, tt + 1)
                do(tt_op(a, a, bc(cnt[:], [P, H, n], 1), ALU.mult))
                do(dve.tensor_reduce(mx, a, AX.X, ALU.add))
                do(dve.reciprocal(mx, mx))
                do(tt_op(a, a, bc(mx, [P, H, n], 2), ALU.mult), att_p)

            def att_out(layer):
                need(dve, att_y, layer, 1)
                do(ts(ssa, ssa, 1.0 / GW, EPS, ALU.mult, ALU.add), att_v)
                need(dve, att_rs2, layer, 1)
                t = has(dve, layer, "ya")
                for tt in range(TT):
                    do(ts(ya[:, tt, :], t[:, tt * T:(tt + 1) * T], ssa[:, tt:tt + 1], None, ALU.mult),
                       att_n if tt else None)

            def s5_products(j, src, f):
                b = j % 2
                do(tt_op(p5[:, b, 0], src, bc(e_re[:, j, :], [P, 2, T], 1), ALU.mult))
                do(tt_op(p5[:, b, 1], src, bc(e_im[:, j, :], [P, 2, T], 1), ALU.mult), f)

            def s5_input(layer, js):
                for j in js:
                    if j == (0 if layer else 4):
                        dve.wait_ge(tab.sem, layer + 1)
                    t = has(dve, layer, ("bu", j))
                    if j >= 2:
                        need(dve, s5_z, layer, j - 1)
                    s5_products(j, v3(t, 2), s5_in)

            def s5_scan(layer, js):
                for j in js:
                    need(dve, s5_z, layer, j + 1)
                    for i in range(2):
                        z = z5[:, j, i, :]
                        do(dve.tensor_tensor_scan(z, s5p[:, layer, 2, j:j + 1].to_broadcast([P, T]), z, 0.0,
                                                  ALU.mult, ALU.add))

            def s5_rotate_back(layer, js):
                for j in js:
                    if j == 0:
                        need(dve, s5_z, layer, 8)
                    if j >= 2:
                        need(dve, s5_h, layer, j - 1)
                    s5_products(j, z5[:, j], s5_back)

            def s5_skip(layer):
                t = has(dve, layer, "y5")
                for m in range(2):
                    do(stt(y5[:, m, :], u5[:, m, :], pp(layer, "s5_d", m, 1), t[:, m * T:(m + 1) * T],
                           ALU.mult, ALU.add), s5_y if m else None)

            def s5_gate(layer):
                need(dve, s5_sig, layer, 1)
                do(tt_op(g5, g5, g5s, ALU.mult))
                do(tt_op(q5, g5, g5, ALU.mult), s5_sq)

            def s5_sums(layer):
                t = has(dve, layer, "o5", 0, 256)
                do(ts(y5[:, 0, :], t, 1.0 / GW, EPS, ALU.mult, ALU.add), s5_ss)

            def s5_out(layer):
                need(dve, s5_rs, layer, 1)
                for m in range(2):
                    do(stt(mixT[:, 6 + m, :], g5[:, m, :], pp(layer, "s5_out", m, 1), y5[:, 0, :],
                           ALU.mult, ALU.mult), mix_done if m else None)

            def residual(q):
                return x[:, q // 2, (q % 2) * 512:(q % 2) * 512 + 512]

            def ffn(e, nb):
                for c in range(NC_):
                    dve.wait_ge(sil_ready.sem, NC_ * e + c + 1)
                    for b in range(nb):
                        ins = tt_op(av[:, b, :], sil[:, b, :], ps[:, b, FC:2 * FC], ALU.mult)
                    ins.then_inc(av_ready.sem, 1)
                    yield c

            dve.wait_ge(par_sem, 16)
            do(dve.memset(ovf[:], 0))
            pole_angles()
            def add_dense(q):
                if q % 2 == 0:
                    dve.wait_ge(y_done.sem if q else y_first.sem, 2 if q else 1)
                do(tt_op(residual(q), residual(q), ps[:, 4 + q, :], ALU.add), x_ffn)

            for layer in range(DEPTH):
                norm(layer, 1, add_dense if layer else None)
                if layer == 0:
                    pole_factors()
                    rotation_tables(do, dve, 0, 0, 4, tab_tmp_v, pw_v)
                    level_masks()
                do(dve.memset(rk[:, :, 0:1], 0.0))
                do(dve.memset(xbc[:, :, 0:CONV - 1], 0.0))
                rwkv_mix(layer, 0)
                rwkv_mix(layer, 1)
                s5_input(layer, (0, 1))
                rwkv_mix(layer, 2)
                s5_input(layer, (2, 3, 4))
                rwkv_mix(layer, 3)
                for m in range(2):
                    do(ts(kk[:, m, :], pf[:, 2 + m, :], pp(layer, "k_k", m, 1), None, ALU.mult))
                do(tt_op(kk2, kk, kk, ALU.mult), rk_sq)
                s5_input(layer, (5, 6, 7))
                rwkv_decay(layer)
                rwkv_keys(layer)
                s5_scan(layer, range(0, 4))
                need(dve, rk_exp, layer, 1)
                rwkv_hats(layer)
                s5_scan(layer, range(4, 8))
                s5_rotate_back(layer, range(0, 2))
                rwkv_matrices(layer, 0)
                s5_rotate_back(layer, range(2, 4))
                rwkv_level(layer, 0, 0)
                s5_rotate_back(layer, range(4, 8))
                rwkv_level(layer, 0, 1)
                s5_skip(layer)
                conv(layer, (0, 1))
                if layer == 0:
                    distance_masks(0)
                rwkv_level(layer, 0, 2)
                conv(layer, (2, 3))
                s5_gate(layer)
                rwkv_level(layer, 0, 3)
                s5_sums(layer)
                dt_first(layer)
                rwkv_level(layer, 0, 4)
                need(dve, ssd_sg, layer, 1)
                do(tt_op(cv, cv, sg, ALU.mult), ssd_xbc)
                s5_out(layer)
                do(tt_op(zv[:, :, 0:GW], zv[:, :, 0:GW], xd, ALU.mult))
                if layer == 0:
                    distance_masks(1)
                rwkv_level(layer, 0, 5)
                dt_rest(layer)
                att_squares(layer)
                rwkv_level(layer, 0, 6)
                ssd_x(layer)
                att_sums(layer)
                ssd_scores(layer)
                t = has(dve, layer, "S", 0, 256)
                for m in range(2):
                    do(stt(s0[:, m, :], t[:, m * P:(m + 1) * P], dec[:, m:m + 1], blk[:], ALU.mult, ALU.mult),
                       rk_s if m else None)
                att_norm(layer)
                rwkv_matrices(layer, 1)
                group_centre(layer, 0)
                rwkv_level(layer, 1, 0)
                group_variance(layer, 0)
                ssd_weights(layer)
                att_scores(layer, 0)
                att_maximum(layer, 0)
                rwkv_level(layer, 1, 1)
                group_scale(layer, 0)
                att_scores(layer, 1)
                ssd_gate(layer)
                att_maximum(layer, 1)
                rwkv_level(layer, 1, 2)
                rwkv_out(layer, 0)
                att_softmax(layer, 0)
                rwkv_level(layer, 1, 3)
                ssd_norm(layer)
                att_softmax(layer, 1)
                to_mix(layer, "syt", 0, "ssd_norm")
                rwkv_level(layer, 1, 4)
                rwkv_level(layer, 1, 5)
                rwkv_level(layer, 1, 6)
                att_out(layer)
                to_mix(layer, "yat", 2, "att_out")
                group_centre(layer, 1)
                group_variance(layer, 1)
                group_scale(layer, 1)
                rwkv_out(layer, 1)

                def add_mixed(q):
                    t = has(dve, layer, ("wo", q))
                    do(tt_op(residual(q), residual(q), t, ALU.add), x_mixed)

                norm(layer, 2, add_mixed)
                if layer == 0:
                    for c in ffn(0, 2):
                        pass

            do(dve.memset(rtab, 0.0))
            lg3 = rlg.rearrange("p (a e) -> p a e", a=2)
            g4, q4 = (rt[:, o:o + 128].rearrange("p (a e j) -> p a e j", a=2, e=NE) for o in (256, 384))
            le = lg3.unsqueeze(3).to_broadcast([P, 2, NE, NE])
            lj = lg3.unsqueeze(2).to_broadcast([P, 2, NE, NE])
            sel = rt[:, 0:16]
            sel3, rl3 = (a.rearrange("p (a e) -> p a e", a=2) for a in (sel, rl))
            dve.wait_ge(router_s.sem, 1)
            do(tt_op(lg3, v3(ps[:, 0, 0:16], 2), bc(pp(1, "router_b"), [P, 2, NE], 1), ALU.add))
            do(tt_op(q4, lj, le, ALU.is_equal))
            do(tt_op(q4, q4, bc(tie[:], [P, 2, NE, NE], 1), ALU.mult))
            do(tt_op(g4, lj, le, ALU.is_gt))
            do(tt_op(g4, g4, q4, ALU.add))
            do(dve.tensor_reduce(rrk.rearrange("p (a e) -> p a e", a=2), g4, AX.X, ALU.add))
            do(ts(sel, rrk, float(2), None, ALU.is_lt), router_d)
            do(dve.tensor_reduce(rmx, lg3, AX.X, ALU.max))
            do(tt_op(rl3, lg3, bc(rmx, [P, 2, NE], 2), ALU.subtract), router_m)
            do(dve.tensor_copy(rsel[:, :, 0:NE], sel3))
            dve.wait_ge(router_a.sem, 1)
            do(tt_op(rl, rl, sel, ALU.mult))
            do(dve.tensor_reduce(rmx, rl3, AX.X, ALU.add))
            do(dve.reciprocal(rmx, rmx))
            do(tt_op(rgate[:, :, 0:NE], rl3, bc(rmx, [P, 2, NE], 2), ALU.mult))
            dve.wait_ge(router_s.sem, 2)
            do(dve.tensor_copy(rpos[:, :, 0:NE], v3(ps[:, 1, 0:16], 2)))

            def count_overflow():
                do(dve.tensor_reduce(rmx[:, 0:1], ps[:, 5, 0:8], AX.X, ALU.max))
                do(ts(ovf[:], rmx[:, 0:1], float(P), None, ALU.is_gt), router_d)

            def choose(col, f):
                for a in range(2):
                    ts(G[:, a, :], iota[:], rpos[:, a, bass.ds(col, 1)], rsel[:, a, bass.ds(col, 1)],
                       ALU.is_equal, ALU.mult)
                    ins = ts(Gg[:, a, :], iota[:], rpos[:, a, bass.ds(col, 1)], rgate[:, a, bass.ds(col, 1)],
                             ALU.is_equal, ALU.mult)
                ins.then_inc(f.sem, 1)

            def add_pieces(ve, qs, banks=(1, 3, 1, 3)):
                for q in qs:
                    dve.wait_ge(sc_full.sem, 4 * ve + q + 1)
                    tt_op(residual(q), residual(q), ps[:, banks[q], :], ALU.add).then_inc(x_added.sem, 1)

            def experts(first, ps_no):
                choose(0, g_ready)
                dve.memset(GT, 0.0).then_inc(gt_ready.sem, 1)
                for hf in range(2):
                    dve.memset(ys[:, hf * 512:(hf + 1) * 512], 0.0).then_inc(ys_ready.sem, 1)
                if ps_no == 0:
                    count_overflow()
                with dve.Fori(first, first + NE) as e:
                    ve = e - 1 + ps_no
                    for r in range(2):
                        dve.wait_ge(gat_full.sem, 2 * (e - 1) + r + 1)
                        tt_op(xgT[:, 4 * r:4 * r + 4, :], v3(ps[:, 6 + r, :], 4),
                              bc(pp(1, "ln_ffn", 4 * r, 4), [P, 4, P], 2), ALU.mult).then_inc(xg_ready.sem, 1)
                    add_pieces(ve, (0, 1))
                    for c in ffn(e, 1):
                        if c == 0:
                            add_pieces(ve, (2, 3))
                            dve.wait_ge(gt_full.sem, e)
                            dve.tensor_copy(GT, v3(ps[:, 2, 0:2 * P], 2)).then_inc(gt_ready.sem, 1)
                        if c == 5:
                            choose(e - first + 1, g_ready)
                add_pieces(first + NE - 1 + ps_no, range(4), LAST_BANKS)

            experts(1, 0)
            over = dve.value_load(ovf[0:1, 0:1])
            with dve.If(over > 0):
                do(ts(rpos, rpos, -float(P), None, ALU.add))
                experts(1 + NE, 1)



def kernel(**inputs):
    from concourse import bacc as _bacc
    from concourse.bass_utils import run_bass_kernel_spmd as _run

    a = {k: np.asarray(v) for k, v in inputs.items()}
    L = DEPTH

    def cols(v):
        return v.reshape(L, -1, P).transpose(0, 2, 1)

    def row(v):
        return np.broadcast_to(v[:, None, :], (L, P, v.shape[1]))

    def poles(v):
        return v.reshape(L, 8, P).transpose(0, 2, 1)

    moe_b = np.broadcast_to(a["moe_router_b"], (L, NE))
    parts = {
        "ln_mix": cols(a["ln_mix"]), "ln_ffn": cols(a["ln_ffn"]),
        "conv_w": a["ssd_conv_w"].reshape(L, CONV, 4, P).transpose(0, 3, 2, 1).reshape(L, P, 16),
        "conv_b": cols(a["ssd_conv_b"]), "ssd_norm": cols(a["ssd_norm"]), "att_out": cols(a["att_out_norm"]),
        "q_gain": np.concatenate([a["att_q_norm"]] * 2, axis=1)[:, :, None],
        "k_gain": np.concatenate([a["att_k_norm"]] * 2, axis=1)[:, :, None],
        "mu": cols(a["rwkv_mu"]), "w0": cols(a["rwkv_w0"]), "a0": cols(a["rwkv_a0"]), "k_k": cols(a["rwkv_k_k"]),
        "k_a": cols(a["rwkv_k_a"]), "r_k": cols(a["rwkv_r_k"]), "ln_w": cols(a["rwkv_ln_w"]),
        "ln_b": cols(a["rwkv_ln_b"]), "s5_d": cols(a["s5_d"]), "glu_b": cols(a["s5_glu_b"]),
        "s5_out": cols(a["s5_out_norm"]), "a_re": poles(a["s5_a_re"]), "a_im": poles(a["s5_a_im"]),
        "log_dt": poles(np.broadcast_to(a["s5_log_dt"][:, :, None], (L, 16, 64))),
        "dt_bias": row(a["ssd_dt_bias"]), "a_log": row(a["ssd_a_log"]), "ssd_d": row(a["ssd_d"]),
        "router_b": row(moe_b),
    }
    params = np.concatenate([parts[k] for k in PCOLS], axis=2)

    def b_rows(b):
        w = np.zeros((L, 2, 4, 2, 16, 2, 64), b.dtype)
        v = b.reshape(L, 2, 4, 2, 64, 16)
        for g in range(2):
            w[:, :, :, g, :, g, :] = v[:, :, :, g].transpose(0, 1, 2, 4, 3)
        return w.transpose(0, 2, 3, 4, 1, 5, 6).reshape(L, P, 256)

    def c_cols(c):
        return c.reshape(L, 8, 2, 16, 64).transpose(0, 2, 4, 1, 3).reshape(L, P, P)

    def k_rows(w):
        return w.reshape(L, -1, P, w.shape[2]).transpose(0, 2, 1, 3).reshape(L, P, -1)

    small = np.concatenate([
        np.concatenate([a["rwkv_w2"], a["rwkv_a2"]], axis=1), a["rwkv_g2"], k_rows(a["s5_glu_w"]),
        b_rows(a["s5_b_re"]), b_rows(a["s5_b_im"]), c_cols(a["s5_c_re"]), c_cols(a["s5_c_im"]),
        k_rows(np.broadcast_to(a["moe_router_w"], (L, D, NE)))], axis=2)

    w_in = a["w_in"]
    q0 = 772
    r0 = q0 + 768
    s0 = r0 + 1024
    starts = [r0 + P * i for i in range(8)] + [s0, s0 + P] + [P * i for i in range(4)] + [q0 + P * i for i in range(4)]
    mix = np.zeros((L, M_UNITS, P, MUNIT), w_in.dtype)
    w_out = a["w_out"].reshape(L, 8, P, D)
    tm = np.concatenate([w_in[:, :, 512:768], w_in[:, :, q0 + 512:q0 + 768], w_in[:, :, 768:772]], axis=2)
    for at, (kind, i) in enumerate(UNITS):
        if kind == "fm":
            mix[:, at, :, :D] = k_rows(w_in[:, :, starts[i]:starts[i] + P])
        elif kind == "tm":
            mix[:, at, :, :2 * TMW] = k_rows(tm[:, 2 * P * i:2 * P * (i + 1)])
        else:
            mix[:, at, :, :D] = w_out[:, i]

    def gate_up(g, u):
        n = g.shape[0]
        w = np.stack([v.reshape(n, GUQ, GUK, P, NC_, FC) for v in (g, u)], axis=6)
        return np.ascontiguousarray(w.transpose(0, 4, 1, 3, 2, 6, 5)).reshape(n, GU_UNITS, P, GUK, 2 * FC)

    arrays = {
        "x": a["x"].reshape(T, D), "params": params, "small_w": small, "mix_w": mix,
        "gu_dense": gate_up(a["ffn_w_gate"], a["ffn_w_up"])[0], "d_dense": a["ffn_w_down"][0],
        "gu_moe": gate_up(a["moe_w_gate"][0], a["moe_w_up"][0]), "d_moe": a["moe_w_down"][0],
    }
    arrays = {k: np.ascontiguousarray(v) for k, v in arrays.items()}
    nc = _bacc.Bacc("TRN2", target_bir_lowering=False, num_devices=1)
    args = [nc.dram_tensor(f"in_{k}", v.shape, mybir.dt.from_np(v.dtype), kind="ExternalInput").ap()
            for k, v in arrays.items()]
    out = nc.dram_tensor("out_x", (T, D), F32, kind="ExternalOutput").ap()
    trunk(nc, *args, out)
    r = _run(nc, [{f"in_{k}": v for k, v in arrays.items()}], core_ids=[0])
    return r.results[0]["out_x"].reshape(1, T, D)
```
